# Optimizing a Trainium2 kernel written in Bass

```python
import jax, jax.numpy as jnp
from jax import lax
import numpy as np
import math

D_MODEL = 1024
BATCH = 1
SEQ = 256
DEPTH = 1

RET_HEADS = 8
RET_DK = 64
RET_DV = 128
RET_CHUNK = 128
ROPE_BASE = 10000.0
SB_HEADS = 8
SB_DH = 64
SB_BLOCK = 128
PEER_HEADS = 8
N_KEYS = 128
N_EXPERTS = N_KEYS * N_KEYS
PEER_TOPK = 16
PEER_DKEY = 256
PEER_CHUNK = 128
EPS = 1e-6

RET_QK = RET_HEADS * RET_DK
RET_V = RET_HEADS * RET_DV
SB_W = SB_HEADS * SB_DH
IN_SIZES = (RET_QK, RET_QK, RET_V, RET_V, SB_W, SB_W, SB_W, D_MODEL, D_MODEL)
IN_WIDTH = sum(IN_SIZES)


def rmsnorm(x, g):
    xf = x.astype(jnp.float32)
    y = xf * lax.rsqrt(jnp.mean(xf * xf, axis=-1, keepdims=True) + EPS)
    return (y * g.astype(jnp.float32)).astype(x.dtype)

def group_norm(y, g):
    yf = y.astype(jnp.float32)
    mu = jnp.mean(yf, axis=-1, keepdims=True)
    var = jnp.mean(jnp.square(yf - mu), axis=-1, keepdims=True)
    return (yf - mu) * lax.rsqrt(var + EPS) * g.astype(jnp.float32)

def rope(x, pos):
    half = x.shape[-1] // 2
    freqs = ROPE_BASE ** (-jnp.arange(half, dtype=jnp.float32) / half)
    ang = pos[:, None] * freqs[None, :]
    cos = jnp.cos(ang)[:, None, :]
    sin = jnp.sin(ang)[:, None, :]
    xf = x.astype(jnp.float32)
    x1, x2 = xf[..., :half], xf[..., half:]
    return jnp.concatenate([x1 * cos - x2 * sin, x1 * sin + x2 * cos], axis=-1)

def retention(q, k, v):
    B, S, H, dk = q.shape
    dv = v.shape[-1]
    C = RET_CHUNK
    n = S // C
    log_g = jnp.log1p(-jnp.exp2(-5.0 - jnp.arange(H, dtype=jnp.float32)))
    i = jnp.arange(C, dtype=jnp.float32)
    diff = i[:, None] - i[None, :]
    dmask = jnp.where(diff >= 0, jnp.exp(log_g[:, None, None] * jnp.maximum(diff, 0.0)), 0.0)
    q_dec = jnp.exp(log_g[:, None] * (i + 1.0)).T[None, :, :, None]
    k_dec = jnp.exp(log_g[:, None] * (C - 1.0 - i)).T[None, :, :, None]
    c_dec = jnp.exp(log_g * C)[None, :, None, None]

    def chunks(t):
        return jnp.moveaxis(t.reshape(B, n, C, H, t.shape[-1]), 1, 0)

    def step(state, xs):
        qc, kc, vc = xs
        scores = jnp.einsum('bihd,bjhd->bhij', qc, kc) * dmask[None]
        y = jnp.einsum('bhij,bjhe->bihe', scores, vc)
        y = y + jnp.einsum('bihd,bhde->bihe', qc, state) * q_dec
        state = state * c_dec + jnp.einsum('bjhd,bjhe->bhde', kc * k_dec, vc)
        return state, y

    state0 = jnp.zeros((B, H, dk, dv), jnp.float32)
    _, ys = lax.scan(step, state0, (chunks(q), chunks(k), chunks(v)))
    return jnp.moveaxis(ys, 0, 1).reshape(B, S, H, dv)

def stick_breaking(q, k, v):
    B, S, H, d = q.shape
    n = S // SB_BLOCK
    scale = SB_DH ** -0.5
    qh = jnp.transpose(q, (0, 2, 1, 3))
    kh = jnp.transpose(k, (0, 2, 1, 3))
    vh = jnp.transpose(v, (0, 2, 1, 3))
    qb = jnp.moveaxis(qh.reshape(B, H, n, SB_BLOCK, d), 2, 0)
    kpos = jnp.arange(S)

    def block(args):
        qi, bi = args
        z = jnp.einsum('bhtd,bhsd->bhts', qi, kh).astype(jnp.float32) * scale
        tpos = bi * SB_BLOCK + jnp.arange(SB_BLOCK)
        mask = kpos[None, :] < tpos[:, None]
        log_stay = jnp.where(mask, jax.nn.log_sigmoid(-z), 0.0)
        later = lax.cumsum(log_stay, axis=3, reverse=True) - log_stay
        w = jnp.where(mask, jnp.exp(jax.nn.log_sigmoid(z) + later), 0.0)
        return jnp.einsum('bhts,bhsd->bhtd', w.astype(vh.dtype), vh)

    out = lax.map(block, (qb, jnp.arange(n)))
    out = jnp.moveaxis(out, 0, 2).reshape(B, H, S, d)
    return jnp.transpose(out, (0, 2, 1, 3)).reshape(B, S, H * d)

def peer(x, w_q, sub_keys_1, sub_keys_2, u_tab, v_tab):
    B, S, D = x.shape
    T = PEER_CHUNK
    n = S // T
    xc = jnp.moveaxis(x.reshape(B, n, T, D), 1, 0)
    k1 = sub_keys_1.astype(jnp.float32)
    k2 = sub_keys_2.astype(jnp.float32)

    def block(xb):
        q = (xb @ w_q).reshape(B, T, PEER_HEADS, 2, PEER_DKEY // 2).astype(jnp.float32)
        s1 = jnp.einsum('bthd,nd->bthn', q[..., 0, :], k1)
        s2 = jnp.einsum('bthd,nd->bthn', q[..., 1, :], k2)
        v1, i1 = lax.top_k(s1, PEER_TOPK)
        v2, i2 = lax.top_k(s2, PEER_TOPK)
        cand_s = (v1[..., :, None] + v2[..., None, :]).reshape(B, T, PEER_HEADS, PEER_TOPK * PEER_TOPK)
        cand_i = (i1[..., :, None] * N_KEYS + i2[..., None, :]).reshape(B, T, PEER_HEADS, PEER_TOPK * PEER_TOPK)
        top_s, pos = lax.top_k(cand_s, PEER_TOPK)
        idx = jnp.take_along_axis(cand_i, pos, axis=-1)
        g = jax.nn.softmax(top_s, axis=-1)
        u_sel = jnp.take(u_tab, idx, axis=0)
        h = jnp.einsum('bthkd,btd->bthk', u_sel, xb)
        a = (jax.nn.gelu(h.astype(jnp.float32)) * g).astype(xb.dtype)
        return jnp.einsum('bthk,bthkd->btd', a, jnp.take(v_tab, idx, axis=0))

    y = lax.map(block, xc)
    return jnp.moveaxis(y, 0, 1).reshape(B, S, D)

def first_inputs(seed: int = 0) -> dict:
    key = jax.random.key(seed)
    ks = jax.random.split(key, 17)
    f = jnp.float32
    nrm = lambda k, shape, s: jax.random.normal(k, shape, f) * s
    gain = lambda k, shape: 1.0 + 0.02 * jax.random.normal(k, shape, f)
    return {
        'x': jax.random.normal(ks[0], (BATCH, SEQ, D_MODEL), f),
        'norm_attn': gain(ks[1], (DEPTH, D_MODEL)),
        'w_in': nrm(ks[2], (DEPTH, D_MODEL, IN_WIDTH), D_MODEL ** -0.5),
        'ret_q_norm': gain(ks[3], (DEPTH, RET_DK)),
        'ret_k_norm': gain(ks[4], (DEPTH, RET_DK)),
        'ret_group_norm': gain(ks[5], (DEPTH, RET_V)),
        'sb_q_norm': gain(ks[6], (DEPTH, SB_DH)),
        'sb_k_norm': gain(ks[7], (DEPTH, SB_DH)),
        'w_branch_ret': nrm(ks[8], (DEPTH, RET_V, D_MODEL), RET_V ** -0.5),
        'w_branch_sb': nrm(ks[9], (DEPTH, SB_W, D_MODEL), SB_W ** -0.5),
        'w_out': nrm(ks[10], (DEPTH, D_MODEL, D_MODEL), D_MODEL ** -0.5),
        'norm_ffn': gain(ks[11], (DEPTH, D_MODEL)),
        'peer_w_q': nrm(ks[12], (DEPTH, D_MODEL, PEER_HEADS * PEER_DKEY), D_MODEL ** -0.5),
        'peer_sub_keys_1': nrm(ks[13], (DEPTH, N_KEYS, PEER_DKEY // 2), (PEER_DKEY // 2) ** -0.5),
        'peer_sub_keys_2': nrm(ks[14], (DEPTH, N_KEYS, PEER_DKEY // 2), (PEER_DKEY // 2) ** -0.5),
        'peer_u': nrm(ks[15], (DEPTH, N_EXPERTS, D_MODEL), D_MODEL ** -0.5),
        'peer_v': nrm(ks[16], (DEPTH, N_EXPERTS, D_MODEL), PEER_HEADS ** -0.5),
    }

def first_block(x, norm_attn, w_in, ret_q_norm, ret_k_norm, ret_group_norm, sb_q_norm, sb_k_norm,
              w_branch_ret, w_branch_sb, w_out, norm_ffn, peer_w_q, peer_sub_keys_1,
              peer_sub_keys_2, peer_u, peer_v):
    B, S, D = x.shape
    pos = jnp.arange(S, dtype=jnp.float32)
    split_points = np.cumsum(IN_SIZES)[:-1].tolist()
    for l in range(DEPTH):
        xn = rmsnorm(x, norm_attn[l])
        proj = xn @ w_in[l]
        rq, rk, rv, rg, sq, sk, sv, ga, gb = jnp.split(proj, split_points, axis=-1)

        rq = rope(rmsnorm(rq.reshape(B, S, RET_HEADS, RET_DK), ret_q_norm[l]), pos)
        rk = rope(rmsnorm(rk.reshape(B, S, RET_HEADS, RET_DK), ret_k_norm[l]), pos) * (RET_DK ** -0.5)
        ret = retention(rq, rk, rv.reshape(B, S, RET_HEADS, RET_DV).astype(jnp.float32))
        ret = group_norm(ret, ret_group_norm[l].reshape(RET_HEADS, RET_DV)).reshape(B, S, RET_V)
        ret = ret.astype(x.dtype) * jax.nn.silu(rg)
        y_a = ret @ w_branch_ret[l]

        sq = rmsnorm(sq.reshape(B, S, SB_HEADS, SB_DH), sb_q_norm[l])
        sk = rmsnorm(sk.reshape(B, S, SB_HEADS, SB_DH), sb_k_norm[l])
        sb = stick_breaking(sq, sk, sv.reshape(B, S, SB_HEADS, SB_DH))
        y_b = sb @ w_branch_sb[l]

        mixed = jax.nn.sigmoid(ga) * y_a + jax.nn.sigmoid(gb) * y_b
        x = x + mixed @ w_out[l]

        hn = rmsnorm(x, norm_ffn[l])
        x = x + peer(hn, peer_w_q[l], peer_sub_keys_1[l], peer_sub_keys_2[l], peer_u[l], peer_v[l])
    return x


D_MIX = D_MODEL
ATTN_HEADS = 8
ATTN_HD = 64
ATTN_W = ATTN_HEADS * ATTN_HD
MOBA_BLOCK = 256
MOBA_TOPK = 3
Q_BLOCK = 128
REC_HEADS = 4
REC_DK = 128
REC_DV = 128
REC_W = REC_HEADS * REC_DK
REC_VW = REC_HEADS * REC_DV
REC_CHUNK = 64
PEER_NKEYS = 128
PEER_N = PEER_NKEYS * PEER_NKEYS
PEER_TOKEN_BLOCK = 128
NORM_EPS = 1e-6
IN_WIDTHS = [ATTN_W, ATTN_W, ATTN_W, REC_W, REC_W, REC_VW, REC_VW]
IN_COLS = sum(IN_WIDTHS)
IN_SPLITS = [int(c) for c in np.cumsum(IN_WIDTHS)[:-1]]


def rmsnorm_2(x, g):
    xf = x.astype(jnp.float32)
    y = xf * lax.rsqrt(jnp.mean(xf * xf, axis=-1, keepdims=True) + NORM_EPS)
    return (y * g.astype(jnp.float32)).astype(x.dtype)

def alibi_slopes(n):
    return 2.0 ** (-8.0 * jnp.arange(1, n + 1, dtype=jnp.float32) / n)

def moba_attention(q, k, v):
    B, S, H, hd = q.shape
    nb = -(-S // MOBA_BLOCK)
    pad = nb * MOBA_BLOCK - S
    kp = jnp.pad(k, ((0, 0), (0, pad), (0, 0), (0, 0)))
    vp = jnp.pad(v, ((0, 0), (0, pad), (0, 0), (0, 0)))
    kb = kp.reshape(B, nb, MOBA_BLOCK, H, hd).transpose(0, 3, 1, 2, 4)
    vb = vp.reshape(B, nb, MOBA_BLOCK, H, hd).transpose(0, 3, 1, 2, 4)
    kmean = jnp.mean(kb.astype(jnp.float32), axis=3)
    gate = jnp.einsum('bshd,bhnd->bhsn', q.astype(jnp.float32), kmean)
    pos = jnp.arange(S)
    past = jnp.arange(nb)[None, :] < (pos // MOBA_BLOCK)[:, None]
    gate = jnp.where(past[None, None], gate, -jnp.inf)
    ksel = min(MOBA_TOPK, nb)
    _, sel = lax.top_k(gate, ksel)
    nq = S // Q_BLOCK
    qq = q.reshape(B, nq, Q_BLOCK, H, hd).transpose(0, 1, 3, 2, 4).reshape(B * nq, H, Q_BLOCK, hd)
    ss = sel.reshape(B, H, nq, Q_BLOCK, ksel).transpose(0, 2, 1, 3, 4).reshape(B * nq, H, Q_BLOCK, ksel)
    b_idx = jnp.repeat(jnp.arange(B, dtype=jnp.int32), nq)
    qb_idx = jnp.tile(jnp.arange(nq, dtype=jnp.int32), B)
    slopes = alibi_slopes(H)
    scale = hd ** -0.5
    off = jnp.arange(MOBA_BLOCK)
    gather = jax.vmap(lambda kk, s: kk[s])

    def one_block(args):
        qblk, sblk, b, qi = args
        kh = kb[b]
        vh = vb[b]
        tpos = qi * Q_BLOCK + jnp.arange(Q_BLOCK)
        own = (qi * Q_BLOCK) // MOBA_BLOCK
        k_s = gather(kh, sblk).astype(jnp.float32)
        v_s = gather(vh, sblk).astype(jnp.float32)
        k_o = lax.dynamic_index_in_dim(kh, own, axis=1, keepdims=False).astype(jnp.float32)
        v_o = lax.dynamic_index_in_dim(vh, own, axis=1, keepdims=False).astype(jnp.float32)
        qf = qblk.astype(jnp.float32) * scale
        s_sel = jnp.einsum('hqd,hqjkd->hqjk', qf, k_s)
        kpos_sel = sblk[..., None] * MOBA_BLOCK + off
        dist_sel = (tpos[None, :, None, None] - kpos_sel).astype(jnp.float32)
        s_sel = s_sel - slopes[:, None, None, None] * dist_sel
        s_sel = jnp.where((sblk < own)[..., None], s_sel, -jnp.inf)
        s_own = jnp.einsum('hqd,hkd->hqk', qf, k_o)
        kpos_own = own * MOBA_BLOCK + off
        dist_own = (tpos[:, None] - kpos_own[None, :]).astype(jnp.float32)
        s_own = s_own - slopes[:, None, None] * dist_own[None]
        s_own = jnp.where((kpos_own[None, :] <= tpos[:, None])[None], s_own, -jnp.inf)
        logits = jnp.concatenate([s_sel.reshape(H, Q_BLOCK, ksel * MOBA_BLOCK), s_own], axis=-1)
        p = jax.nn.softmax(logits, axis=-1)
        p_sel = p[..., :ksel * MOBA_BLOCK].reshape(H, Q_BLOCK, ksel, MOBA_BLOCK)
        p_own = p[..., ksel * MOBA_BLOCK:]
        o = jnp.einsum('hqjk,hqjkd->qhd', p_sel, v_s) + jnp.einsum('hqk,hkd->qhd', p_own, v_o)
        return o.astype(q.dtype)

    out = lax.map(one_block, (qq, ss, b_idx, qb_idx))
    return out.reshape(B, S, H * hd)

def hgrn2(q, f_pre, i, g, lb, norm_g):
    B, S, _ = q.shape
    nc = S // REC_CHUNK
    f = lb + (1.0 - lb) * jax.nn.sigmoid(f_pre.astype(jnp.float32))
    logf = jnp.log(f)
    kk = 1.0 - f
    qf = jax.nn.silu(q.astype(jnp.float32))
    vf = i.astype(jnp.float32)

    def heads(t, d):
        return t.reshape(B, nc, REC_CHUNK, REC_HEADS, d).transpose(1, 0, 3, 2, 4)

    causal = jnp.tril(jnp.ones((REC_CHUNK, REC_CHUNK), dtype=bool))

    def step(state, inp):
        qc, lfc, kc, vc = inp
        cum = jnp.cumsum(lfc, axis=2)
        diff = cum[:, :, :, None, :] - cum[:, :, None, :, :]
        decay = jnp.where(causal[None, None, :, :, None], jnp.exp(jnp.minimum(diff, 0.0)), 0.0)
        scores = jnp.einsum('bhtd,bhtsd,bhsd->bhts', qc, decay, kc)
        o = jnp.einsum('bhts,bhsv->bhtv', scores, vc) + jnp.einsum('bhtd,bhdv->bhtv', qc * jnp.exp(cum), state)
        last = cum[:, :, -1:, :]
        state = jnp.exp(last[:, :, 0, :])[..., None] * state + jnp.einsum('bhsd,bhsv->bhdv', kc * jnp.exp(last - cum), vc)
        return state, o

    state0 = jnp.zeros((B, REC_HEADS, REC_DK, REC_DV), jnp.float32)
    _, o = lax.scan(step, state0, (heads(qf, REC_DK), heads(logf, REC_DK), heads(kk, REC_DK), heads(vf, REC_DV)))
    o = o.transpose(1, 0, 3, 2, 4).reshape(B, S, REC_HEADS, REC_DV)
    o = rmsnorm_2(o, norm_g.reshape(REC_HEADS, REC_DV))
    o = o * jax.nn.silu(g.astype(jnp.float32)).reshape(B, S, REC_HEADS, REC_DV)
    return o.reshape(B, S, REC_VW).astype(q.dtype)

def peer_2(x, wq, subkeys, u, v):
    B, S, D = x.shape
    T = B * S
    xt = x.reshape(T // PEER_TOKEN_BLOCK, PEER_TOKEN_BLOCK, D)

    def one(xb):
        qp = (xb @ wq).reshape(PEER_TOKEN_BLOCK, PEER_HEADS, 2, PEER_DKEY // 2)
        s = jnp.einsum('thcd,hcnd->thcn', qp.astype(jnp.float32), subkeys.astype(jnp.float32))
        v1, i1 = lax.top_k(s[:, :, 0], PEER_TOPK)
        v2, i2 = lax.top_k(s[:, :, 1], PEER_TOPK)
        cand = (v1[..., :, None] + v2[..., None, :]).reshape(PEER_TOKEN_BLOCK, PEER_HEADS, PEER_TOPK * PEER_TOPK)
        cidx = (i1[..., :, None] * PEER_NKEYS + i2[..., None, :]).reshape(PEER_TOKEN_BLOCK, PEER_HEADS, PEER_TOPK * PEER_TOPK)
        sc, p = lax.top_k(cand, PEER_TOPK)
        eidx = jnp.take_along_axis(cidx, p, axis=-1)
        gates = jax.nn.softmax(sc, axis=-1)
        ue = u[eidx]
        ve = v[eidx]
        act = jax.nn.gelu(jnp.einsum('td,thkd->thk', xb, ue).astype(jnp.float32), approximate=False)
        return jnp.einsum('thk,thkd->td', (gates * act).astype(x.dtype), ve)

    return lax.map(one, xt).reshape(B, S, D)

def second_inputs(seed: int = 0) -> dict:
    key = jax.random.key(seed)
    ks = jax.random.split(key, 12)
    nrm = jax.random.normal
    x = nrm(ks[0], (BATCH, SEQ, D_MODEL), jnp.float32)
    norm1_g = 1.0 + 0.05 * nrm(ks[1], (DEPTH, D_MODEL), jnp.float32)
    w_in = nrm(ks[2], (DEPTH, D_MODEL, IN_COLS), jnp.float32) * D_MODEL ** -0.5
    rec_lb_logits = 0.5 * nrm(ks[3], (DEPTH + 1, REC_W), jnp.float32)
    rec_norm_g = 1.0 + 0.05 * nrm(ks[4], (DEPTH, REC_VW), jnp.float32)
    w_out = nrm(ks[5], (DEPTH, D_MIX, D_MODEL), jnp.float32) * D_MIX ** -0.5
    norm2_g = 1.0 + 0.05 * nrm(ks[6], (DEPTH, D_MODEL), jnp.float32)
    peer_wq = nrm(ks[7], (DEPTH, D_MODEL, PEER_HEADS * PEER_DKEY), jnp.float32) * D_MODEL ** -0.5
    peer_subkeys = nrm(ks[8], (DEPTH, PEER_HEADS, 2, PEER_NKEYS, PEER_DKEY // 2), jnp.float32) * (PEER_DKEY // 2) ** -0.5
    peer_u = nrm(ks[9], (DEPTH, PEER_N, D_MODEL), jnp.float32) * D_MODEL ** -0.5
    peer_v = 0.1 * nrm(ks[10], (DEPTH, PEER_N, D_MODEL), jnp.float32)
    normf_g = 1.0 + 0.05 * nrm(ks[11], (D_MODEL,), jnp.float32)
    return {'x': x, 'norm1_g': norm1_g, 'w_in': w_in, 'rec_lb_logits': rec_lb_logits,
            'rec_norm_g': rec_norm_g, 'w_out': w_out, 'norm2_g': norm2_g, 'peer_wq': peer_wq,
            'peer_subkeys': peer_subkeys, 'peer_u': peer_u, 'peer_v': peer_v, 'normf_g': normf_g}

def second_block(x, norm1_g, w_in, rec_lb_logits, rec_norm_g, w_out, norm2_g, peer_wq, peer_subkeys, peer_u, peer_v, normf_g):
    B, S, _ = x.shape
    lb_all = jnp.cumsum(jax.nn.softmax(rec_lb_logits.astype(jnp.float32), axis=0), axis=0)
    h = x
    for layer in range(DEPTH):
        xn = rmsnorm_2(h, norm1_g[layer])
        proj = xn @ w_in[layer]
        q_a, k_a, v_a, q_r, f_r, i_r, g_r = jnp.split(proj, IN_SPLITS, axis=-1)
        attn = moba_attention(q_a.reshape(B, S, ATTN_HEADS, ATTN_HD),
                              k_a.reshape(B, S, ATTN_HEADS, ATTN_HD),
                              v_a.reshape(B, S, ATTN_HEADS, ATTN_HD))
        rec = hgrn2(q_r, f_r, i_r, g_r, lb_all[layer], rec_norm_g[layer])
        h = h + jnp.concatenate([attn, rec], axis=-1) @ w_out[layer]
        hn = rmsnorm_2(h, norm2_g[layer])
        h = h + peer_2(hn, peer_wq[layer], peer_subkeys[layer], peer_u[layer], peer_v[layer])
    return rmsnorm_2(h, normf_g)


def setup_inputs(seed=0):
    out = dict(first_inputs(seed))
    for name, value in second_inputs(seed + 1).items():
        if name != "x":
            out[name + "_2"] = value
    return out


def reference(
    x, norm_attn, w_in, ret_q_norm, ret_k_norm, ret_group_norm, sb_q_norm, sb_k_norm,
    w_branch_ret, w_branch_sb, w_out, norm_ffn, peer_w_q, peer_sub_keys_1, peer_sub_keys_2,
    peer_u, peer_v, norm1_g_2, w_in_2, rec_lb_logits_2, rec_norm_g_2, w_out_2, norm2_g_2,
    peer_wq_2, peer_subkeys_2, peer_u_2, peer_v_2, normf_g_2,
):
    x = first_block(
        x, norm_attn, w_in, ret_q_norm, ret_k_norm, ret_group_norm, sb_q_norm, sb_k_norm,
        w_branch_ret, w_branch_sb, w_out, norm_ffn, peer_w_q, peer_sub_keys_1, peer_sub_keys_2,
        peer_u, peer_v,
    )
    return second_block(
        x, norm1_g_2, w_in_2, rec_lb_logits_2, rec_norm_g_2, w_out_2, norm2_g_2, peer_wq_2,
        peer_subkeys_2, peer_u_2, peer_v_2, normf_g_2,
    )


_drawn_inputs = setup_inputs


def setup_inputs(seed=0):
    import zlib

    import numpy as np

    out = dict(_drawn_inputs(seed))
    spreads = {}
    factors = {'ret_q_norm': 3.087,
     'ret_k_norm': 3.537,
     'ret_group_norm': 3.331,
     'sb_q_norm': 4.626,
     'sb_k_norm': 4.966,
     'rec_norm_g_2': 3.239,
     'norm2_g_2': 5.721}
    for name, (base, spread) in spreads.items():
        noise = np.random.default_rng([zlib.crc32(name.encode()), seed]).standard_normal(out[name].shape)
        drawn = base * np.exp(spread * noise) if base else spread * noise
        out[name] = __import__('jax').numpy.asarray(drawn.astype(out[name].dtype))
    for name, factor in factors.items():
        out[name] = (out[name] * factor).astype(out[name].dtype)
    return out
```

```python
from contextlib import ExitStack

import numpy as np
import concourse.bass as bass
from concourse import mybir

P = 128
F32 = mybir.dt.float32
F16 = mybir.dt.float16
U32 = mybir.dt.uint32
ALU = mybir.AluOpType
ACT = mybir.ActivationFunctionType
AX = mybir.AxisListType

D = 1024
S = 256
TT = S // P
KC = D // P
EPS = 1e-6

HEADS = 8
HD = 64
RDV = 128
REC_H = 4
TOPK = 16
NKEY = 128
GATE_SCALE = 2.0 ** 14

SLOT = 2048
SC = SLOT // KC
RING = 4

IN1 = [("rq", 0, 512), ("rk", 512, 512), ("sq", 3072, 512), ("sk", 3584, 512), ("rv", 1024, 1024),
       ("sv", 4096, 512), ("rg", 2048, 1024), ("ga", 4608, 1024), ("gb", 5632, 1024)]
IN2 = [("qa", 0, 512), ("ka", 512, 512), ("fr", 2048, 512), ("qr", 1536, 512), ("va", 1024, 512),
       ("ir", 2560, 512), ("gr", 3072, 512)]


def slots_of(groups):
    return [(n, o) for n, _, w in groups for o in range(0, w, SC)]


IN1_SLOTS, IN2_SLOTS = slots_of(IN1), slots_of(IN2)
N_EXP = NKEY * NKEY
E_TILES = N_EXP // P
TPS = SLOT // D
U_SLOTS = E_TILES // TPS
U_MID = 12
G_GROUPS = S // 4

ORDER = [("in1", len(IN1_SLOTS)), ("ret", 4), ("sb", 2), ("out1", 4), ("q1", 8), ("u1", U_SLOTS), ("v1", U_SLOTS),
         ("in2", len(IN2_SLOTS)), ("out2", 4), ("q2", 8), ("u2", U_SLOTS), ("v2", U_SLOTS)]
FIRST, N_SLOTS = {}, 0
for _name, _n in ORDER:
    FIRST[_name] = N_SLOTS
    N_SLOTS += _n

def schedule1():
    steps = []
    for s in range(len(IN1_SLOTS)):
        steps.append(("proj", s))
        if s in (1, 3, 5, 7):
            steps.append(("headnorm", s // 2))
        if s in (3, 5, 7, 9):
            steps.append(("headT", (s - 3) // 2))
        if 12 <= s < 12 + HEADS:
            steps.append(("ret_scores", s - 12))
        if 13 <= s < 13 + HEADS:
            steps.append(("ret_values", s - 13))
        if s == 13 + HEADS:
            steps.append(("ret_norm", 0))
        if 14 <= s < 14 + HEADS:
            steps.append(("sb_scores", s - 14))
        if 15 <= s < 15 + HEADS:
            steps.append(("sb_later", s - 15))
        if 16 <= s < 16 + HEADS:
            steps.append(("sb_values", s - 16))
    return steps


def schedule2():
    steps = [("proj", s) for s in range(8)] + [("rec_prep", 0)] + [("proj", 8), ("proj", 9)]
    for i in range(HEADS + 2):
        if 10 + i < len(IN2_SLOTS):
            steps.append(("proj", 10 + i))
        if i < HEADS:
            steps.append(("m_scores", i))
        if i < 9:
            steps.append(("rec_level", i))
        if 1 <= i <= HEADS:
            steps.append(("m_turn", i - 1))
        if 2 <= i:
            steps.append(("m_values", i - 2))
    return steps


def block_program(nc, weights, const1, const2, gains, keys_in, x, out):
    with ExitStack() as ctx:
        def sb(name, shape, dt=F32):
            return ctx.enter_context(nc.sbuf_tensor(name, shape, dt))

        def sem(name):
            return ctx.enter_context(nc.semaphore(name))

        ring = sb("ring", [P, RING, SLOT])
        act = sb("act", [P, S, NKEY])
        xres = sb("xres", [P, TT, D])
        hT = sb("hT", [P, KC, S])
        ident = sb("ident", [P, P])
        zeros = sb("zeros", [P, P])
        iota = sb("iota", [P, NKEY], F16)
        iota16 = sb("iota16", [P, TOPK])
        gcol = sb("gcol", [P, 4, KC])
        scores = sb("scores", [P, TT, HEADS, 2, NKEY])
        qT = sb("qT", [P, 2, 2, S])
        cand = sb("cand", [P, 3, TOPK * TOPK])
        val = sb("val", [P, HEADS, 2, TOPK])
        idx = sb("idx", [P, HEADS, 2, TOPK], U32)
        top = sb("top", [P, HEADS, TOPK])
        pos = sb("pos", [P, HEADS, TOPK], U32)
        esel = sb("esel", [P, TT, 3, HEADS, TOPK])
        stat = sb("stat", [P, 8, 16])
        ps = ctx.enter_context(nc.psum_tensor("ps", [P, 8, 512], F32))

        small = qT[:, :, :, :].rearrange("p a b c -> p (a b c)")
        idxf = small[:, 0:256].rearrange("p (h c k) -> p h c k", h=HEADS, c=2)
        posab = small[:, 256:512].rearrange("p (c h k) -> p c h k", c=2, h=HEADS).bitcast(U32)
        posf = small[:, 512:768].rearrange("p (c h k) -> p c h k", c=2, h=HEADS)
        late = scores[:, :, :, :, :].rearrange("p t h c k -> p (t h c k)")
        eselT = late[:, 2048:2048 + 5 * S].rearrange("p (w t) -> p w t", w=5)
        ghalf = late[:, 3328:3456].bitcast(F16)
        hot2 = late[:, 0:512].bitcast(F16).rearrange("p (b q k) -> p b q k", b=2, q=4)
        hot1 = late[:, 512:1536].bitcast(F16).rearrange("p (b w q k) -> p b w q k", b=2, w=2, q=4)
        sel = late[:, 0:1024].rearrange("p (b e t) -> p b e t", b=2, e=TPS)

        flat = act[:, :, :].rearrange("p a b -> p (a b)")

        def carve(at, *shape):
            n = int(np.prod(shape))
            names = "abcd"[:len(shape)]
            ap = flat[:, at:at + n]
            if len(shape) > 1:
                ap = ap.rearrange(f"p ({' '.join(names)}) -> p {' '.join(names)}",
                                  **{c: k for c, k in zip(names[1:], shape[1:])})
            return ap, at + n

        at = 0
        xs, at = carve(at, TT, D)
        raw1 = {}
        for n, _, w in IN1:
            raw1[n], at = carve(at, TT, w)
        tmp_at = at
        tmpA, at = carve(at, TT, 512)
        tmpB, at = carve(at, TT, 512)
        headsT1 = {}
        for n in ("rq", "rk", "sq", "sk"):
            headsT1[n], at = carve(at, HEADS // 2, S)
        c1, at = carve(at, const1.shape[1])
        retm, at = carve(at, 2, 384)
        rety, _ = carve(tmp_at, TT, HEADS, RDV)
        sbt, at = carve(at, 2, 6, 384)
        keys1, at = carve(at, 2, NKEY)
        assert at <= S * NKEY, at
        start = TT * D
        retT, _ = carve(start, KC, S)
        sbT, _ = carve(start + 2 * TT * 512, HEADS // 2, S)
        mixed, _ = carve(start + 4 * TT * 512, TT, D)
        mT = hT

        cc = 0

        def col(n, *shape):
            nonlocal cc
            k = int(np.prod((n,) + shape))
            ap = c1[:, cc:cc + k]
            cc += k
            return ap
        rope = col(TT * 4 * HD).rearrange("p (t k c) -> p t k c", t=TT, k=4)
        dmask = col(HEADS * 384).rearrange("p (h c) -> p h c", h=HEADS)
        tri = col(P)
        ones = col(P)
        strict = col(384)
        hgain = col(4 * HD).rearrange("p (k c) -> p k c", k=4)
        ggain = col(HEADS * RDV).rearrange("p (h e) -> p h e", h=HEADS)
        assert cc == const1.shape[1]

        at = TT * D
        raw2 = {}
        for n in ("va", "ir", "gr"):
            raw2[n], at = carve(at, TT, 512)
        colT = {}
        for n in ("qa", "ka", "fr", "qr"):
            colT[n], at = carve(at, 4, S)
        c2, at = carve(at, const2.shape[1])
        ml, at = carve(at, 2, 384)
        mpT, at = carve(at, 2, 384)
        catT, at = carve(at, KC, S)
        cum, at = carve(at, REC_H, TT, P)
        kk, at = carve(at, REC_H, TT, P)
        dlt, at = carve(at, REC_H, TT, P)
        qL, at = carve(at, REC_H, TT, P)
        kL, at = carve(at, REC_H, TT, P)
        Ssum, at = carve(at, TT, REC_H, P)
        Sx, at = carve(at, REC_H, P)
        ry, at = carve(at, TT, REC_H, P)
        rt, at = carve(at, TT, REC_H, P)
        lbs, at = carve(at, 8, REC_H)
        keys2, at = carve(at, HEADS * 2, NKEY)
        assert at <= S * NKEY, at
        c2a = c2[:, 0:HEADS * 384].rearrange("p (h c) -> p h c", h=HEADS)
        o = HEADS * 384
        lmask = c2[:, o:o + 8 * P].rearrange("p (l c) -> p l c", l=8)
        o += 8 * P
        ones2 = c2[:, o:o + P]
        o += P
        lbl = c2[:, o:o + 2 * REC_H].rearrange("p (k h) -> p k h", k=2)
        o += 2 * REC_H
        rgain = c2[:, o:o + 512].rearrange("p (h e) -> p h e", h=REC_H)
        o += 512
        assert o == const2.shape[1]
        fgain = flat[:, TT * D:TT * D + D]

        def mstat(h, k, t):
            return stat[:, 4, (h % 2) * 6 + 2 * k + t:(h % 2) * 6 + 2 * k + t + 1]

        def mstat2(h, k):
            return stat[:, 4, (h % 2) * 6 + 2 * k:(h % 2) * 6 + 2 * k + 2]

        def level(ap, l):
            h = 1 << (l - 1)
            if len(ap.shape) == 4:
                ap = ap.rearrange("p h t c -> p (h t c)")
            return ap.rearrange("p (n b) -> p n b", b=2 * h), h

        slot_in = [sem(f"slot_in{j}") for j in range(RING)]
        slot_used = sem("slot_used")
        const_in = sem("const_in")
        const2_in = sem("const2_in")
        keys2_in = sem("keys2_in")
        x_in = sem("x_in")
        out_done = sem("out_done")
        dve_step = sem("dve_step")
        act_step = sem("act_step")
        nsq = sem("norm_sums_ready")
        nvar = sem("norm_var_ready")
        nstd = sem("norm_std_ready")
        nxs = sem("norm_scaled_ready")
        nT = sem("norm_transposed")
        nout = sem("norm_out_ready")
        nfree = sem("norm_out_act")
        proj_copied = sem("proj_copied")
        hvar = sem("head_var_ready")
        hstd = sem("head_std_ready")
        hready = sem("head_ready")
        hTr = sem("head_transposed")
        hTc = sem("head_transposed_copied")
        rs_ready = sem("ret_scores_ready")
        rm_ready = sem("ret_masked_ready")
        rv_ready = sem("ret_values_ready")
        rv_copied = sem("ret_values_copied")
        rg_var = sem("ret_var_ready")
        rg_std = sem("ret_std_ready")
        rg_ready = sem("ret_gated_ready")
        z_ready = sem("sb_scores_ready")
        neg_ready = sem("sb_negabs_ready")
        ln_ready = sem("sb_log_ready")
        stay_ready = sem("sb_stay_ready")
        later_ready = sem("sb_later_ready")
        arg_ready = sem("sb_arg_ready")
        wexp_ready = sem("sb_exp_ready")
        w_ready = sem("sb_weights_ready")
        so_ready = sem("sb_out_ready")
        so_copied = sem("sb_out_copied")
        t_ready = sem("transposed")
        t_copied = sem("transposed_copied")
        ya_used = sem("branch_used")
        mix_ready = sem("mixed_ready")
        o_used = sem("out_proj_used")
        m_ready = sem("moba_scores_ready")
        m_max = sem("moba_max_ready")
        m_exp = sem("moba_exp_ready")
        m_prob = sem("moba_probs_ready")
        m_T = sem("moba_transposed")
        m_Tc = sem("moba_transposed_copied")
        m_out = sem("moba_out_ready")
        m_outc = sem("moba_out_copied")
        g_lbm = sem("rec_lb_max_ready")
        g_lbe = sem("rec_lb_exp_ready")
        g_f = sem("rec_forget_ready")
        g_log = sem("rec_log_ready")
        g_dlt = sem("rec_diff_ready")
        g_exp = sem("rec_exp_ready")
        g_qk = sem("rec_level_ready")
        g_s = sem("rec_scores_ready")
        g_sc = sem("rec_scores_used")
        g_sum = sem("rec_sum_ready")
        g_sx = sem("rec_cross_copied")
        g_y = sem("rec_values_ready")
        g_yc = sem("rec_values_copied")
        g_var = sem("rec_var_ready")
        g_std = sem("rec_std_ready")
        g_out = sem("rec_gated_ready")
        peer = []
        for b in (1, 2):
            peer.append({n: sem(f"peer{b}_{n}") for n in (
                "q_copied", "s_ready", "s_copied", "gelu_done", "sums_ready", "exp_ready",
                "sel_ready", "selT_ready", "parts_ready", "hot_ready", "gates_ready", "gates_used", "tile_ready",
                "acc_ready", "done", "top_free")})
        fin_sq = sem("final_sum_ready")
        fin_var = sem("final_var_ready")
        fin_std = sem("final_std_ready")
        fin_ready = sem("final_ready")
        fgain_in = sem("final_gain_in")

        block = ctx.enter_context(nc.Block())

        def bank(i, a=0, b=512):
            return ps[:, i, a:b]

        def slot_ready(pe, i):
            pe.wait_ge(slot_in[i % RING], 16 * (i // RING + 1))

        @block.sync
        def _(sp):
            for j in range(RING):
                sp.dma_start(ring[:, j, :], weights[j]).then_inc(slot_in[j], 16)
            full = N_SLOTS // RING
            with sp.Fori(1, full) as k:
                for j in range(RING):
                    sp.wait_ge(slot_used, k * RING + (j - RING + 1))
                    sp.dma_start(ring[:, j, :], weights[k * RING + j]).then_inc(slot_in[j], 16)
            for i in range(full * RING, N_SLOTS):
                sp.wait_ge(slot_used, i - RING + 1)
                sp.dma_start(ring[:, i % RING, :], weights[i]).then_inc(slot_in[i % RING], 16)

        @block.gpsimd
        def _(pool):
            for t in range(TT):
                pool.dma_start(xres[:, t, :], x[0, t * P:(t + 1) * P, :]).then_inc(x_in, 16)
            pool.dma_start(ident[:, :], gains["ident"]).then_inc(const_in, 16)
            pool.dma_start(gcol[:, :, :], gains["gcol"]).then_inc(const_in, 16)
            pool.dma_start(zeros[:, :], gains["zeros"]).then_inc(const_in, 16)
            pool.dma_start(iota[:, :], gains["iota"]).then_inc(const_in, 16)
            pool.dma_start(iota16[:, :], gains["iota16"]).then_inc(const_in, 16)
            pool.dma_start(keys1[:, :, :], keys_in[0]).then_inc(const_in, 16)
            pool.dma_start(c1, const1).then_inc(const_in, 16)
            pool.wait_ge(peer[0]["acc_ready"], 1)
            pool.dma_start(c2, const2).then_inc(const2_in, 16)
            pool.dma_start(keys2, keys_in[1]).then_inc(keys2_in, 16)
            pool.wait_ge(peer[1]["acc_ready"], 1)
            pool.dma_start(fgain, gains["fgain"]).then_inc(fgain_in, 16)

        N_CONST = 16 * 7

        def tiles(ap):
            return ap.rearrange("p t (h c) -> p (t h) c", c=HD)

        @block.tensor
        def _(pe):
            def norm_transposes(k):
                pe.wait_ge(nxs, TT * (k + 1))
                for b in range(4):
                    for j in range(2):
                        for t in range(TT):
                            mm = pe.transpose(bank(b, j * S + t * P, j * S + (t + 1) * P),
                                              xs[:, t, (2 * b + j) * P:(2 * b + j + 1) * P], ident[:, :])
                    mm.then_inc(nT, 1)
                pe.wait_ge(nout, 4 * (k + 1))
                pe.wait_ge(nfree, 4 * (k + 1))

            def turn16(src, k):
                for b in range(4):
                    for j in range(2):
                        for t in range(TT):
                            mm = pe.transpose(bank(b, j * S + t * P, j * S + (t + 1) * P), src(t, 2 * b + j),
                                              ident[:, :])
                    mm.then_inc(t_ready, 1)
                pe.wait_ge(t_copied, 4 * (k + 1))

            def natural(lhs, i, u, wait):
                slot_ready(pe, i)
                if u >= 2:
                    pe.wait_ge(wait, u - 1)
                for t in range(TT):
                    for kc in range(KC):
                        mm = pe.matmul(bank(4 + u % 2, t * SC, (t + 1) * SC), lhs[:, kc, t * P:(t + 1) * P],
                                       ring[:, i % RING, kc * SC:(kc + 1) * SC], start=(kc == 0), stop=(kc == KC - 1))
                return mm

            def columns(i, u, wait):
                slot_ready(pe, i)
                if u >= 2:
                    pe.wait_ge(wait, u - 1)
                for c in range(2):
                    for kc in range(KC):
                        mm = pe.matmul(bank(4 + u % 2, c * S, (c + 1) * S),
                                       ring[:, i % RING, kc * SC + c * P:kc * SC + (c + 1) * P], hT[:, kc, :],
                                       start=(kc == 0), stop=(kc == KC - 1))
                return mm

            def rows(h):
                return slice(HD * (h % 2), HD * (h % 2) + HD)

            def attention1():
                for what, i in schedule1():
                    if what == "proj":
                        natural(hT, i, i, proj_copied).then_inc(slot_used, 1)
                    elif what == "headT":
                        name = ("rq", "rk", "sq", "sk")[i]
                        pe.wait_ge(hready, i + 1)
                        for r in range(2):
                            if 2 * i + r:
                                pe.wait_ge(hTc, 2 * i + r)
                            for j in range(2):
                                for t in range(TT):
                                    c = (2 * r + j) * P
                                    mm = pe.transpose(bank(7, j * S + t * P, j * S + (t + 1) * P),
                                                      raw1[name][:, t, c:c + P], ident[:, :])
                            mm.then_inc(hTr, 1)
                    elif what == "ret_scores":
                        if i == 0:
                            pe.wait_ge(hTc, 4)
                        else:
                            pe.wait_ge(rm_ready, i)
                        q, kT = headsT1["rq"][rows(i), i // 2, :], headsT1["rk"][rows(i), i // 2, :]
                        pe.matmul(bank(3, 0, S), kT[:, 0:P], q, start=True, stop=True)
                        pe.matmul(bank(3, S, S + P), kT[:, P:S], q[:, P:S], start=True, stop=True).then_inc(rs_ready, 1)
                    elif what == "ret_values":
                        pe.wait_ge(rm_ready, i + 1)
                        if i == 0:
                            pe.wait_ge(proj_copied, 12)
                        else:
                            pe.wait_ge(rv_copied, i)
                        m, v = retm[:, i % 2, :], raw1["rv"][:, :, i * RDV:(i + 1) * RDV]
                        pe.matmul(bank(6, 0, P), m[:, 0:P], v[:, 0, :], start=True, stop=True)
                        pe.matmul(bank(6, P, 2 * P), m[:, P:S], v[:, 0, :], start=True, stop=False)
                        pe.matmul(bank(6, P, 2 * P), m[:, S:S + P], v[:, 1, :], start=False, stop=True)\
                          .then_inc(rv_ready, 1)
                    elif what == "sb_scores":
                        if i == 0:
                            pe.wait_ge(hTc, 8)
                        else:
                            pe.wait_ge(neg_ready, i)
                        q, kT = headsT1["sq"][rows(i), i // 2, :], headsT1["sk"][rows(i), i // 2, :]
                        pe.matmul(bank(0, 0, S), kT[:, 0:P], q, start=True, stop=True)
                        pe.matmul(bank(0, S, S + P), kT[:, P:S], q[:, P:S], start=True, stop=True).then_inc(z_ready, 1)
                    elif what == "sb_later":
                        pe.wait_ge(stay_ready, i + 1)
                        if i:
                            pe.wait_ge(arg_ready, i)
                        ls = sbt[:, i % 2, 0, :]
                        pe.matmul(bank(1, 0, S), tri, ls[:, 0:S], start=True, stop=False, skip_group_check=True)
                        pe.matmul(bank(1, P, S), ones, ls[:, S:S + P], start=False, stop=True, skip_group_check=True)
                        pe.matmul(bank(1, S, S + P), tri, ls[:, S:S + P], start=True, stop=True,
                                  skip_group_check=True).then_inc(later_ready, 1)
                    elif what == "sb_values":
                        pe.wait_ge(w_ready, i + 1)
                        if i == 0:
                            pe.wait_ge(proj_copied, 14)
                        if i >= 2:
                            pe.wait_ge(so_copied, i - 1)
                        w, v = sbt[:, i % 2, 5, :], raw1["sv"][:, :, i * HD:(i + 1) * HD]
                        pe.matmul(ps[rows(i), 2, 0:S], v[:, 0, :], w[:, 0:S], start=True, stop=False,
                                  skip_group_check=True)
                        pe.matmul(ps[rows(i), 2, P:S], v[:, 1, :], w[:, S:S + P], start=False, stop=True,
                                  skip_group_check=True).then_inc(so_ready, 1)
                pe.wait_ge(rg_ready, 1)
                pe.wait_ge(so_copied, HEADS)
                turn16(lambda t, c: rety[:, t, c, :], 0)
                pe.wait_ge(proj_copied, len(IN1_SLOTS))
                for u in range(4):
                    natural(retT, FIRST["ret"] + u, u, ya_used).then_inc(slot_used, 1)
                for j in range(2):
                    i = FIRST["sb"] + j
                    slot_ready(pe, i)
                    for t in range(TT):
                        u = 4 + TT * j + t
                        pe.wait_ge(ya_used, u - 1)
                        for kc in range(4):
                            mm = pe.matmul(bank(4 + u % 2), sbT[:, kc, t * P:(t + 1) * P],
                                           ring[:, i % RING, kc * 512:(kc + 1) * 512], start=(kc == 0), stop=(kc == 3))
                    mm.then_inc(slot_used, 1)
                pe.wait_ge(mix_ready, 1)
                turn16(lambda t, c: mixed[:, t, c * P:(c + 1) * P], 1)
                for u in range(4):
                    natural(mT, FIRST["out1"] + u, u, o_used).then_inc(slot_used, 1)

            def attention2():
                base = len(IN1_SLOTS)
                pe.wait_ge(const2_in, 16)
                for what, i in schedule2():
                    if what == "proj":
                        if IN2_SLOTS[i][0] in colT:
                            mm = columns(FIRST["in2"] + i, base + i, proj_copied)
                        else:
                            mm = natural(hT, FIRST["in2"] + i, base + i, proj_copied)
                        mm.then_inc(slot_used, 1)
                    elif what == "m_scores":
                        if i == 0:
                            pe.wait_ge(proj_copied, base + 4)
                        else:
                            pe.wait_ge(m_max, i)
                        q, kT = colT["qa"][rows(i), i // 2, :], colT["ka"][rows(i), i // 2, :]
                        pe.matmul(bank(0, 0, P), q[:, 0:P], kT[:, 0:P], start=True, stop=True)
                        pe.matmul(bank(0, P, P + S), q[:, P:S], kT, start=True, stop=True).then_inc(m_ready, 1)
                    elif what == "m_turn":
                        pe.wait_ge(m_prob, i + 1)
                        if i:
                            pe.wait_ge(m_Tc, i)
                        p = ml[:, i % 2, :]
                        for c in range(3):
                            mm = pe.transpose(bank(1, c * P, (c + 1) * P), p[:, c * P:(c + 1) * P], ident[:, :])
                        mm.then_inc(m_T, 1)
                    elif what == "m_values":
                        pe.wait_ge(m_Tc, i + 1)
                        if i == 0:
                            pe.wait_ge(proj_copied, base + 10)
                        if i >= 2:
                            pe.wait_ge(m_outc, i - 1)
                        w, v = mpT[:, i % 2, :], raw2["va"][:, :, i * HD:(i + 1) * HD]
                        pe.matmul(ps[rows(i), 2, 0:S], v[:, 0, :], w[:, 0:S], start=True, stop=False,
                                  skip_group_check=True)
                        pe.matmul(ps[rows(i), 2, P:S], v[:, 1, :], w[:, S:S + P], start=False, stop=True,
                                  skip_group_check=True).then_inc(m_out, 1)
                    elif what == "rec_level":
                        pe.wait_ge(g_qk, i + 1)
                        kl, ql = (kk, colT["qr"].rearrange("p h (t c) -> p h t c", t=TT)) if i == 0 else (kL, qL)
                        if i < 8:
                            for t in range(TT):
                                if i:
                                    pe.wait_ge(g_sc, TT * (i - 1) + t + 1)
                                for h in range(REC_H):
                                    mm = pe.matmul(bank(6 + t, h * P, (h + 1) * P), kl[:, h, t, :], ql[:, h, t, :],
                                                   start=True, stop=True)
                                mm.then_inc(g_s, 1)
                        else:
                            pe.wait_ge(g_sc, TT * 8 - 1)
                            for h in range(REC_H):
                                mm = pe.matmul(bank(6, h * P, (h + 1) * P), kl[:, h, 0, :], ql[:, h, 1, :],
                                               start=True, stop=True)
                            mm.then_inc(g_s, 1)
                pe.wait_ge(g_sx, 1)
                pe.wait_ge(g_sc, TT * 8)
                ir = raw2["ir"]
                for t in range(TT):
                    for h in range(REC_H):
                        mm = pe.matmul(bank(6 + t, h * P, (h + 1) * P), Ssum[:, t, h, :], ir[:, t, h * P:(h + 1) * P],
                                       start=True, stop=(t == 0))
                        if t:
                            mm = pe.matmul(bank(6 + t, h * P, (h + 1) * P), Sx[:, h, :], ir[:, 0, h * P:(h + 1) * P],
                                           start=False, stop=True)
                    mm.then_inc(g_y, 1)
                pe.wait_ge(g_out, 1)
                for b in range(2):
                    for j in range(2):
                        for t in range(TT):
                            mm = pe.transpose(bank(6 + b, j * S + t * P, j * S + (t + 1) * P), ry[:, t, 2 * b + j, :],
                                              ident[:, :])
                    mm.then_inc(t_ready, 1)
                pe.wait_ge(t_copied, 8 + 2)
                pe.wait_ge(m_outc, HEADS)
                for u in range(4):
                    natural(catT, FIRST["out2"] + u, 4 + u, o_used).then_inc(slot_used, 1)

            def experts(b, keys):
                n = peer[b]
                for h in range(HEADS + 1):
                    if h < HEADS:
                        columns(FIRST[f"q{b + 1}"] + h, h, n["q_copied"])\
                            .then_inc(slot_used, 1)
                    if h:
                        g = h - 1
                        pe.wait_ge(n["q_copied"], g + 1)
                        if g >= 2:
                            pe.wait_ge(n["s_copied"], g - 1)
                        for t in range(TT):
                            for c in range(2):
                                kT = keys[:, c if b == 0 else 2 * g + c, :]
                                mm = pe.matmul(bank(6 + g % 2, (2 * t + c) * P, (2 * t + c + 1) * P),
                                               qT[:, g % 2, c, t * P:(t + 1) * P], kT, start=True, stop=True)
                        mm.then_inc(n["s_ready"], 1)

                def u_slot(k, j, first):
                    r = (FIRST[f"u{b + 1}"] + j) % RING
                    pe.wait_ge(slot_in[r], k * 16 + 16 * ((FIRST[f"u{b + 1}"] + j) // RING + 1))
                    if not first:
                        pe.wait_ge(n["gelu_done"], k * RING + (j - RING + 1))
                    for e in range(TPS):
                        for kc in range(KC):
                            mm = pe.matmul(bank(j, e * S, (e + 1) * S),
                                           ring[:, r, e * D + kc * P:e * D + (kc + 1) * P], hT[:, kc, :],
                                           start=(kc == 0), stop=(kc == KC - 1))
                    mm.then_inc(slot_used, 1)

                for j in range(RING):
                    u_slot(0, j, True)
                with pe.Fori(1, U_MID) as k:
                    for j in range(RING):
                        u_slot(k, j, False)
                pe.wait_ge(n["sel_ready"], 1)
                pe.wait_ge(n["s_copied"], HEADS)
                for w in range(3):
                    for t in range(TT):
                        mm = pe.transpose(bank(4 + w // 2, (w % 2) * S + t * P, (w % 2) * S + (t + 1) * P),
                                          esel[:, t, w, :, :].rearrange("p h k -> p (h k)"), ident[:, :])
                mm.then_inc(n["selT_ready"], 1)
                with pe.Fori(U_MID, U_SLOTS // RING) as k:
                    for j in range(RING):
                        u_slot(k, j, False)

                def gates(g, j, first):
                    pe.wait_ge(n["hot_ready"], g + 1)
                    if not first:
                        pe.wait_ge(n["gates_used"], g - 1)
                    for q in range(4):
                        for part in range(2):
                            mm = pe.matmul(bank(6 + j, q * P, (q + 1) * P), hot2[:, j, q, :], hot1[:, j, part, q, :],
                                           start=(part == 0), stop=(part == 1))
                    mm.then_inc(n["gates_ready"], 1)

                gates(0, 0, True)
                gates(1, 1, True)
                with pe.Fori(1, G_GROUPS // 2) as k:
                    for j in range(2):
                        gates(k * 2 + j, j, False)

                pe.wait_ge(n["gelu_done"], U_SLOTS)
                for a in range(4):
                    pe.matmul(bank(a), zeros[:, :], hT[:, 0:2, :], start=True, stop=False, skip_group_check=True)

                def v_slot(k, j):
                    r = (FIRST[f"v{b + 1}"] + j) % RING
                    pe.wait_ge(slot_in[r], k * 16 + 16 * ((FIRST[f"v{b + 1}"] + j) // RING + 1))
                    pe.wait_ge(n["tile_ready"], k * RING + (j + 1))
                    for e in range(TPS):
                        for t in range(TT):
                            for half in range(2):
                                c = e * D + half * 512
                                mm = pe.matmul(bank(2 * t + half), sel[:, j % 2, e, t * P:(t + 1) * P],
                                               ring[:, r, c:c + 512], start=False, stop=False, skip_group_check=True)
                    mm.then_inc(slot_used, 1)

                with pe.Fori(0, U_SLOTS // RING) as k:
                    for j in range(RING):
                        v_slot(k, j)
                for a in range(4):
                    mm = pe.matmul(bank(a), zeros[:, :], hT[:, 0:2, :], start=False, stop=True, skip_group_check=True)
                mm.then_inc(n["acc_ready"], 1)

            pe.wait_ge(const_in, N_CONST)
            norm_transposes(0)
            attention1()
            norm_transposes(1)
            experts(0, keys1)
            norm_transposes(2)
            attention2()
            norm_transposes(3)
            pe.wait_ge(keys2_in, 16)
            experts(1, keys2)

        @block.scalar
        def _(eng):
            steps = [0]

            def settle(ins):
                steps[0] += 1
                ins.then_inc(act_step, 1)
                eng.wait_ge(act_step, steps[0])

            def norm(k, sem_in, count):
                eng.wait_ge(sem_in, count)
                for t in range(TT):
                    eng.activation(xs[:, t, :], xres[:, t, :], ACT.Square, accum_out=stat[:, 0, t:t + 1])\
                       .then_inc(nsq, 1)
                eng.wait_ge(nvar, k + 1)
                eng.activation(stat[:, 2, 0:TT], stat[:, 1, 0:TT], ACT.Sqrt).then_inc(nstd, 1)
                for b in (1, 3):
                    eng.wait_ge(nT, 4 * k + b + 1)
                    for j in range(2):
                        c = 2 * b + j
                        eng.activation(hT[:, c, :], bank(b, j * S, (j + 1) * S), ACT.Copy, scale=gcol[:, k, c:c + 1])\
                           .then_inc(nfree, 1)

            def turned(dst, k):
                for b in range(4):
                    eng.wait_ge(t_ready, 4 * k + b + 1)
                    eng.activation(dst[:, 2 * b:2 * b + 2, :], bank(b).rearrange("p (j c) -> p j c", j=2), ACT.Copy)\
                       .then_inc(t_copied, 1)

            def rows(h):
                return slice(HD * (h % 2), HD * (h % 2) + HD)

            FUNC = {"rg": ACT.Silu, "ga": ACT.Sigmoid, "gb": ACT.Sigmoid, "qr": ACT.Silu, "gr": ACT.Silu,
                    "fr": ACT.Sigmoid}

            def attention1():
                for what, i in schedule1():
                    if what == "proj":
                        name, off = IN1_SLOTS[i]
                        eng.wait_ge(slot_used, i + 1)
                        eng.activation(raw1[name][:, :, off:off + SC], bank(4 + i % 2).rearrange("p (t c) -> p t c", t=TT),
                                       FUNC.get(name, ACT.Copy)).then_inc(proj_copied, 1)
                    elif what == "headnorm":
                        eng.wait_ge(hvar, i + 1)
                        eng.activation(stat[:, 7, :], stat[:, 6, :], ACT.Sqrt).then_inc(hstd, 1)
                    elif what == "headT":
                        name = ("rq", "rk", "sq", "sk")[i]
                        for r in range(2):
                            eng.wait_ge(hTr, 2 * i + r + 1)
                            eng.activation(headsT1[name][:, 2 * r:2 * r + 2, :],
                                           bank(7).rearrange("p (j c) -> p j c", j=2), ACT.Copy).then_inc(hTc, 1)
                    elif what == "ret_values":
                        eng.wait_ge(rv_ready, i + 1)
                        eng.activation(rety[:, :, i, :], bank(6, 0, S).rearrange("p (t c) -> p t c", t=TT), ACT.Copy)\
                           .then_inc(rv_copied, 1)
                    elif what == "ret_norm":
                        eng.wait_ge(rg_var, 1)
                        eng.activation(stat[:, 4, :], stat[:, 5, :], ACT.Sqrt).then_inc(rg_std, 1)
                    elif what == "sb_scores":
                        eng.wait_ge(neg_ready, i + 1)
                        b = sbt[:, i % 2, :, :]
                        settle(eng.activation(b[:, 3, :], b[:, 2, :], ACT.Exp))
                        eng.activation(b[:, 4, :], b[:, 3, :], ACT.Ln, bias=1.0).then_inc(ln_ready, 1)
                    elif what == "sb_later":
                        eng.wait_ge(arg_ready, i + 1)
                        b = sbt[:, i % 2, :, :]
                        eng.activation(b[:, 3, :], b[:, 2, :], ACT.Exp).then_inc(wexp_ready, 1)
                    elif what == "sb_values":
                        eng.wait_ge(so_ready, i + 1)
                        eng.activation(sbT[rows(i), i // 2, :], ps[rows(i), 2, 0:S], ACT.Copy).then_inc(so_copied, 1)
                turned(retT, 0)
                turned(mT, 1)

            def attention2():
                base = len(IN1_SLOTS)
                eng.wait_ge(g_lbm, 1)
                eng.activation(lbs[:, 4:6, :], lbs[:, 2:4, :], ACT.Exp).then_inc(g_lbe, 1)
                for what, i in schedule2():
                    if what == "proj":
                        name, off = IN2_SLOTS[i]
                        u = base + i
                        eng.wait_ge(slot_used, FIRST["in2"] + i + 1)
                        dst = (colT[name][:, off // P:off // P + 2, :] if name in colT else raw2[name][:, :, off:off + SC])
                        eng.activation(dst, bank(4 + u % 2).rearrange("p (t c) -> p t c", t=2), FUNC.get(name, ACT.Copy))\
                           .then_inc(proj_copied, 1)
                    elif what == "m_scores":
                        eng.wait_ge(m_max, i + 1)
                        for t in range(TT):
                            c = slice(0, P) if t == 0 else slice(P, P + S)
                            eng.activation(ml[:, i % 2, c], ml[:, i % 2, c], ACT.Exp, bias=mstat(i, 0, t),
                                           accum_out=mstat(i, 1, t)).then_inc(m_exp, 1)
                    elif what == "m_turn":
                        eng.wait_ge(m_T, i + 1)
                        if i >= 2:
                            eng.wait_ge(m_out, i - 1)
                        eng.activation(mpT[:, i % 2, :], bank(1, 0, 384), ACT.Copy).then_inc(m_Tc, 1)
                    elif what == "m_values":
                        eng.wait_ge(m_out, i + 1)
                        eng.activation(catT[rows(i), i // 2, :], ps[rows(i), 2, 0:S], ACT.Copy).then_inc(m_outc, 1)
                    elif what == "rec_prep":
                        eng.wait_ge(g_f, 1)
                        eng.activation(dlt.rearrange("p h t c -> p (h t c)"), colT["fr"].rearrange("p h c -> p (h c)"),
                                       ACT.Ln).then_inc(g_log, 1)
                    elif what == "rec_level" and i:
                        eng.wait_ge(g_dlt, i)
                        if i < 8:
                            v, h = level(dlt, i)
                            eng.activation(v[:, :, h:], v[:, :, h:], ACT.Exp)
                            eng.activation(v[:, :, 0:h], v[:, :, 0:h], ACT.Exp, scale=-1.0).then_inc(g_exp, 1)
                        else:
                            eng.activation(dlt[:, :, 0, :], dlt[:, :, 0, :], ACT.Exp, scale=-1.0)
                            eng.activation(dlt[:, :, 1, :], cum[:, :, 1, :], ACT.Exp).then_inc(g_exp, 1)
                            eng.wait_ge(g_s, TT * 8 + 1)
                            eng.activation(Sx.rearrange("p h c -> p (h c)"), bank(6), ACT.Copy).then_inc(g_sx, 1)
                for t in range(TT):
                    eng.wait_ge(g_y, t + 1)
                    eng.activation(ry[:, t, :, :].rearrange("p h c -> p (h c)"), bank(6 + t), ACT.Copy).then_inc(g_yc, 1)
                eng.wait_ge(g_var, 1)
                eng.activation(stat[:, 7, 0:8], stat[:, 6, 0:8], ACT.Sqrt).then_inc(g_std, 1)
                for b in range(2):
                    eng.wait_ge(t_ready, 8 + b + 1)
                    eng.activation(catT[:, 4 + 2 * b:6 + 2 * b, :], bank(6 + b).rearrange("p (j c) -> p j c", j=2),
                                   ACT.Copy).then_inc(t_copied, 1)

            def experts(b):
                n = peer[b]
                for h in range(HEADS + 1):
                    if h < HEADS:
                        eng.wait_ge(slot_used, FIRST[f"q{b + 1}"] + h + 1)
                        if h >= 2:
                            eng.wait_ge(n["s_ready"], h - 1)
                        eng.activation(qT[:, h % 2, :, :], bank(4 + h % 2).rearrange("p (c t) -> p c t", c=2), ACT.Copy)\
                           .then_inc(n["q_copied"], 1)
                    if h:
                        eng.wait_ge(n["s_ready"], h)
                        eng.activation(scores[:, :, h - 1, :, :],
                                       bank(6 + (h - 1) % 2).rearrange("p (t c k) -> p t c k", t=TT, c=2), ACT.Copy)\
                           .then_inc(n["s_copied"], 1)

                def gelu(k, j):
                    eng.wait_ge(slot_used, k * RING + (FIRST[f"u{b + 1}"] + j + 1))
                    dst = act[:, :, bass.ds(k * (RING * TPS) + j * TPS, TPS)].rearrange("p t e -> p e t")
                    eng.activation(dst, bank(j).rearrange("p (e t) -> p e t", e=TPS),
                                   ACT.Gelu_apprx_tanh if b == 0 else ACT.Gelu).then_inc(n["gelu_done"], 1)

                with eng.Fori(0, U_MID) as k:
                    for j in range(RING):
                        gelu(k, j)
                eng.wait_ge(n["sums_ready"], 1)
                eng.activation(esel[:, :, 2, :, :].rearrange("p t h k -> p t (h k)"),
                               esel[:, :, 2, :, :].rearrange("p t h k -> p t (h k)"), ACT.Exp).then_inc(n["exp_ready"], 1)
                with eng.Fori(U_MID, U_SLOTS // RING) as k:
                    for j in range(RING):
                        gelu(k, j)

            norm(0, x_in, 16 * TT)
            attention1()
            norm(1, o_used, 4)
            experts(0)
            norm(2, peer[0]["done"], 4)
            attention2()
            norm(3, o_used, 8)
            experts(1)
            eng.wait_ge(peer[1]["done"], 4)
            for t in range(TT):
                eng.activation(xs[:, t, :], xres[:, t, :], ACT.Square, accum_out=stat[:, 0, t:t + 1]).then_inc(fin_sq, 1)
            eng.wait_ge(fin_var, 1)
            eng.activation(stat[:, 2, 0:TT], stat[:, 1, 0:TT], ACT.Sqrt).then_inc(fin_std, 1)
            for t in range(TT):
                eng.wait_ge(fin_ready, t + 1)
                eng.dma_start(out[0, t * P:(t + 1) * P, :], xs[:, t, :]).then_inc(out_done, 16)
            eng.wait_ge(out_done, 16 * TT)

        @block.vector
        def _(eng):
            steps = [0]

            def tick(ins):
                steps[0] += 1
                ins.then_inc(dve_step, 1)

            def settle(ins):
                tick(ins)
                eng.wait_ge(dve_step, steps[0])

            def norm(k):
                eng.wait_ge(nsq, TT * (k + 1))
                eng.tensor_scalar(stat[:, 1, 0:TT], stat[:, 0, 0:TT], 1.0 / D, EPS, ALU.mult, ALU.add).then_inc(nvar, 1)
                eng.wait_ge(nstd, k + 1)
                settle(eng.reciprocal(stat[:, 3, 0:TT], stat[:, 2, 0:TT]))
                for t in range(TT):
                    eng.tensor_scalar(xs[:, t, :], xres[:, t, :], stat[:, 3, t:t + 1], None, ALU.mult).then_inc(nxs, 1)
                for b in (0, 2):
                    eng.wait_ge(nT, 4 * k + b + 1)
                    for j in range(2):
                        c = 2 * b + j
                        eng.tensor_scalar(hT[:, c, :], bank(b, j * S, (j + 1) * S), gcol[:, k, c:c + 1], None, ALU.mult)\
                           .then_inc(nout, 1)

            def over(ap, n):
                return ap.unsqueeze(2).to_broadcast([P, ap.shape[1], n])

            def attention1():
                for what, i in schedule1():
                    if what == "headnorm":
                        name = ("rq", "rk", "sq", "sk")[i]
                        X = tiles(raw1[name])
                        A, B = tiles(tmpA), tiles(tmpB)
                        eng.wait_ge(proj_copied, 2 * i + 2)
                        if i:
                            eng.wait_ge(hready, i)
                        settle(eng.tensor_tensor(A, X, X, ALU.mult))
                        settle(eng.tensor_reduce(stat[:, 5, :], A, AX.X, ALU.add))
                        eng.tensor_scalar(stat[:, 6, :], stat[:, 5, :], 1.0 / HD, EPS, ALU.mult, ALU.add).then_inc(hvar, 1)
                        eng.wait_ge(hstd, i + 1)
                        settle(eng.reciprocal(stat[:, 5, :], stat[:, 7, :]))
                        settle(eng.tensor_tensor(X, X, over(stat[:, 5, :], HD), ALU.mult))
                        g = hgain[:, i:i + 1, :].to_broadcast([P, 16, HD])
                        last = eng.tensor_tensor(X, X, g, ALU.mult)
                        if i < 2:
                            settle(last)
                            X4, A4, B4 = (v.rearrange("p (t h) c -> p t h c", t=TT) for v in (X, A, B))
                            for t in range(TT):
                                cs = rope[:, t, 2 * i:2 * i + 1, :].to_broadcast([P, HEADS, HD])
                                sn = rope[:, t, 2 * i + 1:2 * i + 2, :].to_broadcast([P, HEADS, HD])
                                tick(eng.tensor_tensor(A4[:, t], X4[:, t], cs, ALU.mult))
                                settle(eng.tensor_tensor(B4[:, t], X4[:, t], sn, ALU.mult))
                            H2 = HD // 2
                            tick(eng.tensor_tensor(X[:, :, 0:H2], A[:, :, 0:H2], B[:, :, H2:HD], ALU.subtract))
                            last = eng.tensor_tensor(X[:, :, H2:HD], B[:, :, 0:H2], A[:, :, H2:HD], ALU.add)
                        last.then_inc(hready, 1)
                    elif what == "ret_scores":
                        eng.wait_ge(rs_ready, i + 1)
                        if i >= 2:
                            eng.wait_ge(rv_ready, i - 1)
                        eng.tensor_tensor(retm[:, i % 2, :], bank(3, 0, 384), dmask[:, i, :], ALU.mult).then_inc(rm_ready, 1)
                    elif what == "ret_norm":
                        Y = rety.rearrange("p t h c -> p (t h) c")
                        A = xs.rearrange("p t (h c) -> p (t h) c", c=RDV)
                        eng.wait_ge(rv_copied, HEADS)
                        settle(eng.tensor_reduce(stat[:, 4, :], Y, AX.X, ALU.add))
                        settle(eng.tensor_scalar(stat[:, 5, :], stat[:, 4, :], 1.0 / RDV, None, ALU.mult))
                        settle(eng.tensor_tensor(Y, Y, over(stat[:, 5, :], RDV), ALU.subtract))
                        settle(eng.tensor_tensor(A, Y, Y, ALU.mult))
                        settle(eng.tensor_reduce(stat[:, 4, :], A, AX.X, ALU.add))
                        eng.tensor_scalar(stat[:, 5, :], stat[:, 4, :], 1.0 / RDV, EPS, ALU.mult, ALU.add)\
                           .then_inc(rg_var, 1)
                        eng.wait_ge(rg_std, 1)
                        settle(eng.reciprocal(stat[:, 5, :], stat[:, 4, :]))
                        settle(eng.tensor_tensor(Y, Y, over(stat[:, 5, :], RDV), ALU.mult))
                        for t in range(TT):
                            tick(eng.tensor_tensor(rety[:, t], rety[:, t], ggain, ALU.mult))
                        eng.wait_ge(dve_step, steps[0])
                        eng.wait_ge(proj_copied, 18)
                        eng.tensor_tensor(Y, Y, raw1["rg"].rearrange("p t (h c) -> p (t h) c", c=RDV), ALU.mult)\
                           .then_inc(rg_ready, 1)
                    elif what == "sb_scores":
                        b = sbt[:, i % 2, :, :]
                        z = bank(0, 0, 384)
                        sc = HD ** -0.5
                        eng.wait_ge(z_ready, i + 1)
                        if i >= 2:
                            eng.wait_ge(w_ready, i - 1)
                        tick(eng.tensor_scalar(b[:, 0, :], z, -sc, 0.0, ALU.mult, ALU.min))
                        settle(eng.tensor_scalar(b[:, 1, :], z, sc, 0.0, ALU.mult, ALU.min))
                        eng.tensor_tensor(b[:, 2, :], b[:, 0, :], b[:, 1, :], ALU.add).then_inc(neg_ready, 1)
                        eng.wait_ge(ln_ready, i + 1)
                        eng.wait_ge(dve_step, steps[0])
                        tick(eng.tensor_tensor(b[:, 1, :], b[:, 1, :], b[:, 4, :], ALU.subtract))
                        settle(eng.tensor_tensor(b[:, 0, :], b[:, 0, :], b[:, 4, :], ALU.subtract))
                        eng.tensor_tensor(b[:, 0, :], b[:, 0, :], strict, ALU.mult).then_inc(stay_ready, 1)
                    elif what == "sb_later":
                        b = sbt[:, i % 2, :, :]
                        eng.wait_ge(later_ready, i + 1)
                        eng.tensor_tensor(b[:, 2, :], b[:, 1, :], bank(1, 0, 384), ALU.add).then_inc(arg_ready, 1)
                        if i >= 2:
                            eng.wait_ge(so_ready, i - 1)
                        eng.wait_ge(wexp_ready, i + 1)
                        eng.tensor_tensor(b[:, 5, :], b[:, 3, :], strict, ALU.mult).then_inc(w_ready, 1)
                for u in range(4):
                    eng.wait_ge(slot_used, FIRST["ret"] + u + 1)
                    if u == 0:
                        eng.wait_ge(proj_copied, len(IN1_SLOTS))
                    c = slice(u * SC, (u + 1) * SC)
                    eng.tensor_tensor(mixed[:, :, c], bank(4 + u % 2).rearrange("p (t c) -> p t c", t=TT),
                                      raw1["ga"][:, :, c], ALU.mult).then_inc(ya_used, 1)
                for u in range(4, 8):
                    j, t = (u - 4) // TT, (u - 4) % TT
                    c = slice(j * 512, (j + 1) * 512)
                    eng.wait_ge(slot_used, FIRST["sb"] + j + 1)
                    eng.tensor_tensor(tmpA[:, 0, :], bank(4 + u % 2), raw1["gb"][:, t, c], ALU.mult).then_inc(ya_used, 1)
                    eng.wait_ge(ya_used, u + 1)
                    last = eng.tensor_tensor(mixed[:, t, c], mixed[:, t, c], tmpA[:, 0, :], ALU.add)
                    if u < 7:
                        settle(last)
                last.then_inc(mix_ready, 1)
                residual(0)

            def residual(k):
                for u in range(4):
                    c = slice(u * SC, (u + 1) * SC)
                    eng.wait_ge(slot_used, FIRST[f"out{k + 1}"] + u + 1)
                    eng.tensor_tensor(xres[:, :, c], xres[:, :, c], bank(4 + u % 2).rearrange("p (t c) -> p t c", t=TT),
                                      ALU.add).then_inc(o_used, 1)

            def attention2():
                base = len(IN1_SLOTS)
                eng.wait_ge(const2_in, 16)
                settle(eng.tensor_tensor(lbs[:, 0, :], lbl[:, 0, :], lbl[:, 1, :], ALU.max))
                tick(eng.tensor_tensor(lbs[:, 2, :], lbl[:, 0, :], lbs[:, 0, :], ALU.subtract))
                eng.tensor_tensor(lbs[:, 3, :], lbl[:, 1, :], lbs[:, 0, :], ALU.subtract).then_inc(g_lbm, 1)
                tick(eng.memset(qL, 0.0))
                tick(eng.memset(kL, 0.0))
                tick(eng.memset(Ssum, 0.0))
                eng.wait_ge(g_lbe, 1)
                settle(eng.tensor_tensor(lbs[:, 0, :], lbs[:, 4, :], lbs[:, 5, :], ALU.add))
                settle(eng.reciprocal(lbs[:, 1, :], lbs[:, 0, :]))
                settle(eng.tensor_tensor(lbs[:, 6, :], lbs[:, 4, :], lbs[:, 1, :], ALU.mult))
                settle(eng.tensor_scalar(lbs[:, 7, :], lbs[:, 6, :], -1.0, 1.0, ALU.mult, ALU.add))
                for what, i in schedule2():
                    if what == "m_scores":
                        l = ml[:, i % 2, :]
                        eng.wait_ge(m_ready, i + 1)
                        if i >= 2:
                            eng.wait_ge(m_T, i - 1)
                        settle(eng.scalar_tensor_tensor(l, bank(0, 0, 384), HD ** -0.5, c2a[:, i, :], ALU.mult, ALU.add))
                        eng.tensor_reduce(mstat(i, 0, 0), l[:, 0:P], AX.X, ALU.max, negate=True)
                        eng.tensor_reduce(mstat(i, 0, 1), l[:, P:P + S], AX.X, ALU.max, negate=True).then_inc(m_max, 1)
                    elif what == "m_turn":
                        l = ml[:, i % 2, :]
                        eng.wait_ge(m_exp, TT * (i + 1))
                        settle(eng.reciprocal(mstat2(i, 2), mstat2(i, 1)))
                        eng.tensor_scalar(l[:, 0:P], l[:, 0:P], mstat(i, 2, 0), None, ALU.mult)
                        eng.tensor_scalar(l[:, P:P + S], l[:, P:P + S], mstat(i, 2, 1), None, ALU.mult).then_inc(m_prob, 1)
                    elif what == "rec_prep":
                        f = colT["fr"]
                        eng.wait_ge(proj_copied, base + 8)
                        for h in range(REC_H):
                            tick(eng.tensor_scalar(f[:, h, :], f[:, h, :], lbs[:, 7, h:h + 1], lbs[:, 6, h:h + 1],
                                                   ALU.mult, ALU.add))
                        eng.wait_ge(dve_step, steps[0])
                        eng.tensor_scalar(kk.rearrange("p h t c -> p (h t c)"), f.rearrange("p h c -> p (h c)"), -1.0, 1.0,
                                          ALU.mult, ALU.add).then_inc(g_f, 1)
                        eng.wait_ge(g_log, 1)
                        for h in range(REC_H):
                            for t in range(TT):
                                tick(eng.tensor_tensor_scan(cum[:, h, t, :], ones2, dlt[:, h, t, :], 0.0, ALU.mult, ALU.add))
                        eng.wait_ge(dve_step, steps[0])
                    elif what == "rec_level":
                        q = colT["qr"].rearrange("p h (t c) -> p h t c", t=TT)
                        if i == 0:
                            eng.wait_ge(g_f, 1)
                            eng.nop().then_inc(g_qk, 1)
                        elif i < 8:
                            d, h = level(dlt, i)
                            c = level(cum, i)[0]
                            eng.wait_ge(g_qk, i)
                            eng.tensor_tensor(d, c, c[:, :, h - 1:h].to_broadcast([P, c.shape[1], 2 * h]), ALU.subtract)\
                               .then_inc(g_dlt, 1)
                            eng.wait_ge(g_exp, i)
                            eng.wait_ge(g_s, TT * i)
                            eng.tensor_tensor(level(qL, i)[0][:, :, h:], d[:, :, h:], level(q, i)[0][:, :, h:], ALU.mult)
                            eng.tensor_tensor(level(kL, i)[0][:, :, 0:h], d[:, :, 0:h], level(kk, i)[0][:, :, 0:h], ALU.mult)\
                               .then_inc(g_qk, 1)
                        else:
                            eng.wait_ge(g_qk, i)
                            eng.tensor_tensor(dlt[:, :, 0, :], cum[:, :, 0, :],
                                              cum[:, :, 0, P - 1:P].to_broadcast([P, REC_H, P]), ALU.subtract)\
                               .then_inc(g_dlt, 1)
                            eng.wait_ge(g_exp, i)
                            eng.wait_ge(g_s, TT * i)
                            eng.tensor_tensor(qL[:, :, 1, :], dlt[:, :, 1, :], q[:, :, 1, :], ALU.mult)
                            eng.tensor_tensor(kL[:, :, 0, :], dlt[:, :, 0, :], kk[:, :, 0, :], ALU.mult).then_inc(g_qk, 1)
                        if i < 8:
                            for t in range(TT):
                                eng.wait_ge(g_s, TT * i + t + 1)
                                m = lmask[:, i:i + 1, :].bitcast(U32).to_broadcast([P, REC_H, P])
                                eng.copy_predicated(Ssum[:, t, :, :], m, bank(6 + t).rearrange("p (h c) -> p h c", h=REC_H))\
                                   .then_inc(g_sc, 1)
                Y = ry.rearrange("p t h c -> p (t h) c")
                A = rt.rearrange("p t h c -> p (t h) c")
                eng.wait_ge(g_yc, TT)
                settle(eng.tensor_tensor(A, Y, Y, ALU.mult))
                settle(eng.tensor_reduce(stat[:, 5, 0:8], A, AX.X, ALU.add))
                eng.tensor_scalar(stat[:, 6, 0:8], stat[:, 5, 0:8], 1.0 / P, EPS, ALU.mult, ALU.add).then_inc(g_var, 1)
                eng.wait_ge(g_std, 1)
                settle(eng.reciprocal(stat[:, 5, 0:8], stat[:, 7, 0:8]))
                settle(eng.tensor_tensor(Y, Y, over(stat[:, 5, 0:8], P), ALU.mult))
                for t in range(TT):
                    tick(eng.tensor_tensor(ry[:, t], ry[:, t], rgain, ALU.mult))
                eng.wait_ge(dve_step, steps[0])
                eng.wait_ge(proj_copied, base + len(IN2_SLOTS))
                eng.tensor_tensor(Y, Y, raw2["gr"].rearrange("p t (h c) -> p (t h) c", c=P), ALU.mult).then_inc(g_out, 1)
                residual(1)

            def top16(ins, tmp, vals, ids):
                for s, v in zip(ins, vals):
                    tick(eng.max(v[:, 0:8], s))
                eng.wait_ge(dve_step, steps[0])
                for s, w, v, x in zip(ins, tmp, vals, ids):
                    tick(eng.max_index(x[:, 0:8], v[:, 0:8], s))
                    tick(eng.match_replace(w, v[:, 0:8], s, -3.0e38))
                eng.wait_ge(dve_step, steps[0])
                for w, v in zip(tmp, vals):
                    tick(eng.max(v[:, 8:16], w))
                eng.wait_ge(dve_step, steps[0])
                for w, v, x in zip(tmp, vals, ids):
                    tick(eng.max_index(x[:, 8:16], v[:, 8:16], w))
                eng.wait_ge(dve_step, steps[0])

            def experts(b):
                n = peer[b]
                for t in range(TT):
                    for h in range(HEADS):
                        if t == 0:
                            eng.wait_ge(n["s_copied"], h + 1)
                        top16([scores[:, t, h, c, :] for c in range(2)], [cand[:, 2, c * NKEY:(c + 1) * NKEY] for c in range(2)],
                              [val[:, h, c, :] for c in range(2)], [idx[:, h, c, :] for c in range(2)])
                        s = cand[:, 0, :]
                        settle(eng.tensor_tensor(s.rearrange("p (a b) -> p a b", a=TOPK), over(val[:, h, 0, :], TOPK),
                                                 val[:, h, 1:2, :].to_broadcast([P, TOPK, TOPK]), ALU.add))
                        top16([s], [cand[:, 1, :]], [top[:, h, :]], [pos[:, h, :]])
                    tick(eng.tensor_scalar(posab[:, 0, :, :], pos[:, :, :], 4, None, ALU.logical_shift_right))
                    tick(eng.tensor_scalar(posab[:, 1, :, :], pos[:, :, :], TOPK - 1, None, ALU.bitwise_and))
                    tick(eng.tensor_copy(idxf[:, :, :, :], idx[:, :, :, :]))
                    eng.wait_ge(dve_step, steps[0])
                    settle(eng.tensor_copy(posf[:, :, :, :], posab[:, :, :, :]))
                    hk = HEADS * TOPK
                    big = scores[:, 0, :, :, :].rearrange("p h c k -> p (h c k)")
                    eq = big.rearrange("p (m a) -> p m a", a=TOPK)
                    eq4 = big.rearrange("p (h k a) -> p h k a", h=HEADS, k=TOPK)
                    for c in range(2):
                        settle(eng.tensor_tensor(eq, iota16[:, :].unsqueeze(1).to_broadcast([P, hk, TOPK]),
                                                 over(posf[:, c, :, :].rearrange("p h k -> p (h k)"), TOPK), ALU.is_equal))
                        settle(eng.tensor_tensor(eq4, eq4, idxf[:, :, c, :].unsqueeze(2).to_broadcast([P, HEADS, TOPK, TOPK]),
                                                 ALU.mult))
                        settle(eng.tensor_reduce(esel[:, t, c, :, :].rearrange("p h k -> p (h k)"), eq, AX.X, ALU.add))
                    last = eng.tensor_tensor(esel[:, t, 2, :, :], top[:, :, :], top[:, :, 0:1].to_broadcast([P, HEADS, TOPK]),
                                             ALU.subtract)
                    if t == 0:
                        settle(last)
                last.then_inc(n["sums_ready"], 1)
                eng.wait_ge(n["exp_ready"], 1)
                g = esel[:, :, 2, :, :]
                for t in range(TT):
                    tick(eng.tensor_reduce(stat[:, 0, t * HEADS:(t + 1) * HEADS], g[:, t], AX.X, ALU.add))
                eng.wait_ge(dve_step, steps[0])
                settle(eng.reciprocal(stat[:, 1, 0:16], stat[:, 0, 0:16]))
                for t in range(TT):
                    last = eng.tensor_tensor(g[:, t], g[:, t], over(stat[:, 1, t * HEADS:(t + 1) * HEADS], TOPK), ALU.mult)
                    if t == 0:
                        tick(last)
                last.then_inc(n["sel_ready"], 1)
                eng.wait_ge(n["selT_ready"], 1)
                tick(eng.tensor_copy(eselT[:, 0:2, :], bank(4).rearrange("p (w t) -> p w t", w=2)))
                settle(eng.tensor_scalar(eselT[:, 2, :], bank(5, 0, S), GATE_SCALE, None, ALU.mult))
                settle(eng.tensor_copy(ghalf[:, :], eselT[:, 2, :]))
                settle(eng.tensor_copy(eselT[:, 3, :], ghalf[:, :]))
                settle(eng.tensor_tensor(eselT[:, 4, :], eselT[:, 2, :], eselT[:, 3, :], ALU.subtract))

                def hot(g, j, first):
                    if not first:
                        eng.wait_ge(n["gates_ready"], g - 1)
                    for q in range(4):
                        def at(row):
                            return eselT[:, row, bass.ds(g * 4 + q, 1)]
                        eng.tensor_scalar(hot2[:, j, q, :], iota[:, :], at(1), None, ALU.is_equal)
                        for part in range(2):
                            last = eng.tensor_scalar(hot1[:, j, part, q, :], iota[:, :], at(0), at(3 + part),
                                                     ALU.is_equal, ALU.mult)
                    last.then_inc(n["hot_ready"], 1)

                def apply(g, j):
                    eng.wait_ge(n["gates_ready"], g + 1)
                    a = act[:, bass.ds(g * 4, 4), :]
                    eng.scalar_tensor_tensor(a, bank(6 + j).rearrange("p (q k) -> p q k", q=4), 1.0 / GATE_SCALE, a,
                                             ALU.mult, ALU.mult).then_inc(n["gates_used"], 1)

                hot(0, 0, True)
                hot(1, 1, True)
                eng.wait_ge(n["gelu_done"], U_SLOTS)
                apply(0, 0)
                with eng.Fori(0, G_GROUPS // 2 - 1) as k:
                    hot(k * 2 + 2, 0, False)
                    apply(k * 2 + 1, 1)
                    hot(k * 2 + 3, 1, False)
                    apply(k * 2 + 2, 0)
                apply(G_GROUPS - 1, 1)
                eng.wait_ge(n["gates_used"], G_GROUPS)

                def tile(k, j, first):
                    if not first:
                        eng.wait_ge(slot_used, k * RING + (FIRST[f"v{b + 1}"] + j - 1))
                    src = act[:, :, bass.ds(k * (RING * TPS) + j * TPS, TPS)].rearrange("p t e -> p e t")
                    eng.tensor_copy(sel[:, j % 2, :, :], src).then_inc(n["tile_ready"], 1)

                for j in range(RING):
                    tile(0, j, j < 2)
                with eng.Fori(1, U_SLOTS // RING) as k:
                    for j in range(RING):
                        tile(k, j, False)
                eng.wait_ge(n["acc_ready"], 1)
                for a in range(4):
                    c = slice((a % 2) * 512, (a % 2 + 1) * 512)
                    eng.tensor_tensor(xres[:, a // 2, c], xres[:, a // 2, c], bank(a), ALU.add).then_inc(n["done"], 1)

            eng.wait_ge(const_in, N_CONST)
            eng.wait_ge(x_in, 16 * TT)
            norm(0)
            attention1()
            norm(1)
            experts(0)
            norm(2)
            attention2()
            norm(3)
            experts(1)
            eng.wait_ge(fin_sq, TT)
            eng.tensor_scalar(stat[:, 1, 0:TT], stat[:, 0, 0:TT], 1.0 / D, EPS, ALU.mult, ALU.add).then_inc(fin_var, 1)
            eng.wait_ge(fin_std, 1)
            settle(eng.reciprocal(stat[:, 3, 0:TT], stat[:, 2, 0:TT]))
            eng.wait_ge(fgain_in, 16)
            for t in range(TT):
                settle(eng.tensor_scalar(xs[:, t, :], xres[:, t, :], stat[:, 3, t:t + 1], None, ALU.mult))
                eng.tensor_tensor(xs[:, t, :], xs[:, t, :], fgain, ALU.mult).then_inc(fin_ready, 1)


def shape_constants():
    f = np.float32
    half = HD // 2
    pos = np.arange(S, dtype=f)
    freqs = (f(10000.0) ** (-np.arange(half, dtype=f) / f(half))).astype(f)
    ang = pos[:, None] * freqs[None, :]
    cos, sin = np.cos(ang), np.sin(ang)
    cos, sin = np.concatenate([cos, cos], 1), np.concatenate([sin, sin], 1)
    sc = f(HD ** -0.5)
    rope = np.stack([cos, sin, cos * sc, sin * sc], 1).reshape(TT, P, 4 * HD).transpose(1, 0, 2).reshape(P, -1)
    j, i = np.arange(P)[:, None], np.arange(S)[None, :]
    i1 = np.arange(P, S)[None, :]
    lg = np.log1p(-np.exp2(-5.0 - np.arange(HEADS)))

    def decay(key, query):
        d = query - key
        return np.where(d >= 0, np.exp(lg[:, None, None] * np.maximum(d, 0)), 0.0)
    dm = np.concatenate([decay(j, i), decay(j + P, i1)], 2).transpose(1, 0, 2).reshape(P, -1)
    tri = (np.arange(P)[:, None] > np.arange(P)[None, :]).astype(f)
    strict = np.concatenate([j < i, j + P < i1], 1).astype(f)
    c1 = [rope, dm, tri, np.ones((P, P)), strict]
    t = np.arange(P)[:, None]
    s0, s1 = np.arange(P)[None, :], np.arange(S)[None, :]
    slopes = 2.0 ** (-8.0 * np.arange(1, HEADS + 1) / HEADS)

    def alibi(q, k):
        return np.where(k <= q, -slopes[:, None, None] * (q - k), -1.0e30)
    ab = np.concatenate([alibi(t, s0), alibi(t + P, s1)], 2).transpose(1, 0, 2).reshape(P, -1)
    k_, q_ = np.arange(P)[:, None], np.arange(P)[None, :]
    lm = [k_ == q_]
    for l in range(7):
        b = 1 << l
        lm.append((k_ // (2 * b) == q_ // (2 * b)) & (k_ % (2 * b) < b) & (q_ % (2 * b) >= b))
    lm = np.stack(lm, 1).astype(f).reshape(P, -1)
    c2 = [ab, lm, np.ones((P, P))]
    return [a.astype(f) for a in c1], [a.astype(f) for a in c2]


def rows_of(v):
    return np.broadcast_to(np.asarray(v).reshape(1, -1), (P, np.asarray(v).size))


def slot_rows(w, width):
    r, c = w.shape
    return w.reshape(r // P, P, c // width, width).transpose(2, 1, 0, 3).reshape(c // width, P, SLOT)


def u_slots(u):
    return u.reshape(U_SLOTS, TPS, P, KC, P).transpose(0, 4, 1, 3, 2).reshape(U_SLOTS, P, SLOT)


def v_slots(v):
    return v.reshape(U_SLOTS, TPS, P, D).transpose(0, 2, 1, 3).reshape(U_SLOTS, P, SLOT)


def kernel(**inputs):
    import concourse.bacc as _bacc
    from concourse.bass_utils import run_bass_kernel_spmd as _run

    w = {k: np.asarray(v) for k, v in inputs.items()}
    in1, in2 = w["w_in"][0], w["w_in_2"][0]
    parts = [slot_rows(in1[:, a:a + n], SC) for _, a, n in IN1]
    parts += [slot_rows(w["w_branch_ret"][0], SC), slot_rows(w["w_branch_sb"][0], 512), slot_rows(w["w_out"][0], SC),
              slot_rows(w["peer_w_q"][0], SC), u_slots(w["peer_u"][0]), v_slots(w["peer_v"][0])]
    parts += [slot_rows(in2[:, a:a + n], SC) for _, a, n in IN2]
    parts += [slot_rows(w["w_out_2"][0], SC), slot_rows(w["peer_wq_2"][0], SC), u_slots(w["peer_u_2"][0]),
              v_slots(w["peer_v_2"][0])]
    c1, c2 = shape_constants()
    c1 += [rows_of(w[k][0]) for k in ("ret_q_norm", "ret_k_norm", "sb_q_norm", "sb_k_norm")]
    c1 += [rows_of(w["ret_group_norm"][0])]
    c2 += [w["rec_lb_logits_2"].reshape(2, REC_H, P).transpose(2, 0, 1).reshape(P, -1), rows_of(w["rec_norm_g_2"][0])]
    gcol = np.stack([w[k][0].reshape(KC, P) for k in ("norm_attn", "norm_ffn", "norm1_g_2", "norm2_g_2")])
    arrays = {
        "weights": np.concatenate(parts),
        "const1": np.concatenate(c1, 1),
        "const2": np.concatenate(c2, 1),
        "fgain": rows_of(w["normf_g_2"]),
        "gcol": gcol.transpose(2, 0, 1),
        "ident": np.eye(P, dtype=np.float32),
        "zeros": np.zeros((P, P), np.float32),
        "iota": np.broadcast_to(np.arange(NKEY, dtype=np.float16), (P, NKEY)),
        "iota16": np.broadcast_to(np.arange(TOPK, dtype=np.float32), (P, TOPK)),
        "keys1": np.stack([w["peer_sub_keys_1"][0].T, w["peer_sub_keys_2"][0].T], 1),
        "keys2": w["peer_subkeys_2"][0].reshape(HEADS * 2, NKEY, P).transpose(2, 0, 1),
        "x": w["x"],
    }
    arrays = {k: np.ascontiguousarray(v) for k, v in arrays.items()}
    nc = _bacc.Bacc("TRN2", target_bir_lowering=False, num_devices=1)
    ap = {k: nc.dram_tensor("in_" + k, v.shape, mybir.dt.from_np(v.dtype), kind="ExternalInput").ap() for k, v in arrays.items()}
    out = nc.dram_tensor("out", (1, S, D), F32, kind="ExternalOutput").ap()
    block_program(nc, ap["weights"], ap["const1"], ap["const2"], ap, (ap["keys1"], ap["keys2"]), ap["x"], out)
    r = _run(nc, [{"in_" + k: v for k, v in arrays.items()}], core_ids=[0])
    return r.results[0]["out"]
```

```python
from contextlib import ExitStack

import numpy as np
import concourse.bass as bass
from concourse import mybir

P = 128
F32 = mybir.dt.float32
F16 = mybir.dt.float16
F32R = mybir.dt.float32r
U32 = mybir.dt.uint32
ALU = mybir.AluOpType
ACT = mybir.ActivationFunctionType
AX = mybir.AxisListType

D = 1024
S = 256
TT = S // P
KC = D // P
EPS = 1e-6

HEADS = 8
HD = 64
RDV = 128
REC_H = 4
TOPK = 16
NKEY = 128

SLOT = 1024
SC = 256
KH = SLOT // SC
HALVES = KC // KH
RING = 4

IN1 = [("rq", 0, 512), ("rk", 512, 512), ("sq", 3072, 512), ("sk", 3584, 512), ("rv", 1024, 1024),
       ("sv", 4096, 512), ("rg", 2048, 1024), ("ga", 4608, 1024), ("gb", 5632, 1024)]
IN2 = [("qa", 0, 512), ("ka", 512, 512), ("fr", 2048, 512), ("qr", 1536, 512), ("va", 1024, 512),
       ("ir", 2560, 512), ("gr", 3072, 512)]


def slots_of(groups):
    return [(n, o) for n, _, w in groups for o in range(0, w, SC)]


IN1_SLOTS, IN2_SLOTS = slots_of(IN1), slots_of(IN2)
N_EXP = NKEY * NKEY
E_TILES = N_EXP // P
ROUNDS = E_TILES // RING
Q_TILES = 2 * HEADS
HALF = NKEY // 2
HALF_ROUND = ROUNDS // 2
U_MID = 12
GROUPS = S // 4
GATE_SCALE = 2.0 ** 14
assert GROUPS == E_TILES // 2
BEFORE_V = Q_TILES + E_TILES

ORDER = [("in1", HALVES * len(IN1_SLOTS)), ("ret", HALVES * 4), ("sb", 4), ("out1", HALVES * 4), ("q1", Q_TILES),
         ("u1", E_TILES), ("v1", E_TILES), ("in2", HALVES * len(IN2_SLOTS)), ("out2", HALVES * 4), ("q2", Q_TILES),
         ("u2", E_TILES), ("v2", E_TILES)]
FIRST, N_SLOTS = {}, 0
for _name, _n in ORDER:
    FIRST[_name] = N_SLOTS
    N_SLOTS += _n
assert all(FIRST[_k] % RING == 0 for _k in ("q1", "u1", "v1", "in2", "q2", "u2", "v2")) and N_SLOTS % RING == 0

def schedule1():
    steps = []
    for s in range(len(IN1_SLOTS)):
        steps.append(("proj", s))
        if s in (1, 3, 5, 7):
            steps.append(("headnorm", s // 2))
        if s in (3, 5, 7, 9):
            steps.append(("headT", (s - 3) // 2))
        if 12 <= s < 12 + HEADS:
            steps.append(("ret_scores", s - 12))
        if 13 <= s < 13 + HEADS:
            steps.append(("ret_values", s - 13))
        if s == 13 + HEADS:
            steps.append(("ret_norm", 0))
        if 14 <= s < 14 + HEADS:
            steps.append(("sb_scores", s - 14))
        if 15 <= s < 15 + HEADS:
            steps.append(("sb_later", s - 15))
        if 16 <= s < 16 + HEADS:
            steps.append(("sb_values", s - 16))
    return steps


def schedule2():
    steps = [("proj", s) for s in range(8)] + [("rec_prep", 0)] + [("proj", 8), ("proj", 9)]
    for i in range(HEADS + 2):
        if 10 + i < len(IN2_SLOTS):
            steps.append(("proj", 10 + i))
        if i < HEADS:
            steps.append(("m_scores", i))
        if i < 9:
            steps.append(("rec_level", i))
        if 1 <= i <= HEADS:
            steps.append(("m_turn", i - 1))
        if 2 <= i:
            steps.append(("m_values", i - 2))
    return steps


def block_program(nc, weights, const1, const2, gains, keys_in, x, out):
    with ExitStack() as ctx:
        def sb(name, shape, dt=F32):
            return ctx.enter_context(nc.sbuf_tensor(name, shape, dt))

        def over_at(name, base, at, shape, dt=F32):
            return nc.alloc_sbuf_tensor_at(name, shape, dt, offset=offset_of[base] + at)

        def sem(name):
            return ctx.enter_context(nc.semaphore(name))

        offset_of = {}

        def placed(name, shape, dt=F32):
            offset_of[name] = nc.sbuf_base
            return sb(name, shape, dt)

        ring = sb("ring", [P, RING, SLOT])
        whi = sb("whi", [P, RING, SLOT], F32R)
        wlo = sb("wlo", [P, RING, SLOT], F32R)
        act = sb("act", [P, S, NKEY])
        xres = sb("xres", [P, TT, D])
        hT = placed("hT", [P, KC, S])
        hhi = sb("hhi", [P, KC, S], F32R)
        hlo = over_at("hlo", "hT", 0, [P, KC, S], F32R)
        ident = sb("ident", [P, P])
        iota = sb("iota", [P, NKEY], F16)
        iota16 = sb("iota16", [P, TOPK])
        gcol = sb("gcol", [P, 4, KC])
        idx = sb("idx", [P, TT, HEADS, 2, TOPK], U32)
        top = sb("top", [P, TT, HEADS, TOPK])
        pos = sb("pos", [P, TT, HEADS, TOPK], U32)
        val = sb("val", [P, 2, TOPK])
        esel = sb("esel", [P, TT, 3, HEADS, TOPK])
        stat = sb("stat", [P, 8, 16])
        work = placed("work", [P, 3840])
        ps = ctx.enter_context(nc.psum_tensor("ps", [P, 8, 512], F32))

        scores = work[:, 0:2048].rearrange("p (b t c k) -> p b t c k", b=4, t=TT, c=2)
        qT = work[:, 2048:3072].rearrange("p (b c t) -> p b c t", b=2, c=2)
        cand = work[:, 3072:3840].rearrange("p (b k) -> p b k", b=3)
        small = work[:, 2048:2816]
        idxf = small[:, 0:256].rearrange("p (h c k) -> p h c k", h=HEADS, c=2)
        posab = small[:, 256:512].rearrange("p (c h k) -> p c h k", c=2, h=HEADS).bitcast(U32)
        posf = small[:, 512:768].rearrange("p (c h k) -> p c h k", c=2, h=HEADS)
        half16 = work[:, 2048:3840].bitcast(F16)
        rowT = half16[:, 0:4 * S].rearrange("p (w t) -> p w t", w=4)
        hot2 = half16[:, 1024:2048].rearrange("p (b q k) -> p b q k", b=2, q=4)
        hot1 = half16[:, 2048:3072].rearrange("p (b w q k) -> p b w q k", b=2, w=2, q=4)
        eq1 = half16[:, 3072:3584].rearrange("p (b q k) -> p b q k", b=2, q=4)
        shi = over_at("shi", "work", 0, [P, 2, 2, S], F32R)
        slo = over_at("slo", "work", 4096, [P, 2, 2, S], F32R)

        flat = act[:, :, :].rearrange("p a b -> p (a b)")

        def carve(at, *shape):
            n = int(np.prod(shape))
            names = "abcd"[:len(shape)]
            ap = flat[:, at:at + n]
            if len(shape) > 1:
                ap = ap.rearrange(f"p ({' '.join(names)}) -> p {' '.join(names)}",
                                  **{c: k for c, k in zip(names[1:], shape[1:])})
            return ap, at + n

        at = 0
        xs, at = carve(at, TT, D)
        raw1 = {}
        for n, _, w in IN1:
            raw1[n], at = carve(at, TT, w)
        tmp_at = at
        tmpA, at = carve(at, TT, 512)
        tmpB, at = carve(at, TT, 512)
        headsT1 = {}
        for n in ("rq", "rk", "sq", "sk"):
            headsT1[n], at = carve(at, HEADS // 2, S)
        c1, at = carve(at, const1.shape[1])
        retm, at = carve(at, 2, 384)
        rety, _ = carve(tmp_at, TT, HEADS, RDV)
        sbt, at = carve(at, 2, 6, 384)
        keys1, at = carve(at, 2, NKEY)
        assert at <= S * NKEY, at
        start = TT * D
        retT, _ = carve(start, KC, S)
        sbT, _ = carve(start + 2 * TT * 512, HEADS // 2, S)
        mixed, _ = carve(start + 4 * TT * 512, TT, D)
        mT = hT

        cc = 0

        def col(n, *shape):
            nonlocal cc
            k = int(np.prod((n,) + shape))
            ap = c1[:, cc:cc + k]
            cc += k
            return ap
        rope = col(TT * 4 * HD).rearrange("p (t k c) -> p t k c", t=TT, k=4)
        dmask = col(HEADS * 384).rearrange("p (h c) -> p h c", h=HEADS)
        tri = col(P)
        ones = col(P)
        strict = col(384)
        hgain = col(4 * HD).rearrange("p (k c) -> p k c", k=4)
        ggain = col(HEADS * RDV).rearrange("p (h e) -> p h e", h=HEADS)
        assert cc == const1.shape[1]

        at = TT * D
        raw2 = {}
        for n in ("va", "ir", "gr"):
            raw2[n], at = carve(at, TT, 512)
        colT = {}
        for n in ("qa", "ka", "fr", "qr"):
            colT[n], at = carve(at, 4, S)
        c2, at = carve(at, const2.shape[1])
        ml, at = carve(at, 2, 384)
        mpT, at = carve(at, 2, 384)
        catT, at = carve(at, KC, S)
        cum, at = carve(at, REC_H, TT, P)
        kk, at = carve(at, REC_H, TT, P)
        dlt, at = carve(at, REC_H, TT, P)
        qL, at = carve(at, REC_H, TT, P)
        kL, at = carve(at, REC_H, TT, P)
        Ssum, at = carve(at, TT, REC_H, P)
        Sx, at = carve(at, REC_H, P)
        ry, at = carve(at, TT, REC_H, P)
        rt, at = carve(at, TT, REC_H, P)
        lbs, at = carve(at, 8, REC_H)
        keys2, at = carve(at, HEADS * 2, NKEY)
        assert at <= S * NKEY, at
        c2a = c2[:, 0:HEADS * 384].rearrange("p (h c) -> p h c", h=HEADS)
        o = HEADS * 384
        lmask = c2[:, o:o + 8 * P].rearrange("p (l c) -> p l c", l=8)
        o += 8 * P
        ones2 = c2[:, o:o + P]
        o += P
        lbl = c2[:, o:o + 2 * REC_H].rearrange("p (k h) -> p k h", k=2)
        o += 2 * REC_H
        rgain = c2[:, o:o + 512].rearrange("p (h e) -> p h e", h=REC_H)
        o += 512
        assert o == const2.shape[1]
        fgain = flat[:, TT * D:TT * D + D]

        def mstat(h, k, t):
            return stat[:, 4, (h % 2) * 6 + 2 * k + t:(h % 2) * 6 + 2 * k + t + 1]

        def mstat2(h, k):
            return stat[:, 4, (h % 2) * 6 + 2 * k:(h % 2) * 6 + 2 * k + 2]

        def level(ap, l):
            h = 1 << (l - 1)
            if len(ap.shape) == 4:
                ap = ap.rearrange("p h t c -> p (h t c)")
            return ap.rearrange("p (n b) -> p n b", b=2 * h), h

        slot_in = [sem(f"slot_in{j}") for j in range(RING)]
        slot_used = sem("slot_used")
        turn_in = sem("turn_in")
        const_in = sem("const_in")
        const2_in = sem("const2_in")
        keys2_in = sem("keys2_in")
        x_in = sem("x_in")
        out_done = sem("out_done")
        dve_step = sem("dve_step")
        act_step = sem("act_step")
        nsq = sem("norm_sums_ready")
        nvar = sem("norm_var_ready")
        nstd = sem("norm_std_ready")
        nxs = sem("norm_scaled_ready")
        nT = sem("norm_transposed")
        nout = sem("norm_out_ready")
        nfree = sem("norm_out_act")
        proj_copied = sem("proj_copied")
        hvar = sem("head_var_ready")
        hstd = sem("head_std_ready")
        hready = sem("head_ready")
        hTr = sem("head_transposed")
        hTc = sem("head_transposed_copied")
        rs_ready = sem("ret_scores_ready")
        rm_ready = sem("ret_masked_ready")
        rv_ready = sem("ret_values_ready")
        rv_copied = sem("ret_values_copied")
        rg_var = sem("ret_var_ready")
        rg_std = sem("ret_std_ready")
        rg_ready = sem("ret_gated_ready")
        z_ready = sem("sb_scores_ready")
        neg_ready = sem("sb_negabs_ready")
        ln_ready = sem("sb_log_ready")
        stay_ready = sem("sb_stay_ready")
        later_ready = sem("sb_later_ready")
        arg_ready = sem("sb_arg_ready")
        wexp_ready = sem("sb_exp_ready")
        w_ready = sem("sb_weights_ready")
        so_ready = sem("sb_out_ready")
        so_copied = sem("sb_out_copied")
        t_ready = sem("transposed")
        t_copied = sem("transposed_copied")
        ya_used = sem("branch_used")
        mix_ready = sem("mixed_ready")
        o_used = sem("out_proj_used")
        m_ready = sem("moba_scores_ready")
        m_max = sem("moba_max_ready")
        m_exp = sem("moba_exp_ready")
        m_prob = sem("moba_probs_ready")
        m_T = sem("moba_transposed")
        m_Tc = sem("moba_transposed_copied")
        m_out = sem("moba_out_ready")
        m_outc = sem("moba_out_copied")
        g_lbm = sem("rec_lb_max_ready")
        g_lbe = sem("rec_lb_exp_ready")
        g_f = sem("rec_forget_ready")
        g_log = sem("rec_log_ready")
        g_dlt = sem("rec_diff_ready")
        g_exp = sem("rec_exp_ready")
        g_qk = sem("rec_level_ready")
        g_s = sem("rec_scores_ready")
        g_sc = sem("rec_scores_used")
        g_sum = sem("rec_sum_ready")
        g_sx = sem("rec_cross_copied")
        g_y = sem("rec_values_ready")
        g_yc = sem("rec_values_copied")
        g_var = sem("rec_var_ready")
        g_std = sem("rec_std_ready")
        g_out = sem("rec_gated_ready")
        peer = []
        for b in (1, 2):
            peer.append({n: sem(f"peer{b}_{n}") for n in (
                "hlo_ready", "q_copied", "s_ready", "s_copied", "scores_used", "hi_ready", "lo_pool",
                "gelu_done", "sums_ready", "exp_ready", "sel_ready", "selT_ready", "rows_ready", "eq_ready", "hot_ready",
                "gates_ready", "gates_used", "shi_ready", "pair_ready", "acc_ready", "done")})
        fin_sq = sem("final_sum_ready")
        fin_var = sem("final_var_ready")
        fin_std = sem("final_std_ready")
        fin_ready = sem("final_ready")
        fgain_in = sem("final_gain_in")

        block = ctx.enter_context(nc.Block())

        def bank(i, a=0, b=512):
            return ps[:, i, a:b]

        def slot_ready(pe, i):
            pe.wait_ge(slot_in[i % RING], 16 * (i // RING + 1))

        @block.sync
        def _(sp):
            def load(k, j):
                sp.dma_start(ring[:, j, :], weights[k * RING + j]).then_inc(slot_in[j], 16)

            for j in range(RING):
                load(0, j)
            for b in range(2):
                n = peer[b]
                first, q, end = ((1, FIRST["q1"] // RING, FIRST["in2"] // RING),
                                 (FIRST["in2"] // RING, FIRST["q2"] // RING, N_SLOTS // RING))[b]
                if b:
                    for j in range(RING):
                        sp.wait_ge(peer[0]["lo_pool"], BEFORE_V + E_TILES - RING + j + 1)
                        load(first, j)
                    first += 1
                with sp.Fori(first, q + 1) as k:
                    for j in range(RING):
                        sp.wait_ge(slot_used, k * RING + (j - RING + 1))
                        load(k, j)
                with sp.Fori(q + 1, end) as k:
                    for j in range(RING):
                        sp.wait_ge(n["lo_pool"], k * RING + (j + 1 - RING - q * RING))
                        load(k, j)

        @block.gpsimd
        def _(pool):
            for b in range(2):
                n = peer[b]
                with pool.Fori(0, (BEFORE_V + E_TILES) // RING) as k:
                    for j in range(RING):
                        pool.wait_ge(n["hi_ready"], k * RING + (j + 1))
                        pool.tensor_tensor(wlo[:, j, :], ring[:, j, :], whi[:, j, :].bitcast(F32), ALU.subtract)\
                            .then_inc(n["lo_pool"], 1)

        N_TURN, N_CONST = 16 * 2, 16 * 4

        def tiles(ap):
            return ap.rearrange("p t (h c) -> p (t h) c", c=HD)

        @block.tensor
        def _(pe):
            def norm_transposes(k):
                pe.wait_ge(nxs, TT * (k + 1))
                for b in range(4):
                    for j in range(2):
                        for t in range(TT):
                            mm = pe.transpose(bank(b, j * S + t * P, j * S + (t + 1) * P),
                                              xs[:, t, (2 * b + j) * P:(2 * b + j + 1) * P], ident[:, :])
                    mm.then_inc(nT, 1)
                if k % 2 == 0:
                    pe.wait_ge(nout, 4 * (k + 1))
                    pe.wait_ge(nfree, 4 * (k + 1))

            def turn16(src, k):
                for b in range(4):
                    for j in range(2):
                        for t in range(TT):
                            mm = pe.transpose(bank(b, j * S + t * P, j * S + (t + 1) * P), src(t, 2 * b + j),
                                              ident[:, :])
                    mm.then_inc(t_ready, 1)
                pe.wait_ge(t_copied, 4 * (k + 1))

            def natural(lhs, i, u, wait, halves=HALVES):
                for half in range(halves):
                    slot_ready(pe, i + half)
                    if u >= 2 and half == 0:
                        pe.wait_ge(wait, u - 1)
                    for t in range(TT):
                        for c in range(KH):
                            kc = half * KH + c
                            mm = pe.matmul(bank(4 + u % 2, t * SC, (t + 1) * SC), lhs[:, kc, t * P:(t + 1) * P],
                                           ring[:, (i + half) % RING, c * SC:(c + 1) * SC], start=(kc + t == 0),
                                           stop=(half == halves - 1 and c == KH - 1), skip_group_check=True)
                    mm.then_inc(slot_used, 1)

            def columns(i, u, wait):
                for half in range(HALVES):
                    slot_ready(pe, i + half)
                    if u >= 2 and half == 0:
                        pe.wait_ge(wait, u - 1)
                    for t in range(2):
                        for c in range(KH):
                            kc = half * KH + c
                            mm = pe.matmul(bank(4 + u % 2, t * S, (t + 1) * S),
                                           ring[:, (i + half) % RING, c * SC + t * P:c * SC + (t + 1) * P], hT[:, kc, :],
                                           start=(kc + t == 0), stop=(half == HALVES - 1 and c == KH - 1),
                                           skip_group_check=True)
                    mm.then_inc(slot_used, 1)

            def rows(h):
                return slice(HD * (h % 2), HD * (h % 2) + HD)

            def attention1():
                for what, i in schedule1():
                    if what == "proj":
                        natural(hT, HALVES * i, i, proj_copied)
                    elif what == "headT":
                        name = ("rq", "rk", "sq", "sk")[i]
                        pe.wait_ge(hready, i + 1)
                        for r in range(2):
                            if 2 * i + r:
                                pe.wait_ge(hTc, 2 * i + r)
                            for j in range(2):
                                for t in range(TT):
                                    c = (2 * r + j) * P
                                    mm = pe.transpose(bank(7, j * S + t * P, j * S + (t + 1) * P),
                                                      raw1[name][:, t, c:c + P], ident[:, :])
                            mm.then_inc(hTr, 1)
                    elif what == "ret_scores":
                        if i == 0:
                            pe.wait_ge(hTc, 4)
                        else:
                            pe.wait_ge(rm_ready, i)
                        q, kT = headsT1["rq"][rows(i), i // 2, :], headsT1["rk"][rows(i), i // 2, :]
                        pe.matmul(bank(3, 0, S), kT[:, 0:P], q, start=True, stop=True)
                        pe.matmul(bank(3, S, S + P), kT[:, P:S], q[:, P:S], start=True, stop=True).then_inc(rs_ready, 1)
                    elif what == "ret_values":
                        pe.wait_ge(rm_ready, i + 1)
                        if i == 0:
                            pe.wait_ge(proj_copied, 12)
                        else:
                            pe.wait_ge(rv_copied, i)
                        m, v = retm[:, i % 2, :], raw1["rv"][:, :, i * RDV:(i + 1) * RDV]
                        pe.matmul(bank(6, 0, P), m[:, 0:P], v[:, 0, :], start=True, stop=True)
                        pe.matmul(bank(6, P, 2 * P), m[:, P:S], v[:, 0, :], start=True, stop=False)
                        pe.matmul(bank(6, P, 2 * P), m[:, S:S + P], v[:, 1, :], start=False, stop=True)\
                          .then_inc(rv_ready, 1)
                    elif what == "sb_scores":
                        if i == 0:
                            pe.wait_ge(hTc, 8)
                        else:
                            pe.wait_ge(neg_ready, i)
                        q, kT = headsT1["sq"][rows(i), i // 2, :], headsT1["sk"][rows(i), i // 2, :]
                        pe.matmul(bank(0, 0, S), kT[:, 0:P], q, start=True, stop=True)
                        pe.matmul(bank(0, S, S + P), kT[:, P:S], q[:, P:S], start=True, stop=True).then_inc(z_ready, 1)
                    elif what == "sb_later":
                        pe.wait_ge(stay_ready, i + 1)
                        if i:
                            pe.wait_ge(arg_ready, i)
                        ls = sbt[:, i % 2, 0, :]
                        pe.matmul(bank(1, 0, S), tri, ls[:, 0:S], start=True, stop=False, skip_group_check=True)
                        pe.matmul(bank(1, P, S), ones, ls[:, S:S + P], start=False, stop=True, skip_group_check=True)
                        pe.matmul(bank(1, S, S + P), tri, ls[:, S:S + P], start=True, stop=True,
                                  skip_group_check=True).then_inc(later_ready, 1)
                    elif what == "sb_values":
                        pe.wait_ge(w_ready, i + 1)
                        if i == 0:
                            pe.wait_ge(proj_copied, 14)
                        if i >= 2:
                            pe.wait_ge(so_copied, i - 1)
                        w, v = sbt[:, i % 2, 5, :], raw1["sv"][:, :, i * HD:(i + 1) * HD]
                        pe.matmul(ps[rows(i), 2, 0:S], v[:, 0, :], w[:, 0:S], start=True, stop=False,
                                  skip_group_check=True)
                        pe.matmul(ps[rows(i), 2, P:S], v[:, 1, :], w[:, S:S + P], start=False, stop=True,
                                  skip_group_check=True).then_inc(so_ready, 1)
                pe.wait_ge(rg_ready, 1)
                pe.wait_ge(so_copied, HEADS)
                turn16(lambda t, c: rety[:, t, c, :], 0)
                pe.wait_ge(proj_copied, len(IN1_SLOTS))
                for u in range(4):
                    natural(retT, FIRST["ret"] + HALVES * u, u, ya_used)
                for u in range(4):
                    natural(sbT, FIRST["sb"] + u, 4 + u, ya_used, 1)
                pe.wait_ge(mix_ready, 1)
                turn16(lambda t, c: mixed[:, t, c * P:(c + 1) * P], 1)
                for u in range(4):
                    natural(mT, FIRST["out1"] + HALVES * u, u, o_used)

            def attention2():
                base = len(IN1_SLOTS)
                pe.wait_ge(const2_in, 16)
                for what, i in schedule2():
                    if what == "proj":
                        if IN2_SLOTS[i][0] in colT:
                            columns(FIRST["in2"] + HALVES * i, base + i, proj_copied)
                        else:
                            natural(hT, FIRST["in2"] + HALVES * i, base + i, proj_copied)
                    elif what == "m_scores":
                        if i == 0:
                            pe.wait_ge(proj_copied, base + 4)
                        else:
                            pe.wait_ge(m_max, i)
                        q, kT = colT["qa"][rows(i), i // 2, :], colT["ka"][rows(i), i // 2, :]
                        pe.matmul(bank(0, 0, P), q[:, 0:P], kT[:, 0:P], start=True, stop=True)
                        pe.matmul(bank(0, P, P + S), q[:, P:S], kT, start=True, stop=True).then_inc(m_ready, 1)
                    elif what == "m_turn":
                        pe.wait_ge(m_prob, i + 1)
                        if i:
                            pe.wait_ge(m_Tc, i)
                        p = ml[:, i % 2, :]
                        for c in range(3):
                            mm = pe.transpose(bank(1, c * P, (c + 1) * P), p[:, c * P:(c + 1) * P], ident[:, :])
                        mm.then_inc(m_T, 1)
                    elif what == "m_values":
                        pe.wait_ge(m_Tc, i + 1)
                        if i == 0:
                            pe.wait_ge(proj_copied, base + 10)
                        if i >= 2:
                            pe.wait_ge(m_outc, i - 1)
                        w, v = mpT[:, i % 2, :], raw2["va"][:, :, i * HD:(i + 1) * HD]
                        pe.matmul(ps[rows(i), 2, 0:S], v[:, 0, :], w[:, 0:S], start=True, stop=False,
                                  skip_group_check=True)
                        pe.matmul(ps[rows(i), 2, P:S], v[:, 1, :], w[:, S:S + P], start=False, stop=True,
                                  skip_group_check=True).then_inc(m_out, 1)
                    elif what == "rec_level":
                        pe.wait_ge(g_qk, i + 1)
                        kl, ql = (kk, colT["qr"].rearrange("p h (t c) -> p h t c", t=TT)) if i == 0 else (kL, qL)
                        if i < 8:
                            for t in range(TT):
                                if i:
                                    pe.wait_ge(g_sc, TT * (i - 1) + t + 1)
                                for h in range(REC_H):
                                    mm = pe.matmul(bank(6 + t, h * P, (h + 1) * P), kl[:, h, t, :], ql[:, h, t, :],
                                                   start=True, stop=True)
                                mm.then_inc(g_s, 1)
                        else:
                            pe.wait_ge(g_sc, TT * 8 - 1)
                            for h in range(REC_H):
                                mm = pe.matmul(bank(6, h * P, (h + 1) * P), kl[:, h, 0, :], ql[:, h, 1, :],
                                               start=True, stop=True)
                            mm.then_inc(g_s, 1)
                pe.wait_ge(g_sx, 1)
                pe.wait_ge(g_sc, TT * 8)
                ir = raw2["ir"]
                for t in range(TT):
                    for h in range(REC_H):
                        mm = pe.matmul(bank(6 + t, h * P, (h + 1) * P), Ssum[:, t, h, :], ir[:, t, h * P:(h + 1) * P],
                                       start=True, stop=(t == 0))
                        if t:
                            mm = pe.matmul(bank(6 + t, h * P, (h + 1) * P), Sx[:, h, :], ir[:, 0, h * P:(h + 1) * P],
                                           start=False, stop=True)
                    mm.then_inc(g_y, 1)
                pe.wait_ge(g_out, 1)
                for b in range(2):
                    for j in range(2):
                        for t in range(TT):
                            mm = pe.transpose(bank(6 + b, j * S + t * P, j * S + (t + 1) * P), ry[:, t, 2 * b + j, :],
                                              ident[:, :])
                    mm.then_inc(t_ready, 1)
                pe.wait_ge(t_copied, 8 + 2)
                pe.wait_ge(m_outc, HEADS)
                for u in range(4):
                    natural(catT, FIRST["out2"] + HALVES * u, 4 + u, o_used)

            def split_product(dst, wide, narrow, start, stop):
                pe.matmul(dst, wide[0], narrow[0], start=start, stop=False, skip_group_check=True)
                pe.matmul(dst, wide[0], narrow[1], start=False, stop=False, skip_group_check=True)
                return pe.matmul(dst, wide[1], narrow[0], start=False, stop=stop, skip_group_check=True)

            def experts(b, keys):
                n = peer[b]
                first_q, first_u, first_v = FIRST[f"q{b + 1}"], FIRST[f"u{b + 1}"], FIRST[f"v{b + 1}"]
                pe.wait_ge(n["hlo_ready"], 4)

                def tile(j, dst):
                    for kc in range(KC):
                        c = slice(kc * P, (kc + 1) * P)
                        mm = split_product(dst, (whi[:, j, c], wlo[:, j, c]), (hhi[:, kc, :], hlo[:, kc, :]),
                                           kc == 0, kc == KC - 1)
                    mm.then_inc(slot_used, 1)

                for h in range(HEADS + 1):
                    if h < HEADS:
                        for c in range(2):
                            pe.wait_ge(n["lo_pool"], 2 * h + c + 1)
                            if h >= 2 and c == 0:
                                pe.wait_ge(n["q_copied"], h - 1)
                            tile((2 * h + c) % RING, bank(4 + h % 2, c * S, (c + 1) * S))
                    if h:
                        g = h - 1
                        pe.wait_ge(n["q_copied"], g + 1)
                        if g >= 2:
                            pe.wait_ge(n["s_copied"], g - 1)
                        for t in range(TT):
                            for c in range(2):
                                kT = keys[:, c if b == 0 else 2 * g + c, :]
                                mm = pe.matmul(bank(6 + g % 2, (2 * t + c) * P, (2 * t + c + 1) * P),
                                               qT[:, g % 2, c, t * P:(t + 1) * P], kT, start=True, stop=True)
                        mm.then_inc(n["s_ready"], 1)

                def gates(k, base, j):
                    pe.wait_ge(n["hot_ready"], k * RING + (base + j + 1))
                    if not (isinstance(k, int) and k * RING + base + j < 2):
                        pe.wait_ge(n["gates_used"], k * RING + (base + j - 1))
                    for q in range(4):
                        for w in range(2):
                            mm = pe.matmul(bank(6 + j % 2, q * HALF, (q + 1) * HALF), hot2[:, j % 2, q, :],
                                           hot1[:, j % 2, w, q, :], start=(q + w == 0), stop=(w == 1), skip_group_check=True)
                    mm.then_inc(n["gates_ready"], 1)

                def u_round(k, first=False, gated=False):
                    for j in range(RING):
                        pe.wait_ge(n["lo_pool"], k * RING + (Q_TILES + j + 1))
                        if j % 2 == 0 and not first:
                            pe.wait_ge(n["gelu_done"], k * 2 + (j // 2 - 1))
                        tile(j, bank(j // 2, (j % 2) * S, (j % 2 + 1) * S))
                        if gated:
                            gates(k, -HALF_ROUND * RING, j)

                u_round(0, first=True)
                with pe.Fori(1, U_MID) as k:
                    u_round(k)
                pe.wait_ge(n["sel_ready"], 1)
                pe.wait_ge(n["s_copied"], HEADS)
                for w in range(3):
                    for t in range(TT):
                        mm = pe.transpose(bank(4 + w // 2, (w % 2) * S + t * P, (w % 2) * S + (t + 1) * P),
                                          esel[:, t, w, :, :].rearrange("p h k -> p (h k)"), ident[:, :])
                mm.then_inc(n["selT_ready"], 1)
                with pe.Fori(U_MID, HALF_ROUND) as k:
                    u_round(k)
                u_round(HALF_ROUND, gated=True)
                with pe.Fori(HALF_ROUND + 1, ROUNDS) as k:
                    u_round(k, gated=True)

                pe.wait_ge(n["gelu_done"], E_TILES // 2)

                def v_round(k, first=False, last=False, gated=False):
                    for j in range(RING):
                        pe.wait_ge(n["lo_pool"], k * RING + (BEFORE_V + j + 1))
                        if j % 2 == 0:
                            pe.wait_ge(n["pair_ready"], k * 2 + (j // 2 + 1))
                        for t in range(TT):
                            for half in range(2):
                                c, a = slice(half * 512, (half + 1) * 512), slice(t * P, (t + 1) * P)
                                mm = split_product(bank(2 * t + half),
                                                   (shi[:, j // 2, j % 2, a], slo[:, j // 2, j % 2, a]),
                                                   (whi[:, j, c], wlo[:, j, c]), first and j == 0, last and j == RING - 1)
                        mm.then_inc(slot_used, 1)
                        if gated:
                            gates(k, GROUPS, j)

                v_round(0, first=True, gated=True)
                with pe.Fori(1, HALF_ROUND) as k:
                    v_round(k, gated=True)
                with pe.Fori(HALF_ROUND, ROUNDS - 1) as k:
                    v_round(k)
                v_round(ROUNDS - 1, last=True)
                pe.wait_ge(slot_used, first_v + E_TILES)
                pe.nop().then_inc(n["acc_ready"], 1)

            pe.wait_ge(turn_in, N_TURN)
            norm_transposes(0)
            pe.wait_ge(const_in, N_CONST)
            attention1()
            norm_transposes(1)
            experts(0, keys1)
            norm_transposes(2)
            attention2()
            norm_transposes(3)
            pe.wait_ge(keys2_in, 16)
            experts(1, keys2)

        @block.scalar
        def _(eng):
            steps = [0]

            def settle(ins):
                steps[0] += 1
                ins.then_inc(act_step, 1)
                eng.wait_ge(act_step, steps[0])

            def norm(k, sem_in, count):
                eng.wait_ge(sem_in, count)
                for t in range(TT):
                    eng.activation(xs[:, t, :], xres[:, t, :], ACT.Square, accum_out=stat[:, 0, t:t + 1])\
                       .then_inc(nsq, 1)
                eng.wait_ge(nvar, k + 1)
                eng.activation(stat[:, 2, 0:TT], stat[:, 1, 0:TT], ACT.Sqrt).then_inc(nstd, 1)
                for b in (1, 3):
                    eng.wait_ge(nT, 4 * k + b + 1)
                    for j in range(2):
                        c = 2 * b + j
                        if k % 2:
                            eng.activation(hhi[:, c, :], bank(b, j * S, (j + 1) * S), ACT.Copy, scale=gcol[:, k, c:c + 1])
                        eng.activation(hT[:, c, :], bank(b, j * S, (j + 1) * S), ACT.Copy, scale=gcol[:, k, c:c + 1])\
                           .then_inc(nfree, 1)

            def turned(dst, k):
                for b in range(4):
                    eng.wait_ge(t_ready, 4 * k + b + 1)
                    eng.activation(dst[:, 2 * b:2 * b + 2, :], bank(b).rearrange("p (j c) -> p j c", j=2), ACT.Copy)\
                       .then_inc(t_copied, 1)

            def rows(h):
                return slice(HD * (h % 2), HD * (h % 2) + HD)

            FUNC = {"rg": ACT.Silu, "ga": ACT.Sigmoid, "gb": ACT.Sigmoid, "qr": ACT.Silu, "gr": ACT.Silu,
                    "fr": ACT.Sigmoid}

            def attention1():
                for what, i in schedule1():
                    if what == "proj":
                        name, off = IN1_SLOTS[i]
                        eng.wait_ge(slot_used, HALVES * (i + 1))
                        eng.activation(raw1[name][:, :, off:off + SC], bank(4 + i % 2).rearrange("p (t c) -> p t c", t=TT),
                                       FUNC.get(name, ACT.Copy)).then_inc(proj_copied, 1)
                    elif what == "headnorm":
                        eng.wait_ge(hvar, i + 1)
                        eng.activation(stat[:, 7, :], stat[:, 6, :], ACT.Sqrt).then_inc(hstd, 1)
                    elif what == "headT":
                        name = ("rq", "rk", "sq", "sk")[i]
                        for r in range(2):
                            eng.wait_ge(hTr, 2 * i + r + 1)
                            eng.activation(headsT1[name][:, 2 * r:2 * r + 2, :],
                                           bank(7).rearrange("p (j c) -> p j c", j=2), ACT.Copy).then_inc(hTc, 1)
                    elif what == "ret_values":
                        eng.wait_ge(rv_ready, i + 1)
                        eng.activation(rety[:, :, i, :], bank(6, 0, S).rearrange("p (t c) -> p t c", t=TT), ACT.Copy)\
                           .then_inc(rv_copied, 1)
                    elif what == "ret_norm":
                        eng.wait_ge(rg_var, 1)
                        eng.activation(stat[:, 4, :], stat[:, 5, :], ACT.Sqrt).then_inc(rg_std, 1)
                    elif what == "sb_scores":
                        eng.wait_ge(neg_ready, i + 1)
                        b = sbt[:, i % 2, :, :]
                        settle(eng.activation(b[:, 3, :], b[:, 2, :], ACT.Exp))
                        eng.activation(b[:, 4, :], b[:, 3, :], ACT.Ln, bias=1.0).then_inc(ln_ready, 1)
                    elif what == "sb_later":
                        eng.wait_ge(arg_ready, i + 1)
                        b = sbt[:, i % 2, :, :]
                        eng.activation(b[:, 3, :], b[:, 2, :], ACT.Exp).then_inc(wexp_ready, 1)
                    elif what == "sb_values":
                        eng.wait_ge(so_ready, i + 1)
                        eng.activation(sbT[rows(i), i // 2, :], ps[rows(i), 2, 0:S], ACT.Copy).then_inc(so_copied, 1)
                turned(retT, 0)
                turned(mT, 1)

            def attention2():
                base = len(IN1_SLOTS)
                eng.wait_ge(g_lbm, 1)
                eng.activation(lbs[:, 4:6, :], lbs[:, 2:4, :], ACT.Exp).then_inc(g_lbe, 1)
                for what, i in schedule2():
                    if what == "proj":
                        name, off = IN2_SLOTS[i]
                        u = base + i
                        eng.wait_ge(slot_used, FIRST["in2"] + HALVES * (i + 1))
                        dst = (colT[name][:, off // P:off // P + 2, :] if name in colT else raw2[name][:, :, off:off + SC])
                        eng.activation(dst, bank(4 + u % 2).rearrange("p (t c) -> p t c", t=2), FUNC.get(name, ACT.Copy))\
                           .then_inc(proj_copied, 1)
                    elif what == "m_scores":
                        eng.wait_ge(m_max, i + 1)
                        for t in range(TT):
                            c = slice(0, P) if t == 0 else slice(P, P + S)
                            eng.activation(ml[:, i % 2, c], ml[:, i % 2, c], ACT.Exp, bias=mstat(i, 0, t),
                                           accum_out=mstat(i, 1, t)).then_inc(m_exp, 1)
                    elif what == "m_turn":
                        eng.wait_ge(m_T, i + 1)
                        if i >= 2:
                            eng.wait_ge(m_out, i - 1)
                        eng.activation(mpT[:, i % 2, :], bank(1, 0, 384), ACT.Copy).then_inc(m_Tc, 1)
                    elif what == "m_values":
                        eng.wait_ge(m_out, i + 1)
                        eng.activation(catT[rows(i), i // 2, :], ps[rows(i), 2, 0:S], ACT.Copy).then_inc(m_outc, 1)
                    elif what == "rec_prep":
                        eng.wait_ge(g_f, 1)
                        eng.activation(dlt.rearrange("p h t c -> p (h t c)"), colT["fr"].rearrange("p h c -> p (h c)"),
                                       ACT.Ln).then_inc(g_log, 1)
                    elif what == "rec_level" and i:
                        eng.wait_ge(g_dlt, i)
                        if i < 8:
                            v, h = level(dlt, i)
                            eng.activation(v[:, :, h:], v[:, :, h:], ACT.Exp)
                            eng.activation(v[:, :, 0:h], v[:, :, 0:h], ACT.Exp, scale=-1.0).then_inc(g_exp, 1)
                        else:
                            eng.activation(dlt[:, :, 0, :], dlt[:, :, 0, :], ACT.Exp, scale=-1.0)
                            eng.activation(dlt[:, :, 1, :], cum[:, :, 1, :], ACT.Exp).then_inc(g_exp, 1)
                            eng.wait_ge(g_s, TT * 8 + 1)
                            eng.activation(Sx.rearrange("p h c -> p (h c)"), bank(6), ACT.Copy).then_inc(g_sx, 1)
                for t in range(TT):
                    eng.wait_ge(g_y, t + 1)
                    eng.activation(ry[:, t, :, :].rearrange("p h c -> p (h c)"), bank(6 + t), ACT.Copy).then_inc(g_yc, 1)
                eng.wait_ge(g_var, 1)
                eng.activation(stat[:, 7, 0:8], stat[:, 6, 0:8], ACT.Sqrt).then_inc(g_std, 1)
                for b in range(2):
                    eng.wait_ge(t_ready, 8 + b + 1)
                    eng.activation(catT[:, 4 + 2 * b:6 + 2 * b, :], bank(6 + b).rearrange("p (j c) -> p j c", j=2),
                                   ACT.Copy).then_inc(t_copied, 1)

            def experts(b):
                n = peer[b]
                first_q, first_u, first_v = FIRST[f"q{b + 1}"], FIRST[f"u{b + 1}"], FIRST[f"v{b + 1}"]

                def high(m, j, k=0, fresh=False):
                    m = m - first_q
                    eng.wait_ge(slot_in[j], k * 16 + 16 * ((first_q + m) // RING + 1))
                    eng.wait_ge(slot_used, k * RING + (first_q + m - RING + 1))
                    eng.activation(whi[:, j, :], ring[:, j, :], ACT.Copy).then_inc(n["hi_ready"], 1)

                for j in range(RING):
                    high(first_q + j, j)
                for h in range(HEADS + 1):
                    if h < HEADS:
                        eng.wait_ge(slot_used, first_q + 2 * h + 2)
                        if h >= 2:
                            eng.wait_ge(n["s_ready"], h - 1)
                        eng.activation(qT[:, h % 2, :, :], bank(4 + h % 2).rearrange("p (c t) -> p c t", c=2), ACT.Copy)\
                           .then_inc(n["q_copied"], 1)
                        for c in range(2):
                            high(first_q + 2 * h + c + RING, (2 * h + c) % RING)
                    if h:
                        eng.wait_ge(n["s_ready"], h)
                        if h > 4:
                            eng.wait_ge(n["scores_used"], h - 4)
                        eng.activation(scores[:, (h - 1) % 4, :, :, :],
                                       bank(6 + (h - 1) % 2).rearrange("p (t c k) -> p t c k", t=TT, c=2), ACT.Copy)\
                           .then_inc(n["s_copied"], 1)

                def u_round(k):
                    for j in range(0, RING, 2):
                        high(first_u + j + RING, j, k)
                        high(first_u + j + 1 + RING, j + 1, k)
                        dst = act[:, :, bass.ds(k * RING + j, 2)].rearrange("p t e -> p e t")
                        eng.activation(dst, bank(j // 2).rearrange("p (e t) -> p e t", e=2),
                                       ACT.Gelu_apprx_tanh if b == 0 else ACT.Gelu).then_inc(n["gelu_done"], 1)

                with eng.Fori(0, U_MID) as k:
                    u_round(k)
                eng.wait_ge(n["sums_ready"], 1)
                eng.activation(esel[:, :, 2, :, :].rearrange("p t h k -> p t (h k)"),
                               esel[:, :, 2, :, :].rearrange("p t h k -> p t (h k)"), ACT.Exp).then_inc(n["exp_ready"], 1)
                with eng.Fori(U_MID, ROUNDS) as k:
                    u_round(k)

                with eng.Fori(0, ROUNDS - 1) as k:
                    for j in range(RING):
                        high(first_v + j + RING, j, k)

            for t in range(TT):
                eng.dma_start(xres[:, t, :], x[0, t * P:(t + 1) * P, :]).then_inc(x_in, 16)
            eng.dma_start(ident[:, :], gains["ident"]).then_inc(turn_in, 16)
            eng.dma_start(gcol[:, :, :], gains["gcol"]).then_inc(turn_in, 16)
            eng.dma_start(c1, const1).then_inc(const_in, 16)
            eng.dma_start(keys1[:, :, :], keys_in[0]).then_inc(const_in, 16)
            eng.dma_start(iota[:, :], gains["iota"]).then_inc(const_in, 16)
            eng.dma_start(iota16[:, :], gains["iota16"]).then_inc(const_in, 16)
            eng.wait_ge(turn_in, N_TURN)
            norm(0, x_in, 16 * TT)
            attention1()
            norm(1, o_used, 4)
            eng.wait_ge(const_in, N_CONST)
            experts(0)
            eng.wait_ge(peer[0]["done"], 4)
            eng.dma_start(c2, const2).then_inc(const2_in, 16)
            eng.dma_start(keys2, keys_in[1]).then_inc(keys2_in, 16)
            norm(2, peer[0]["done"], 4)
            attention2()
            norm(3, o_used, 8)
            experts(1)
            eng.wait_ge(peer[1]["done"], 4)
            eng.dma_start(fgain, gains["fgain"]).then_inc(fgain_in, 16)
            for t in range(TT):
                eng.activation(xs[:, t, :], xres[:, t, :], ACT.Square, accum_out=stat[:, 0, t:t + 1]).then_inc(fin_sq, 1)
            eng.wait_ge(fin_var, 1)
            eng.activation(stat[:, 2, 0:TT], stat[:, 1, 0:TT], ACT.Sqrt).then_inc(fin_std, 1)
            for t in range(TT):
                eng.wait_ge(fin_ready, t + 1)
                eng.dma_start(out[0, t * P:(t + 1) * P, :], xs[:, t, :]).then_inc(out_done, 16)
            eng.wait_ge(out_done, 16 * TT)

        @block.vector
        def _(eng):
            steps = [0]

            def tick(ins):
                steps[0] += 1
                ins.then_inc(dve_step, 1)

            def settle(ins):
                tick(ins)
                eng.wait_ge(dve_step, steps[0])

            def norm(k):
                eng.wait_ge(nsq, TT * (k + 1))
                eng.tensor_scalar(stat[:, 1, 0:TT], stat[:, 0, 0:TT], 1.0 / D, EPS, ALU.mult, ALU.add).then_inc(nvar, 1)
                eng.wait_ge(nstd, k + 1)
                settle(eng.reciprocal(stat[:, 3, 0:TT], stat[:, 2, 0:TT]))
                for t in range(TT):
                    eng.tensor_scalar(xs[:, t, :], xres[:, t, :], stat[:, 3, t:t + 1], None, ALU.mult).then_inc(nxs, 1)
                for b in (0, 2):
                    eng.wait_ge(nT, 4 * k + b + 1)
                    for j in range(2):
                        c = 2 * b + j
                        if k % 2:
                            eng.tensor_scalar(hhi[:, c, :], bank(b, j * S, (j + 1) * S), gcol[:, k, c:c + 1], None, ALU.mult)
                        eng.tensor_scalar(hT[:, c, :], bank(b, j * S, (j + 1) * S), gcol[:, k, c:c + 1], None, ALU.mult)\
                           .then_inc(nout, 1)
                if k % 2:
                    eng.wait_ge(nout, 4 * (k + 1))
                    eng.wait_ge(nfree, 4 * (k + 1))
                    for b in range(4):
                        c = slice(2 * b, 2 * b + 2)
                        eng.tensor_tensor(hlo[:, c, :], hT[:, c, :], hhi[:, c, :].bitcast(F32), ALU.subtract)\
                           .then_inc(peer[k // 2]["hlo_ready"], 1)

            def over(ap, n):
                return ap.unsqueeze(2).to_broadcast([P, ap.shape[1], n])

            def attention1():
                for what, i in schedule1():
                    if what == "headnorm":
                        name = ("rq", "rk", "sq", "sk")[i]
                        X = tiles(raw1[name])
                        A, B = tiles(tmpA), tiles(tmpB)
                        eng.wait_ge(proj_copied, 2 * i + 2)
                        if i:
                            eng.wait_ge(hready, i)
                        settle(eng.tensor_tensor(A, X, X, ALU.mult))
                        settle(eng.tensor_reduce(stat[:, 5, :], A, AX.X, ALU.add))
                        eng.tensor_scalar(stat[:, 6, :], stat[:, 5, :], 1.0 / HD, EPS, ALU.mult, ALU.add).then_inc(hvar, 1)
                        eng.wait_ge(hstd, i + 1)
                        settle(eng.reciprocal(stat[:, 5, :], stat[:, 7, :]))
                        settle(eng.tensor_tensor(X, X, over(stat[:, 5, :], HD), ALU.mult))
                        g = hgain[:, i:i + 1, :].to_broadcast([P, 16, HD])
                        last = eng.tensor_tensor(X, X, g, ALU.mult)
                        if i < 2:
                            settle(last)
                            X4, A4, B4 = (v.rearrange("p (t h) c -> p t h c", t=TT) for v in (X, A, B))
                            for t in range(TT):
                                cs = rope[:, t, 2 * i:2 * i + 1, :].to_broadcast([P, HEADS, HD])
                                sn = rope[:, t, 2 * i + 1:2 * i + 2, :].to_broadcast([P, HEADS, HD])
                                tick(eng.tensor_tensor(A4[:, t], X4[:, t], cs, ALU.mult))
                                settle(eng.tensor_tensor(B4[:, t], X4[:, t], sn, ALU.mult))
                            H2 = HD // 2
                            tick(eng.tensor_tensor(X[:, :, 0:H2], A[:, :, 0:H2], B[:, :, H2:HD], ALU.subtract))
                            last = eng.tensor_tensor(X[:, :, H2:HD], B[:, :, 0:H2], A[:, :, H2:HD], ALU.add)
                        last.then_inc(hready, 1)
                    elif what == "ret_scores":
                        eng.wait_ge(rs_ready, i + 1)
                        if i >= 2:
                            eng.wait_ge(rv_ready, i - 1)
                        eng.tensor_tensor(retm[:, i % 2, :], bank(3, 0, 384), dmask[:, i, :], ALU.mult).then_inc(rm_ready, 1)
                    elif what == "ret_norm":
                        Y = rety.rearrange("p t h c -> p (t h) c")
                        A = xs.rearrange("p t (h c) -> p (t h) c", c=RDV)
                        eng.wait_ge(rv_copied, HEADS)
                        settle(eng.tensor_reduce(stat[:, 4, :], Y, AX.X, ALU.add))
                        settle(eng.tensor_scalar(stat[:, 5, :], stat[:, 4, :], 1.0 / RDV, None, ALU.mult))
                        settle(eng.tensor_tensor(Y, Y, over(stat[:, 5, :], RDV), ALU.subtract))
                        settle(eng.tensor_tensor(A, Y, Y, ALU.mult))
                        settle(eng.tensor_reduce(stat[:, 4, :], A, AX.X, ALU.add))
                        eng.tensor_scalar(stat[:, 5, :], stat[:, 4, :], 1.0 / RDV, EPS, ALU.mult, ALU.add)\
                           .then_inc(rg_var, 1)
                        eng.wait_ge(rg_std, 1)
                        settle(eng.reciprocal(stat[:, 5, :], stat[:, 4, :]))
                        settle(eng.tensor_tensor(Y, Y, over(stat[:, 5, :], RDV), ALU.mult))
                        for t in range(TT):
                            tick(eng.tensor_tensor(rety[:, t], rety[:, t], ggain, ALU.mult))
                        eng.wait_ge(dve_step, steps[0])
                        eng.wait_ge(proj_copied, 18)
                        eng.tensor_tensor(Y, Y, raw1["rg"].rearrange("p t (h c) -> p (t h) c", c=RDV), ALU.mult)\
                           .then_inc(rg_ready, 1)
                    elif what == "sb_scores":
                        b = sbt[:, i % 2, :, :]
                        z = bank(0, 0, 384)
                        sc = HD ** -0.5
                        eng.wait_ge(z_ready, i + 1)
                        if i >= 2:
                            eng.wait_ge(w_ready, i - 1)
                        tick(eng.tensor_scalar(b[:, 0, :], z, -sc, 0.0, ALU.mult, ALU.min))
                        settle(eng.tensor_scalar(b[:, 1, :], z, sc, 0.0, ALU.mult, ALU.min))
                        eng.tensor_tensor(b[:, 2, :], b[:, 0, :], b[:, 1, :], ALU.add).then_inc(neg_ready, 1)
                        eng.wait_ge(ln_ready, i + 1)
                        eng.wait_ge(dve_step, steps[0])
                        tick(eng.tensor_tensor(b[:, 1, :], b[:, 1, :], b[:, 4, :], ALU.subtract))
                        settle(eng.tensor_tensor(b[:, 0, :], b[:, 0, :], b[:, 4, :], ALU.subtract))
                        eng.tensor_tensor(b[:, 0, :], b[:, 0, :], strict, ALU.mult).then_inc(stay_ready, 1)
                    elif what == "sb_later":
                        b = sbt[:, i % 2, :, :]
                        eng.wait_ge(later_ready, i + 1)
                        eng.tensor_tensor(b[:, 2, :], b[:, 1, :], bank(1, 0, 384), ALU.add).then_inc(arg_ready, 1)
                        if i >= 2:
                            eng.wait_ge(so_ready, i - 1)
                        eng.wait_ge(wexp_ready, i + 1)
                        eng.tensor_tensor(b[:, 5, :], b[:, 3, :], strict, ALU.mult).then_inc(w_ready, 1)
                eng.wait_ge(proj_copied, len(IN1_SLOTS))
                for u in range(8):
                    c = slice((u % 4) * SC, (u % 4 + 1) * SC)
                    y = bank(4 + u % 2).rearrange("p (t c) -> p t c", t=TT)
                    if u < 4:
                        eng.wait_ge(slot_used, FIRST["ret"] + HALVES * (u + 1))
                        eng.tensor_tensor(mixed[:, :, c], y, raw1["ga"][:, :, c], ALU.mult).then_inc(ya_used, 1)
                    else:
                        eng.wait_ge(slot_used, FIRST["sb"] + u - 4 + 1)
                        eng.tensor_tensor(tmpA[:, :, 0:SC], y, raw1["gb"][:, :, c], ALU.mult).then_inc(ya_used, 1)
                        eng.wait_ge(ya_used, u + 1)
                        last = eng.tensor_tensor(mixed[:, :, c], mixed[:, :, c], tmpA[:, :, 0:SC], ALU.add)
                        if u < 7:
                            settle(last)
                last.then_inc(mix_ready, 1)
                residual(0)

            def residual(k):
                for u in range(4):
                    c = slice(u * SC, (u + 1) * SC)
                    eng.wait_ge(slot_used, FIRST[f"out{k + 1}"] + HALVES * (u + 1))
                    eng.tensor_tensor(xres[:, :, c], xres[:, :, c], bank(4 + u % 2).rearrange("p (t c) -> p t c", t=TT),
                                      ALU.add).then_inc(o_used, 1)

            def attention2():
                base = len(IN1_SLOTS)
                eng.wait_ge(const2_in, 16)
                settle(eng.tensor_tensor(lbs[:, 0, :], lbl[:, 0, :], lbl[:, 1, :], ALU.max))
                tick(eng.tensor_tensor(lbs[:, 2, :], lbl[:, 0, :], lbs[:, 0, :], ALU.subtract))
                eng.tensor_tensor(lbs[:, 3, :], lbl[:, 1, :], lbs[:, 0, :], ALU.subtract).then_inc(g_lbm, 1)
                tick(eng.memset(qL, 0.0))
                tick(eng.memset(kL, 0.0))
                tick(eng.memset(Ssum, 0.0))
                eng.wait_ge(g_lbe, 1)
                settle(eng.tensor_tensor(lbs[:, 0, :], lbs[:, 4, :], lbs[:, 5, :], ALU.add))
                settle(eng.reciprocal(lbs[:, 1, :], lbs[:, 0, :]))
                settle(eng.tensor_tensor(lbs[:, 6, :], lbs[:, 4, :], lbs[:, 1, :], ALU.mult))
                settle(eng.tensor_scalar(lbs[:, 7, :], lbs[:, 6, :], -1.0, 1.0, ALU.mult, ALU.add))
                for what, i in schedule2():
                    if what == "m_scores":
                        l = ml[:, i % 2, :]
                        eng.wait_ge(m_ready, i + 1)
                        if i >= 2:
                            eng.wait_ge(m_T, i - 1)
                        settle(eng.scalar_tensor_tensor(l, bank(0, 0, 384), HD ** -0.5, c2a[:, i, :], ALU.mult, ALU.add))
                        eng.tensor_reduce(mstat(i, 0, 0), l[:, 0:P], AX.X, ALU.max, negate=True)
                        eng.tensor_reduce(mstat(i, 0, 1), l[:, P:P + S], AX.X, ALU.max, negate=True).then_inc(m_max, 1)
                    elif what == "m_turn":
                        l = ml[:, i % 2, :]
                        eng.wait_ge(m_exp, TT * (i + 1))
                        settle(eng.reciprocal(mstat2(i, 2), mstat2(i, 1)))
                        eng.tensor_scalar(l[:, 0:P], l[:, 0:P], mstat(i, 2, 0), None, ALU.mult)
                        eng.tensor_scalar(l[:, P:P + S], l[:, P:P + S], mstat(i, 2, 1), None, ALU.mult).then_inc(m_prob, 1)
                    elif what == "rec_prep":
                        f = colT["fr"]
                        eng.wait_ge(proj_copied, base + 8)
                        for h in range(REC_H):
                            tick(eng.tensor_scalar(f[:, h, :], f[:, h, :], lbs[:, 7, h:h + 1], lbs[:, 6, h:h + 1],
                                                   ALU.mult, ALU.add))
                        eng.wait_ge(dve_step, steps[0])
                        eng.tensor_scalar(kk.rearrange("p h t c -> p (h t c)"), f.rearrange("p h c -> p (h c)"), -1.0, 1.0,
                                          ALU.mult, ALU.add).then_inc(g_f, 1)
                        eng.wait_ge(g_log, 1)
                        for h in range(REC_H):
                            for t in range(TT):
                                tick(eng.tensor_tensor_scan(cum[:, h, t, :], ones2, dlt[:, h, t, :], 0.0, ALU.mult, ALU.add))
                        eng.wait_ge(dve_step, steps[0])
                    elif what == "rec_level":
                        q = colT["qr"].rearrange("p h (t c) -> p h t c", t=TT)
                        if i == 0:
                            eng.wait_ge(g_f, 1)
                            eng.nop().then_inc(g_qk, 1)
                        elif i < 8:
                            d, h = level(dlt, i)
                            c = level(cum, i)[0]
                            eng.wait_ge(g_qk, i)
                            eng.tensor_tensor(d, c, c[:, :, h - 1:h].to_broadcast([P, c.shape[1], 2 * h]), ALU.subtract)\
                               .then_inc(g_dlt, 1)
                            eng.wait_ge(g_exp, i)
                            eng.wait_ge(g_s, TT * i)
                            eng.tensor_tensor(level(qL, i)[0][:, :, h:], d[:, :, h:], level(q, i)[0][:, :, h:], ALU.mult)
                            eng.tensor_tensor(level(kL, i)[0][:, :, 0:h], d[:, :, 0:h], level(kk, i)[0][:, :, 0:h], ALU.mult)\
                               .then_inc(g_qk, 1)
                        else:
                            eng.wait_ge(g_qk, i)
                            eng.tensor_tensor(dlt[:, :, 0, :], cum[:, :, 0, :],
                                              cum[:, :, 0, P - 1:P].to_broadcast([P, REC_H, P]), ALU.subtract)\
                               .then_inc(g_dlt, 1)
                            eng.wait_ge(g_exp, i)
                            eng.wait_ge(g_s, TT * i)
                            eng.tensor_tensor(qL[:, :, 1, :], dlt[:, :, 1, :], q[:, :, 1, :], ALU.mult)
                            eng.tensor_tensor(kL[:, :, 0, :], dlt[:, :, 0, :], kk[:, :, 0, :], ALU.mult).then_inc(g_qk, 1)
                        if i < 8:
                            for t in range(TT):
                                eng.wait_ge(g_s, TT * i + t + 1)
                                m = lmask[:, i:i + 1, :].bitcast(U32).to_broadcast([P, REC_H, P])
                                eng.copy_predicated(Ssum[:, t, :, :], m, bank(6 + t).rearrange("p (h c) -> p h c", h=REC_H))\
                                   .then_inc(g_sc, 1)
                Y = ry.rearrange("p t h c -> p (t h) c")
                A = rt.rearrange("p t h c -> p (t h) c")
                eng.wait_ge(g_yc, TT)
                settle(eng.tensor_tensor(A, Y, Y, ALU.mult))
                settle(eng.tensor_reduce(stat[:, 5, 0:8], A, AX.X, ALU.add))
                eng.tensor_scalar(stat[:, 6, 0:8], stat[:, 5, 0:8], 1.0 / P, EPS, ALU.mult, ALU.add).then_inc(g_var, 1)
                eng.wait_ge(g_std, 1)
                settle(eng.reciprocal(stat[:, 5, 0:8], stat[:, 7, 0:8]))
                settle(eng.tensor_tensor(Y, Y, over(stat[:, 5, 0:8], P), ALU.mult))
                for t in range(TT):
                    tick(eng.tensor_tensor(ry[:, t], ry[:, t], rgain, ALU.mult))
                eng.wait_ge(dve_step, steps[0])
                eng.wait_ge(proj_copied, base + len(IN2_SLOTS))
                eng.tensor_tensor(Y, Y, raw2["gr"].rearrange("p t (h c) -> p (t h) c", c=P), ALU.mult).then_inc(g_out, 1)
                residual(1)

            def top16(ins, tmp, vals, ids):
                for s, v in zip(ins, vals):
                    tick(eng.max(v[:, 0:8], s))
                eng.wait_ge(dve_step, steps[0])
                for s, w, v, x in zip(ins, tmp, vals, ids):
                    tick(eng.max_index(x[:, 0:8], v[:, 0:8], s))
                    tick(eng.match_replace(w, v[:, 0:8], s, -3.0e38))
                eng.wait_ge(dve_step, steps[0])
                for w, v in zip(tmp, vals):
                    tick(eng.max(v[:, 8:16], w))
                eng.wait_ge(dve_step, steps[0])
                for w, v, x in zip(tmp, vals, ids):
                    tick(eng.max_index(x[:, 8:16], v[:, 8:16], w))
                eng.wait_ge(dve_step, steps[0])

            def experts(b):
                n = peer[b]
                first_v = FIRST[f"v{b + 1}"]
                for h in range(HEADS):
                    eng.wait_ge(n["s_copied"], h + 1)
                    for t in range(TT):
                        top16([scores[:, h % 4, t, c, :] for c in range(2)], [cand[:, 2, c * NKEY:(c + 1) * NKEY] for c in range(2)],
                              [val[:, c, :] for c in range(2)], [idx[:, t, h, c, :] for c in range(2)])
                        s = cand[:, 0, :]
                        last = eng.tensor_tensor(s.rearrange("p (a b) -> p a b", a=TOPK), over(val[:, 0, :], TOPK),
                                                 val[:, 1:2, :].to_broadcast([P, TOPK, TOPK]), ALU.add)
                        if t == TT - 1:
                            last.then_inc(n["scores_used"], 1)
                            eng.wait_ge(n["scores_used"], h + 1)
                        else:
                            settle(last)
                        top16([s], [cand[:, 1, :]], [top[:, t, h, :]], [pos[:, t, h, :]])
                hk = HEADS * TOPK
                big = work[:, 0:2048]
                eq = big.rearrange("p (m a) -> p m a", a=TOPK)
                eq4 = big.rearrange("p (h k a) -> p h k a", h=HEADS, k=TOPK)
                for t in range(TT):
                    tick(eng.tensor_scalar(posab[:, 0, :, :], pos[:, t, :, :], 4, None, ALU.logical_shift_right))
                    tick(eng.tensor_scalar(posab[:, 1, :, :], pos[:, t, :, :], TOPK - 1, None, ALU.bitwise_and))
                    tick(eng.tensor_copy(idxf[:, :, :, :], idx[:, t, :, :, :]))
                    eng.wait_ge(dve_step, steps[0])
                    settle(eng.tensor_copy(posf[:, :, :, :], posab[:, :, :, :]))
                    for c in range(2):
                        settle(eng.tensor_tensor(eq, iota16[:, :].unsqueeze(1).to_broadcast([P, hk, TOPK]),
                                                 over(posf[:, c, :, :].rearrange("p h k -> p (h k)"), TOPK), ALU.is_equal))
                        settle(eng.tensor_tensor(eq4, eq4, idxf[:, :, c, :].unsqueeze(2).to_broadcast([P, HEADS, TOPK, TOPK]),
                                                 ALU.mult))
                        settle(eng.tensor_reduce(esel[:, t, c, :, :].rearrange("p h k -> p (h k)"), eq, AX.X, ALU.add))
                    last = eng.tensor_tensor(esel[:, t, 2, :, :], top[:, t, :, :],
                                             top[:, t, :, 0:1].to_broadcast([P, HEADS, TOPK]), ALU.subtract)
                    if t == 0:
                        settle(last)
                last.then_inc(n["sums_ready"], 1)
                eng.wait_ge(n["exp_ready"], 1)
                g = esel[:, :, 2, :, :]
                for t in range(TT):
                    tick(eng.tensor_reduce(stat[:, 0, t * HEADS:(t + 1) * HEADS], g[:, t], AX.X, ALU.add))
                eng.wait_ge(dve_step, steps[0])
                settle(eng.reciprocal(stat[:, 1, 0:16], stat[:, 0, 0:16]))
                settle(eng.tensor_scalar(stat[:, 1, 0:16], stat[:, 1, 0:16], GATE_SCALE, None, ALU.mult))
                for t in range(TT):
                    last = eng.tensor_tensor(g[:, t], g[:, t], over(stat[:, 1, t * HEADS:(t + 1) * HEADS], TOPK), ALU.mult)
                    if t == 0:
                        tick(last)
                last.then_inc(n["sel_ready"], 1)
                eng.wait_ge(n["selT_ready"], 1)
                tick(eng.tensor_copy(rowT[:, 0:2, :], bank(4).rearrange("p (w t) -> p w t", w=2)))
                settle(eng.tensor_copy(rowT[:, 2, :], bank(5, 0, S)))
                eng.tensor_tensor(rowT[:, 3, :], bank(5, 0, S), rowT[:, 2, :], ALU.subtract).then_inc(n["rows_ready"], 1)
                eng.wait_ge(n["rows_ready"], 1)

                def hot(k, c, base, half, j):
                    def row(w, width):
                        return rowT[:, w, bass.ds(k * (4 * RING) + 4 * c, 4)].unsqueeze(2).to_broadcast([P, 4, width])
                    eng.tensor_tensor(eq1[:, j], iota[:, half * HALF:(half + 1) * HALF].unsqueeze(1).to_broadcast([P, 4, HALF]),
                                      row(0, HALF), ALU.is_equal).then_inc(n["eq_ready"], 1)
                    eng.tensor_tensor(hot2[:, j], iota[:, :].unsqueeze(1).to_broadcast([P, 4, NKEY]), row(1, NKEY), ALU.is_equal)
                    eng.wait_ge(n["eq_ready"], k * RING + (base + c + 1))
                    eng.tensor_tensor(hot1[:, j, 0], eq1[:, j], row(2, HALF), ALU.mult)
                    eng.tensor_tensor(hot1[:, j, 1], eq1[:, j], row(3, HALF), ALU.mult).then_inc(n["hot_ready"], 1)

                def apply(k, c, base, half, j):
                    eng.wait_ge(n["gates_ready"], k * RING + (base + c + 1))
                    a = act[:, bass.ds(k * (4 * RING) + 4 * c, 4), half * HALF:(half + 1) * HALF]
                    eng.tensor_tensor(a, bank(6 + j, 0, 4 * HALF).rearrange("p (q k) -> p q k", q=4), a, ALU.mult)\
                       .then_inc(n["gates_used"], 1)

                hot(0, 0, 0, 0, 0)
                hot(0, 1, 0, 0, 1)
                eng.wait_ge(n["gelu_done"], E_TILES // 4)
                with eng.Fori(0, HALF_ROUND - 1) as k:
                    for c in range(RING):
                        apply(k, c, 0, 0, c % 2)
                        hot(k, c + 2, 0, 0, c % 2)
                last_k = HALF_ROUND - 1
                for c in range(RING):
                    apply(last_k, c, 0, 0, c % 2)
                    if c < 2:
                        hot(last_k, c + 2, 0, 0, c % 2)
                    else:
                        hot(0, c - 2, GROUPS, 1, c % 2)
                eng.wait_ge(n["gates_used"], GROUPS)

                def pair(p, j, first=False):
                    if not first:
                        eng.wait_ge(slot_used, p * 2 + (first_v - 2))
                    src = act[:, :, bass.ds(p * 2, 2)].rearrange("p t e -> p e t")
                    eng.tensor_copy(shi[:, j, :, :], src).then_inc(n["shi_ready"], 1)
                    eng.wait_ge(n["shi_ready"], p + 1)
                    eng.tensor_tensor(slo[:, j, :, :], src, shi[:, j, :, :].bitcast(F32), ALU.subtract)\
                       .then_inc(n["pair_ready"], 1)

                def gated(k, cs, last=False):
                    for c in cs:
                        apply(k, c, GROUPS, 1, c % 2)
                        if not last or c < 2:
                            hot(k, c + 2, GROUPS, 1, c % 2)

                pair(0, 0, first=True)
                pair(1, 1, first=True)
                eng.wait_ge(n["gelu_done"], E_TILES // 2)
                gated(0, (0, 1))
                pair(2, 0)
                gated(0, (2, 3))
                with eng.Fori(1, HALF_ROUND - 1) as k:
                    pair(k * 2 + 1, 1)
                    gated(k, (0, 1))
                    pair(k * 2 + 2, 0)
                    gated(k, (2, 3))
                pair(2 * last_k + 1, 1)
                gated(last_k, (0, 1, 2, 3), last=True)
                eng.wait_ge(n["gates_used"], 2 * GROUPS)
                pair(2 * last_k + 2, 0)
                with eng.Fori(HALF_ROUND, ROUNDS - 1) as k:
                    pair(k * 2 + 1, 1)
                    pair(k * 2 + 2, 0)
                pair(2 * ROUNDS - 1, 1)
                eng.wait_ge(n["acc_ready"], 1)
                for a in range(4):
                    c = slice((a % 2) * 512, (a % 2 + 1) * 512)
                    eng.scalar_tensor_tensor(xres[:, a // 2, c], bank(a), 1.0 / GATE_SCALE, xres[:, a // 2, c], ALU.mult, ALU.add)\
                       .then_inc(n["done"], 1)

            eng.wait_ge(turn_in, N_TURN)
            eng.wait_ge(x_in, 16 * TT)
            norm(0)
            eng.wait_ge(const_in, N_CONST)
            attention1()
            norm(1)
            experts(0)
            norm(2)
            attention2()
            norm(3)
            experts(1)
            eng.wait_ge(fin_sq, TT)
            eng.tensor_scalar(stat[:, 1, 0:TT], stat[:, 0, 0:TT], 1.0 / D, EPS, ALU.mult, ALU.add).then_inc(fin_var, 1)
            eng.wait_ge(fin_std, 1)
            settle(eng.reciprocal(stat[:, 3, 0:TT], stat[:, 2, 0:TT]))
            eng.wait_ge(fgain_in, 16)
            for t in range(TT):
                settle(eng.tensor_scalar(xs[:, t, :], xres[:, t, :], stat[:, 3, t:t + 1], None, ALU.mult))
                eng.tensor_tensor(xs[:, t, :], xs[:, t, :], fgain, ALU.mult).then_inc(fin_ready, 1)


def shape_constants():
    f = np.float32
    half = HD // 2
    pos = np.arange(S, dtype=f)
    freqs = (f(10000.0) ** (-np.arange(half, dtype=f) / f(half))).astype(f)
    ang = pos[:, None] * freqs[None, :]
    cos, sin = np.cos(ang), np.sin(ang)
    cos, sin = np.concatenate([cos, cos], 1), np.concatenate([sin, sin], 1)
    sc = f(HD ** -0.5)
    rope = np.stack([cos, sin, cos * sc, sin * sc], 1).reshape(TT, P, 4 * HD).transpose(1, 0, 2).reshape(P, -1)
    j, i = np.arange(P)[:, None], np.arange(S)[None, :]
    i1 = np.arange(P, S)[None, :]
    lg = np.log1p(-np.exp2(-5.0 - np.arange(HEADS)))

    def decay(key, query):
        d = query - key
        return np.where(d >= 0, np.exp(lg[:, None, None] * np.maximum(d, 0)), 0.0)
    dm = np.concatenate([decay(j, i), decay(j + P, i1)], 2).transpose(1, 0, 2).reshape(P, -1)
    tri = (np.arange(P)[:, None] > np.arange(P)[None, :]).astype(f)
    strict = np.concatenate([j < i, j + P < i1], 1).astype(f)
    c1 = [rope, dm, tri, np.ones((P, P)), strict]
    t = np.arange(P)[:, None]
    s0, s1 = np.arange(P)[None, :], np.arange(S)[None, :]
    slopes = 2.0 ** (-8.0 * np.arange(1, HEADS + 1) / HEADS)

    def alibi(q, k):
        return np.where(k <= q, -slopes[:, None, None] * (q - k), -1.0e30)
    ab = np.concatenate([alibi(t, s0), alibi(t + P, s1)], 2).transpose(1, 0, 2).reshape(P, -1)
    k_, q_ = np.arange(P)[:, None], np.arange(P)[None, :]
    lm = [k_ == q_]
    for l in range(7):
        b = 1 << l
        lm.append((k_ // (2 * b) == q_ // (2 * b)) & (k_ % (2 * b) < b) & (q_ % (2 * b) >= b))
    lm = np.stack(lm, 1).astype(f).reshape(P, -1)
    c2 = [ab, lm, np.ones((P, P))]
    return [a.astype(f) for a in c1], [a.astype(f) for a in c2]


def rows_of(v):
    return np.broadcast_to(np.asarray(v).reshape(1, -1), (P, np.asarray(v).size))


def slot_rows(w):
    r, c = w.shape
    return w.reshape(r // P // KH, KH, P, c // SC, SC).transpose(3, 0, 2, 1, 4).reshape(-1, P, SLOT)


def slot_tiles(w):
    return w.reshape(-1, P, KC, P).transpose(0, 3, 2, 1).reshape(-1, P, SLOT)


def kernel(**inputs):
    import concourse.bacc as _bacc
    from concourse.bass_utils import run_bass_kernel_spmd as _run

    w = {k: np.asarray(v) for k, v in inputs.items()}
    in1, in2 = w["w_in"][0], w["w_in_2"][0]
    parts = [slot_rows(in1[:, a:a + n]) for _, a, n in IN1]
    parts += [slot_rows(w["w_branch_ret"][0]), slot_rows(w["w_branch_sb"][0]), slot_rows(w["w_out"][0]),
              slot_tiles(w["peer_w_q"][0].T), slot_tiles(w["peer_u"][0]), w["peer_v"][0].reshape(-1, P, D)]
    parts += [slot_rows(in2[:, a:a + n]) for _, a, n in IN2]
    parts += [slot_rows(w["w_out_2"][0]), slot_tiles(w["peer_wq_2"][0].T), slot_tiles(w["peer_u_2"][0]),
              w["peer_v_2"][0].reshape(-1, P, D)]
    c1, c2 = shape_constants()
    c1 += [rows_of(w[k][0]) for k in ("ret_q_norm", "ret_k_norm", "sb_q_norm", "sb_k_norm")]
    c1 += [rows_of(w["ret_group_norm"][0])]
    c2 += [w["rec_lb_logits_2"].reshape(2, REC_H, P).transpose(2, 0, 1).reshape(P, -1), rows_of(w["rec_norm_g_2"][0])]
    gcol = np.stack([w[k][0].reshape(KC, P) for k in ("norm_attn", "norm_ffn", "norm1_g_2", "norm2_g_2")])
    arrays = {
        "weights": np.concatenate(parts),
        "const1": np.concatenate(c1, 1),
        "const2": np.concatenate(c2, 1),
        "fgain": rows_of(w["normf_g_2"]),
        "gcol": gcol.transpose(2, 0, 1),
        "ident": np.eye(P, dtype=np.float32),
        "iota": np.broadcast_to(np.arange(NKEY, dtype=np.float16), (P, NKEY)),
        "iota16": np.broadcast_to(np.arange(TOPK, dtype=np.float32), (P, TOPK)),
        "keys1": np.stack([w["peer_sub_keys_1"][0].T, w["peer_sub_keys_2"][0].T], 1),
        "keys2": w["peer_subkeys_2"][0].reshape(HEADS * 2, NKEY, P).transpose(2, 0, 1),
        "x": w["x"],
    }
    arrays = {k: np.ascontiguousarray(v) for k, v in arrays.items()}
    nc = _bacc.Bacc("TRN2", target_bir_lowering=False, num_devices=1, dynamic_dma_scratch_size=256)
    ap = {k: nc.dram_tensor("in_" + k, v.shape, mybir.dt.from_np(v.dtype), kind="ExternalInput").ap() for k, v in arrays.items()}
    out = nc.dram_tensor("out", (1, S, D), F32, kind="ExternalOutput").ap()
    block_program(nc, ap["weights"], ap["const1"], ap["const2"], ap, (ap["keys1"], ap["keys2"]), ap["x"], out)
    r = _run(nc, [{"in_" + k: v for k, v in arrays.items()}], core_ids=[0])
    return r.results[0]["out"]
```

```python
from contextlib import ExitStack

import numpy as np
import concourse.bass as bass
from concourse import mybir

P = 128
F32 = mybir.dt.float32
F16 = mybir.dt.float16
F32R = mybir.dt.float32r
U32 = mybir.dt.uint32
ALU = mybir.AluOpType
ACT = mybir.ActivationFunctionType
AX = mybir.AxisListType

D = 1024
S = 256
TT = S // P
KC = D // P
EPS = 1e-6

HEADS = 8
HD = 64
RDV = 128
REC_H = 4
TOPK = 16
NKEY = 128

SLOT = 1024
SC = 256
KH = SLOT // SC
HALVES = KC // KH
RING = 4

IN1 = [("rq", 0, 512), ("rk", 512, 512), ("rv", 1024, 1024), ("sq", 3072, 512), ("sk", 3584, 512),
       ("sv", 4096, 512), ("rg", 2048, 1024), ("ga", 4608, 1024), ("gb", 5632, 1024)]
IN2 = [("fr", 2048, 512), ("qr", 1536, 512), ("qa", 0, 512), ("ka", 512, 512), ("va", 1024, 512),
       ("ir", 2560, 512), ("gr", 3072, 512)]


def slots_of(groups):
    return [(n, o) for n, _, w in groups for o in range(0, w, SC)]


IN1_SLOTS, IN2_SLOTS = slots_of(IN1), slots_of(IN2)
N_EXP = NKEY * NKEY
E_TILES = N_EXP // P
ROUNDS = E_TILES // RING
Q_TILES = 2 * HEADS
HALF = NKEY // 2
HALF_ROUND = ROUNDS // 2
U_MID = 12
GROUPS = S // 4
GATE_SCALE = 2.0 ** 14
assert GROUPS == E_TILES // 2

ORDER = [("in1", HALVES * len(IN1_SLOTS)), ("ret", HALVES * 4), ("sb", 4), ("out1", HALVES * 4), ("q1", Q_TILES),
         ("u1", E_TILES), ("v1", E_TILES), ("in2", HALVES * len(IN2_SLOTS)), ("out2", HALVES * 4), ("q2", Q_TILES),
         ("u2", E_TILES), ("v2", E_TILES)]
FIRST, N_SLOTS = {}, 0
for _name, _n in ORDER:
    FIRST[_name] = N_SLOTS
    N_SLOTS += _n
assert all(FIRST[_k] % RING == 0 for _k in ("q1", "u1", "v1", "in2", "q2", "u2", "v2")) and N_SLOTS % RING == 0

HEADNORM = (1, 3, 9, 11)
DVE_SPLITS = range(15, len(IN1_SLOTS))

def schedule1():
    steps = []
    for s in range(len(IN1_SLOTS)):
        steps.append(("proj", s))
        for i in range(4):
            if s == HEADNORM[i]:
                steps.append(("headnorm", i))
            if s == HEADNORM[i] + (4 if i < 2 else 3):
                steps.append(("headT", i))
        if 8 <= s < 8 + HEADS:
            steps.append(("ret_scores", s - 8))
        if 9 <= s < 9 + HEADS:
            steps.append(("ret_values", s - 9))
        if 15 <= s < 15 + HEADS:
            steps.append(("sb_scores", s - 15))
        if 16 <= s < 16 + HEADS:
            steps.append(("sb_later", s - 16))
        if 17 <= s < 17 + HEADS:
            steps.append(("sb_values", s - 17))
        if s in (18, 20, 22, 24):
            steps.append(("ret_norm", (s - 18) // 2))
    return steps


def schedule2():
    steps = []
    for s in range(8 + HEADS + 2):
        level, head = s - 4, s - 8
        if 0 <= level < 9:
            steps.append(("rec_decay", level))
        if 1 <= level < 9:
            steps.append(("rec_take", level - 1))
        if 0 <= level < 9:
            steps.append(("rec_factors", level))
        if 1 <= head <= HEADS:
            steps.append(("m_norm", head - 1))
        if s < len(IN2_SLOTS):
            steps.append(("proj", s))
        if s == 3:
            steps.append(("rec_prep", 0))
        if 0 <= level < 9:
            steps.append(("rec_level", level))
        if 0 <= head < HEADS:
            steps.append(("m_scores", head))
        if 1 <= head <= HEADS:
            steps.append(("m_turn", head - 1))
        if 2 <= head:
            steps.append(("m_values", head - 2))
        if level == 9:
            steps.append(("rec_values", 0))
        if level == 10:
            steps.append(("rec_squares", 0))
        if level == 11:
            steps.append(("rec_norm", 0))
    return steps


def block_program(nc, weights, const1, const2, gains, keys_in, x, out):
    with ExitStack() as ctx:
        def sb(name, shape, dt=F32):
            return ctx.enter_context(nc.sbuf_tensor(name, shape, dt))

        def over_at(name, base, at, shape, dt=F32):
            return nc.alloc_sbuf_tensor_at(name, shape, dt, offset=offset_of[base] + at)

        def sem(name):
            return ctx.enter_context(nc.semaphore(name))

        offset_of = {}

        def placed(name, shape, dt=F32):
            offset_of[name] = nc.sbuf_base
            return sb(name, shape, dt)

        ring = sb("ring", [P, RING, SLOT])
        whi = sb("whi", [P, RING, SLOT], F32R)
        wlo = sb("wlo", [P, RING, SLOT], F32R)
        act = placed("act", [P, S, NKEY])
        xres = sb("xres", [P, TT, D])
        hT = placed("hT", [P, KC, S])
        hhi = sb("hhi", [P, KC, S], F32R)
        hlo = over_at("hlo", "hT", 0, [P, KC, S], F32R)
        ident = sb("ident", [P, P])
        iota = sb("iota", [P, NKEY], F16)
        iota16 = sb("iota16", [P, TOPK])
        gcol = sb("gcol", [P, 4, KC])
        idx = sb("idx", [P, TT, HEADS, 2, TOPK], U32)
        top = sb("top", [P, TT, HEADS, TOPK])
        pos = sb("pos", [P, TT, HEADS, TOPK], U32)
        val = sb("val", [P, 2, TOPK])
        esel = sb("esel", [P, TT, 3, HEADS, TOPK])
        stat = sb("stat", [P, 8, 16])
        work = placed("work", [P, 3840])
        ps = ctx.enter_context(nc.psum_tensor("ps", [P, 8, 512], F32))

        scores = work[:, 0:2048].rearrange("p (b t c k) -> p b t c k", b=4, t=TT, c=2)
        qT = work[:, 2048:3072].rearrange("p (b c t) -> p b c t", b=2, c=2)
        cand = work[:, 3072:3840].rearrange("p (b k) -> p b k", b=3)
        small = work[:, 2048:2816]
        idxf = small[:, 0:256].rearrange("p (h c k) -> p h c k", h=HEADS, c=2)
        posab = small[:, 256:512].rearrange("p (c h k) -> p c h k", c=2, h=HEADS).bitcast(U32)
        posf = small[:, 512:768].rearrange("p (c h k) -> p c h k", c=2, h=HEADS)
        half16 = work[:, 2048:3840].bitcast(F16)
        rowT = half16[:, 0:4 * S].rearrange("p (w t) -> p w t", w=4)
        hot2 = half16[:, 1024:2048].rearrange("p (b q k) -> p b q k", b=2, q=4)
        hot1 = half16[:, 2048:3072].rearrange("p (b w q k) -> p b w q k", b=2, w=2, q=4)
        eq1 = half16[:, 3072:3584].rearrange("p (b q k) -> p b q k", b=2, q=4)
        shi = over_at("shi", "work", 0, [P, 2, 2, S], F32R)
        slo = over_at("slo", "work", 4096, [P, 2, 2, S], F32R)

        flat = act[:, :, :].rearrange("p a b -> p (a b)")

        def carve(at, *shape):
            n = int(np.prod(shape))
            names = "abcd"[:len(shape)]
            ap = flat[:, at:at + n]
            if len(shape) > 1:
                ap = ap.rearrange(f"p ({' '.join(names)}) -> p {' '.join(names)}",
                                  **{c: k for c, k in zip(names[1:], shape[1:])})
            return ap, at + n

        at = 0
        xs, at = carve(at, TT, D)
        raw1 = {}
        for n, _, w in IN1:
            raw1[n], at = carve(at, TT, w)
        tmpA, at = carve(at, TT, 512)
        tmpB_at = at
        tmpB, at = carve(at, TT, 512)
        headsT1 = {}
        headsT_at = at
        for n in ("rq", "rk", "sq", "sk"):
            headsT1[n], at = carve(at, HEADS // 2, S)
        c1, at = carve(at, const1.shape[1])
        retm, at = carve(at, 2, 384)
        rety, _ = carve(TT * D, TT, HEADS, RDV)
        sbt, at = carve(at, 2, 6, 384)
        keys1, at = carve(at, 2, NKEY)
        assert at <= S * NKEY, at
        start = TT * D
        sbT, _ = carve(start + 4 * TT * 512, HEADS // 2, S)
        mixed, _ = carve(start + 2 * TT * 512, TT, D)
        sbhi = over_at("sbhi", "act", 4 * tmpB_at, [P, HEADS // 2, S], F32R)
        sblo = over_at("sblo", "act", 4 * headsT_at, [P, HEADS // 2, S], F32R)

        cc = 0

        def col(n, *shape):
            nonlocal cc
            k = int(np.prod((n,) + shape))
            ap = c1[:, cc:cc + k]
            cc += k
            return ap
        rope = col(TT * 4 * HD).rearrange("p (t k c) -> p t k c", t=TT, k=4)
        dmask = col(HEADS * 384).rearrange("p (h c) -> p h c", h=HEADS)
        tri = col(P)
        ones = col(P)
        strict = col(384)
        hgain = col(4 * HD).rearrange("p (k c) -> p k c", k=4)
        ggain = col(HEADS * RDV).rearrange("p (h e) -> p h e", h=HEADS)
        assert cc == const1.shape[1]

        at = TT * D
        raw2 = {}
        for n in ("va", "ir", "gr"):
            raw2[n], at = carve(at, TT, 512)
        colT = {}
        for n in ("qa", "ka", "fr", "qr"):
            colT[n], at = carve(at, 4, S)
        c2, at = carve(at, const2.shape[1])
        ml, at = carve(at, 2, 384)
        mpT, at = carve(at, 2, 384)
        catT, at = carve(at, KC, S)
        cum, at = carve(at, REC_H, TT, P)
        kk, at = carve(at, REC_H, TT, P)
        dlt, at = carve(at, REC_H, TT, P)
        qL, at = carve(at, REC_H, TT, P)
        kL, at = carve(at, REC_H, TT, P)
        qL2, _ = carve(0, REC_H, TT, P)
        kL2, _ = carve(REC_H * S, REC_H, TT, P)
        Ssum, at = carve(at, TT, REC_H, P)
        Sx, at = carve(at, REC_H, P)
        ry, at = carve(at, TT, REC_H, P)
        rt, at = carve(at, TT, REC_H, P)
        lbs, at = carve(at, 8, REC_H)
        keys2, at = carve(at, HEADS * 2, NKEY)
        assert at <= S * NKEY, at
        c2a = c2[:, 0:HEADS * 384].rearrange("p (h c) -> p h c", h=HEADS)
        o = HEADS * 384
        lmask = c2[:, o:o + 8 * P].rearrange("p (l c) -> p l c", l=8)
        o += 8 * P
        ones2 = c2[:, o:o + P]
        o += P
        lbl = c2[:, o:o + 2 * REC_H].rearrange("p (k h) -> p k h", k=2)
        o += 2 * REC_H
        rgain = c2[:, o:o + 512].rearrange("p (h e) -> p h e", h=REC_H)
        o += 512
        assert o == const2.shape[1]
        fgain = flat[:, TT * D:TT * D + D]

        def mstat(h, k, t):
            return stat[:, 4, (h % 2) * 6 + 2 * k + t:(h % 2) * 6 + 2 * k + t + 1]

        def mstat2(h, k):
            return stat[:, 4, (h % 2) * 6 + 2 * k:(h % 2) * 6 + 2 * k + 2]

        def level(ap, l):
            h = 1 << (l - 1)
            if len(ap.shape) == 4:
                ap = ap.rearrange("p h t c -> p (h t c)")
            return ap.rearrange("p (n b) -> p n b", b=2 * h), h

        slot_in = [sem(f"slot_in{j}") for j in range(RING)]
        hi_ready = sem("hi_ready")
        lo_ready = sem("lo_ready")
        left_ready = sem("left_ready")
        sb_left = sem("sb_left_ready")
        slot_used = sem("slot_used")
        turn_in = sem("turn_in")
        const_in = sem("const_in")
        const2_in = sem("const2_in")
        keys2_in = sem("keys2_in")
        x_in = sem("x_in")
        out_done = sem("out_done")
        dve_step = sem("dve_step")
        act_step = sem("act_step")
        nsq = sem("norm_sums_ready")
        nvar = sem("norm_var_ready")
        nstd = sem("norm_std_ready")
        nxs = sem("norm_scaled_ready")
        nT = sem("norm_transposed")
        nout = sem("norm_out_ready")
        nfree = sem("norm_out_act")
        proj_copied = sem("proj_copied")
        hvar = sem("head_var_ready")
        hstd = sem("head_std_ready")
        hready = sem("head_ready")
        hTr = sem("head_transposed")
        hTc = sem("head_transposed_copied")
        rs_ready = sem("ret_scores_ready")
        rm_ready = sem("ret_masked_ready")
        rv_ready = sem("ret_values_ready")
        rv_copied = sem("ret_values_copied")
        rg_var = sem("ret_var_ready")
        rg_std = sem("ret_std_ready")
        rg_ready = sem("ret_gated_ready")
        z_ready = sem("sb_scores_ready")
        neg_ready = sem("sb_negabs_ready")
        ln_ready = sem("sb_log_ready")
        stay_ready = sem("sb_stay_ready")
        later_ready = sem("sb_later_ready")
        arg_ready = sem("sb_arg_ready")
        wexp_ready = sem("sb_exp_ready")
        w_ready = sem("sb_weights_ready")
        so_ready = sem("sb_out_ready")
        so_copied = sem("sb_out_copied")
        t_ready = sem("transposed")
        t_copied = sem("transposed_copied")
        ya_used = sem("branch_used")
        mix_ready = sem("mixed_ready")
        o_used = sem("out_proj_used")
        m_ready = sem("moba_scores_ready")
        m_max = sem("moba_max_ready")
        m_exp = sem("moba_exp_ready")
        m_prob = sem("moba_probs_ready")
        m_T = sem("moba_transposed")
        m_Tc = sem("moba_transposed_copied")
        m_out = sem("moba_out_ready")
        m_outc = sem("moba_out_copied")
        g_lbm = sem("rec_lb_max_ready")
        g_lbe = sem("rec_lb_exp_ready")
        g_f = sem("rec_forget_ready")
        g_log = sem("rec_log_ready")
        g_dlt = sem("rec_diff_ready")
        g_exp = sem("rec_exp_ready")
        g_qk = sem("rec_level_ready")
        g_s = sem("rec_scores_ready")
        g_sc = sem("rec_scores_used")
        g_sx = sem("rec_cross_copied")
        g_y = sem("rec_values_ready")
        g_yc = sem("rec_values_copied")
        g_var = sem("rec_var_ready")
        g_std = sem("rec_std_ready")
        g_out = sem("rec_gated_ready")
        peer = []
        for b in (1, 2):
            peer.append({n: sem(f"peer{b}_{n}") for n in (
                "q_copied", "s_ready", "s_copied", "scores_used",
                "gelu_done", "sums_ready", "exp_ready", "sel_ready", "selT_ready", "rows_ready", "eq_ready", "hot_ready",
                "gates_ready", "gates_used", "shi_ready", "pair_ready", "acc_ready", "done")})
        fin_sq = sem("final_sum_ready")
        fin_var = sem("final_var_ready")
        fin_std = sem("final_std_ready")
        fin_ready = sem("final_ready")
        fgain_in = sem("final_gain_in")

        block = ctx.enter_context(nc.Block())

        def bank(i, a=0, b=512):
            return ps[:, i, a:b]

        LEFT = {n: 4 * i for i, n in enumerate(("in1", "ret", "mix", "q1", "in2", "cat", "q2"))}

        @block.sync
        def _(sp):
            def load(k, j):
                sp.dma_start(ring[:, j, :], weights[k * RING + j]).then_inc(slot_in[j], 16)

            for t in range(TT):
                sp.dma_start(xres[:, t, :], x[0, t * P:(t + 1) * P, :]).then_inc(x_in, 16)
            for j in range(RING):
                load(0, j)
            sp.dma_start(c1, const1).then_inc(const_in, 16)
            sp.dma_start(keys1[:, :, :], keys_in[0]).then_inc(const_in, 16)
            sp.dma_start(iota[:, :], gains["iota"]).then_inc(const_in, 16)
            sp.dma_start(iota16[:, :], gains["iota16"]).then_inc(const_in, 16)
            with sp.Fori(1, N_SLOTS // RING) as k:
                for j in range(RING):
                    sp.wait_ge(lo_ready, k * RING + (j + 1 - RING))
                    load(k, j)

        @block.gpsimd
        def _(pool):
            with pool.Fori(0, N_SLOTS // RING) as k:
                for j in range(RING):
                    pool.wait_ge(hi_ready, k * RING + (j + 1))
                    pool.tensor_tensor(wlo[:, j, :], ring[:, j, :], whi[:, j, :].bitcast(F32), ALU.subtract)\
                        .then_inc(lo_ready, 1)

        N_TURN, N_CONST = 16 * 2, 16 * 4

        def tiles(ap):
            return ap.rearrange("p t (h c) -> p (t h) c", c=HD)

        @block.tensor
        def _(pe):
            def norm_transposes(k):
                pe.wait_ge(nxs, TT * (k + 1))
                for b in range(4):
                    for j in range(2):
                        for t in range(TT):
                            mm = pe.transpose(bank(b, j * S + t * P, j * S + (t + 1) * P),
                                              xs[:, t, (2 * b + j) * P:(2 * b + j + 1) * P], ident[:, :])
                    mm.then_inc(nT, 1)

            def turn16(src, k):
                for b in range(4):
                    for j in range(2):
                        for t in range(TT):
                            mm = pe.transpose(bank(b, j * S + t * P, j * S + (t + 1) * P), src(t, 2 * b + j),
                                              ident[:, :])
                    mm.then_inc(t_ready, 1)

            def split_product(dst, wide, narrow, start, stop):
                pe.matmul(dst, wide[0], narrow[0], start=start, stop=False, skip_group_check=True)
                pe.matmul(dst, wide[0], narrow[1], start=False, stop=False, skip_group_check=True)
                return pe.matmul(dst, wide[1], narrow[0], start=False, stop=stop, skip_group_check=True)

            def natural(lhs, i, u, wait, halves=HALVES, left=None):
                for half in range(halves):
                    j = (i + half) % RING
                    pe.wait_ge(lo_ready, i + half + 1)
                    if u >= 2 and half == 0:
                        pe.wait_ge(wait, u - 1)
                    for t in range(TT):
                        for c in range(KH):
                            kc = half * KH + c
                            if left is not None and t == 0 and c % 2 == 0:
                                pe.wait_ge(left_ready, left + kc // 2 + 1)
                            mm = split_product(bank(4 + u % 2, t * SC, (t + 1) * SC),
                                               [l[:, kc, t * P:(t + 1) * P] for l in lhs],
                                               [w[:, j, c * SC:(c + 1) * SC] for w in (whi, wlo)], kc + t == 0,
                                               half == halves - 1 and c == KH - 1)
                    mm.then_inc(slot_used, 1)

            def columns(i, u, wait, left=None):
                for half in range(HALVES):
                    j = (i + half) % RING
                    pe.wait_ge(lo_ready, i + half + 1)
                    if u >= 2 and half == 0:
                        pe.wait_ge(wait, u - 1)
                    for t in range(2):
                        for c in range(KH):
                            kc = half * KH + c
                            if left is not None and t == 0 and c % 2 == 0:
                                pe.wait_ge(left_ready, left + kc // 2 + 1)
                            mm = split_product(bank(4 + u % 2, t * S, (t + 1) * S),
                                               [w[:, j, c * SC + t * P:c * SC + (t + 1) * P] for w in (whi, wlo)],
                                               (hhi[:, kc, :], hlo[:, kc, :]), kc + t == 0, half == HALVES - 1 and c == KH - 1)
                    mm.then_inc(slot_used, 1)

            H = (hhi, hlo)

            def rows(h):
                return slice(HD * (h % 2), HD * (h % 2) + HD)

            def attention1():
                for what, i in schedule1():
                    if what == "proj":
                        natural(H, HALVES * i, i, proj_copied, left=LEFT["in1"] if i == 0 else None)
                    elif what == "headT":
                        name = ("rq", "rk", "sq", "sk")[i]
                        pe.wait_ge(hready, i + 1)
                        for r in range(2):
                            if i:
                                pe.wait_ge(hTc, 2 * i + r - 1)
                            for j in range(2):
                                for t in range(TT):
                                    c = (2 * r + j) * P
                                    mm = pe.transpose(bank((7, 1)[r], j * S + t * P, j * S + (t + 1) * P),
                                                      raw1[name][:, t, c:c + P], ident[:, :])
                            mm.then_inc(hTr, 1)
                    elif what == "ret_scores":
                        if i == 0:
                            pe.wait_ge(hTc, 4)
                        else:
                            pe.wait_ge(rm_ready, i)
                        q, kT = headsT1["rq"][rows(i), i // 2, :], headsT1["rk"][rows(i), i // 2, :]
                        pe.matmul(bank(3, 0, S), kT[:, 0:P], q, start=True, stop=True)
                        pe.matmul(bank(3, S, S + P), kT[:, P:S], q[:, P:S], start=True, stop=True).then_inc(rs_ready, 1)
                    elif what == "ret_values":
                        pe.wait_ge(rm_ready, i + 1)
                        if i == 0:
                            pe.wait_ge(proj_copied, 8)
                        else:
                            pe.wait_ge(rv_copied, i)
                        m, v = retm[:, i % 2, :], raw1["rv"][:, :, i * RDV:(i + 1) * RDV]
                        pe.matmul(bank(6, 0, P), m[:, 0:P], v[:, 0, :], start=True, stop=True)
                        pe.matmul(bank(6, P, 2 * P), m[:, P:S], v[:, 0, :], start=True, stop=False)
                        pe.matmul(bank(6, P, 2 * P), m[:, S:S + P], v[:, 1, :], start=False, stop=True)\
                          .then_inc(rv_ready, 1)
                    elif what == "sb_scores":
                        if i == 0:
                            pe.wait_ge(hTc, 8)
                        else:
                            pe.wait_ge(neg_ready, i)
                        q, kT = headsT1["sq"][rows(i), i // 2, :], headsT1["sk"][rows(i), i // 2, :]
                        pe.matmul(bank(0, 0, S), kT[:, 0:P], q, start=True, stop=True)
                        pe.matmul(bank(0, S, S + P), kT[:, P:S], q[:, P:S], start=True, stop=True).then_inc(z_ready, 1)
                    elif what == "sb_later":
                        pe.wait_ge(stay_ready, i + 1)
                        if i:
                            pe.wait_ge(arg_ready, i)
                        ls = sbt[:, i % 2, 0, :]
                        pe.matmul(bank(1, 0, S), tri, ls[:, 0:S], start=True, stop=False, skip_group_check=True)
                        pe.matmul(bank(1, P, S), ones, ls[:, S:S + P], start=False, stop=True, skip_group_check=True)
                        pe.matmul(bank(1, S, S + P), tri, ls[:, S:S + P], start=True, stop=True,
                                  skip_group_check=True).then_inc(later_ready, 1)
                    elif what == "sb_values":
                        pe.wait_ge(w_ready, i + 1)
                        if i == 0:
                            pe.wait_ge(proj_copied, 14)
                        if i >= 2:
                            pe.wait_ge(so_copied, i - 1)
                        w, v = sbt[:, i % 2, 5, :], raw1["sv"][:, :, i * HD:(i + 1) * HD]
                        pe.matmul(ps[rows(i), 2, 0:S], v[:, 0, :], w[:, 0:S], start=True, stop=False,
                                  skip_group_check=True)
                        pe.matmul(ps[rows(i), 2, P:S], v[:, 1, :], w[:, S:S + P], start=False, stop=True,
                                  skip_group_check=True).then_inc(so_ready, 1)
                pe.wait_ge(rg_ready, 1)
                pe.wait_ge(so_copied, HEADS)
                turn16(lambda t, c: rety[:, t, c, :], 0)
                pe.wait_ge(proj_copied, len(IN1_SLOTS))
                for u in range(4):
                    natural(H, FIRST["ret"] + HALVES * u, u, ya_used, left=LEFT["ret"] if u == 0 else None)
                pe.wait_ge(sb_left, 1)
                for u in range(4):
                    natural((sbhi, sblo), FIRST["sb"] + u, 4 + u, ya_used, 1)
                pe.wait_ge(mix_ready, 1)
                turn16(lambda t, c: mixed[:, t, c * P:(c + 1) * P], 1)
                for u in range(4):
                    natural(H, FIRST["out1"] + HALVES * u, u, o_used, left=LEFT["mix"] if u == 0 else None)

            def attention2():
                base = len(IN1_SLOTS)
                pe.wait_ge(const2_in, 16)
                for what, i in schedule2():
                    if what == "proj":
                        if IN2_SLOTS[i][0] in colT:
                            columns(FIRST["in2"] + HALVES * i, base + i, proj_copied, LEFT["in2"] if i == 0 else None)
                        else:
                            natural(H, FIRST["in2"] + HALVES * i, base + i, proj_copied)
                    elif what == "m_scores":
                        if i == 0:
                            pe.wait_ge(proj_copied, base + 8)
                        else:
                            pe.wait_ge(m_max, i)
                        q, kT = colT["qa"][rows(i), i // 2, :], colT["ka"][rows(i), i // 2, :]
                        pe.matmul(bank(0, 0, P), q[:, 0:P], kT[:, 0:P], start=True, stop=True)
                        pe.matmul(bank(0, P, P + S), q[:, P:S], kT, start=True, stop=True).then_inc(m_ready, 1)
                    elif what == "m_turn":
                        pe.wait_ge(m_prob, i + 1)
                        if i:
                            pe.wait_ge(m_Tc, i)
                        p = ml[:, i % 2, :]
                        for c in range(3):
                            mm = pe.transpose(bank(1, c * P, (c + 1) * P), p[:, c * P:(c + 1) * P], ident[:, :])
                        mm.then_inc(m_T, 1)
                    elif what == "m_values":
                        pe.wait_ge(m_Tc, i + 1)
                        if i == 0:
                            pe.wait_ge(proj_copied, base + 10)
                        if i >= 2:
                            pe.wait_ge(m_outc, i - 1)
                        w, v = mpT[:, i % 2, :], raw2["va"][:, :, i * HD:(i + 1) * HD]
                        pe.matmul(ps[rows(i), 2, 0:S], v[:, 0, :], w[:, 0:S], start=True, stop=False,
                                  skip_group_check=True)
                        pe.matmul(ps[rows(i), 2, P:S], v[:, 1, :], w[:, S:S + P], start=False, stop=True,
                                  skip_group_check=True).then_inc(m_out, 1)
                    elif what == "rec_level":
                        pe.wait_ge(g_qk, i + 1)
                        kl, ql = ((kk, colT["qr"].rearrange("p h (t c) -> p h t c", t=TT)) if i == 0 else (kL2, qL2) if i % 2
                                  else (kL, qL))
                        if i < 8:
                            for t in range(TT):
                                if i:
                                    pe.wait_ge(g_sc, TT * (i - 1) + t + 1)
                                for h in range(REC_H):
                                    mm = pe.matmul(bank(6 + t, h * P, (h + 1) * P), kl[:, h, t, :], ql[:, h, t, :],
                                                   start=True, stop=True)
                                mm.then_inc(g_s, 1)
                        else:
                            pe.wait_ge(g_sc, TT * 8 - 1)
                            for h in range(REC_H):
                                mm = pe.matmul(bank(6, h * P, (h + 1) * P), kl[:, h, 0, :], ql[:, h, 1, :],
                                               start=True, stop=True)
                            mm.then_inc(g_s, 1)
                    elif what == "rec_values":
                        pe.wait_ge(g_sx, 1)
                        pe.wait_ge(g_sc, TT * 8)
                        pe.wait_ge(proj_copied, base + 12)
                        ir = raw2["ir"]
                        for t in range(TT):
                            for h in range(REC_H):
                                mm = pe.matmul(bank(6 + t, h * P, (h + 1) * P), Ssum[:, t, h, :], ir[:, t, h * P:(h + 1) * P],
                                               start=True, stop=(t == 0))
                                if t:
                                    mm = pe.matmul(bank(6 + t, h * P, (h + 1) * P), Sx[:, h, :], ir[:, 0, h * P:(h + 1) * P],
                                                   start=False, stop=True)
                            mm.then_inc(g_y, 1)
                pe.wait_ge(g_out, 1)
                for b in range(2):
                    for j in range(2):
                        for t in range(TT):
                            mm = pe.transpose(bank(6 + b, j * S + t * P, j * S + (t + 1) * P), ry[:, t, 2 * b + j, :],
                                              ident[:, :])
                    mm.then_inc(t_ready, 1)
                for u in range(4):
                    natural(H, FIRST["out2"] + HALVES * u, 4 + u, o_used, left=LEFT["cat"] if u == 0 else None)

            def experts(b, keys):
                n = peer[b]
                first_q, first_u, first_v = FIRST[f"q{b + 1}"], FIRST[f"u{b + 1}"], FIRST[f"v{b + 1}"]

                def tile(j, dst, left=None):
                    for kc in range(KC):
                        if left is not None and kc % 2 == 0:
                            pe.wait_ge(left_ready, left + kc // 2 + 1)
                        c = slice(kc * P, (kc + 1) * P)
                        mm = split_product(dst, (whi[:, j, c], wlo[:, j, c]), (hhi[:, kc, :], hlo[:, kc, :]),
                                           kc == 0, kc == KC - 1)
                    mm.then_inc(slot_used, 1)

                for h in range(HEADS + 1):
                    if h < HEADS:
                        for c in range(2):
                            pe.wait_ge(lo_ready, first_q + 2 * h + c + 1)
                            if h >= 2 and c == 0:
                                pe.wait_ge(n["q_copied"], h - 1)
                            tile((2 * h + c) % RING, bank(4 + h % 2, c * S, (c + 1) * S),
                                 LEFT[f"q{b + 1}"] if h + c == 0 else None)
                    if h:
                        g = h - 1
                        pe.wait_ge(n["q_copied"], g + 1)
                        if g >= 2:
                            pe.wait_ge(n["s_copied"], g - 1)
                        for t in range(TT):
                            for c in range(2):
                                kT = keys[:, c if b == 0 else 2 * g + c, :]
                                mm = pe.matmul(bank(6 + g % 2, (2 * t + c) * P, (2 * t + c + 1) * P),
                                               qT[:, g % 2, c, t * P:(t + 1) * P], kT, start=True, stop=True)
                        mm.then_inc(n["s_ready"], 1)

                def gates(k, base, j):
                    pe.wait_ge(n["hot_ready"], k * RING + (base + j + 1))
                    if not (isinstance(k, int) and k * RING + base + j < 2):
                        pe.wait_ge(n["gates_used"], k * RING + (base + j - 1))
                    for q in range(4):
                        for w in range(2):
                            mm = pe.matmul(bank(6 + j % 2, q * HALF, (q + 1) * HALF), hot2[:, j % 2, q, :],
                                           hot1[:, j % 2, w, q, :], start=(q + w == 0), stop=(w == 1), skip_group_check=True)
                    mm.then_inc(n["gates_ready"], 1)

                def u_round(k, first=False, gated=False):
                    for j in range(RING):
                        pe.wait_ge(lo_ready, k * RING + (first_u + j + 1))
                        if j % 2 == 0 and not first:
                            pe.wait_ge(n["gelu_done"], k * 2 + (j // 2 - 1))
                        tile(j, bank(j // 2, (j % 2) * S, (j % 2 + 1) * S))
                        if gated:
                            gates(k, -HALF_ROUND * RING, j)

                u_round(0, first=True)
                with pe.Fori(1, U_MID) as k:
                    u_round(k)
                pe.wait_ge(n["sel_ready"], 1)
                pe.wait_ge(n["s_copied"], HEADS)
                for w in range(3):
                    for t in range(TT):
                        mm = pe.transpose(bank(4 + w // 2, (w % 2) * S + t * P, (w % 2) * S + (t + 1) * P),
                                          esel[:, t, w, :, :].rearrange("p h k -> p (h k)"), ident[:, :])
                mm.then_inc(n["selT_ready"], 1)
                with pe.Fori(U_MID, HALF_ROUND) as k:
                    u_round(k)
                u_round(HALF_ROUND, gated=True)
                with pe.Fori(HALF_ROUND + 1, ROUNDS) as k:
                    u_round(k, gated=True)

                pe.wait_ge(n["gelu_done"], E_TILES // 2)

                def v_round(k, first=False, last=False, gated=False):
                    for j in range(RING):
                        pe.wait_ge(lo_ready, k * RING + (first_v + j + 1))
                        if j % 2 == 0:
                            pe.wait_ge(n["pair_ready"], k * 2 + (j // 2 + 1))
                        for t in range(TT):
                            for half in range(2):
                                c, a = slice(half * 512, (half + 1) * 512), slice(t * P, (t + 1) * P)
                                mm = split_product(bank(2 * t + half),
                                                   (shi[:, j // 2, j % 2, a], slo[:, j // 2, j % 2, a]),
                                                   (whi[:, j, c], wlo[:, j, c]), first and j == 0, last and j == RING - 1)
                        mm.then_inc(slot_used, 1)
                        if gated:
                            gates(k, GROUPS, j)

                v_round(0, first=True, gated=True)
                with pe.Fori(1, HALF_ROUND) as k:
                    v_round(k, gated=True)
                with pe.Fori(HALF_ROUND, ROUNDS - 1) as k:
                    v_round(k)
                v_round(ROUNDS - 1, last=True)
                pe.wait_ge(slot_used, first_v + E_TILES)
                pe.nop().then_inc(n["acc_ready"], 1)

            pe.wait_ge(turn_in, N_TURN)
            norm_transposes(0)
            pe.wait_ge(const_in, N_CONST)
            attention1()
            norm_transposes(1)
            experts(0, keys1)
            norm_transposes(2)
            attention2()
            norm_transposes(3)
            pe.wait_ge(keys2_in, 16)
            experts(1, keys2)

        @block.scalar
        def _(eng):
            steps = [0]

            def settle(ins):
                steps[0] += 1
                ins.then_inc(act_step, 1)
                eng.wait_ge(act_step, steps[0])

            def norm(k, sem_in, count):
                eng.wait_ge(sem_in, count)
                for t in range(TT):
                    eng.activation(xs[:, t, :], xres[:, t, :], ACT.Square, accum_out=stat[:, 0, t:t + 1])\
                       .then_inc(nsq, 1)
                if k == 0:
                    highs_to(1)
                eng.wait_ge(nvar, k + 1)
                eng.activation(stat[:, 2, 0:TT], stat[:, 1, 0:TT], ACT.Sqrt).then_inc(nstd, 1)
                if k == 0:
                    highs_to(RING)
                for b in (1, 3):
                    eng.wait_ge(nT, 4 * k + b + 1)
                    for j in range(2):
                        c = 2 * b + j
                        eng.activation(hhi[:, c, :], bank(b, j * S, (j + 1) * S), ACT.Copy, scale=gcol[:, k, c:c + 1])
                        eng.activation(hT[:, c, :], bank(b, j * S, (j + 1) * S), ACT.Copy, scale=gcol[:, k, c:c + 1])\
                           .then_inc(nfree, 1)

            split = [0]

            def highs_to(end):
                for m in range(split[0], end):
                    eng.wait_ge(slot_in[m % RING], 16 * (m // RING + 1))
                    if m >= RING:
                        eng.wait_ge(slot_used, m - RING + 1)
                    eng.activation(whi[:, m % RING, :], ring[:, m % RING, :], ACT.Copy).then_inc(hi_ready, 1)
                split[0] = end

            def turned(k):
                for b in range(4):
                    eng.wait_ge(t_ready, 4 * k + b + 1)
                    eng.activation(hT[:, 2 * b:2 * b + 2, :], bank(b).rearrange("p (j c) -> p j c", j=2), ACT.Copy)\
                       .then_inc(t_copied, 1)

            def rows(h):
                return slice(HD * (h % 2), HD * (h % 2) + HD)

            FUNC = {"rg": ACT.Silu, "ga": ACT.Sigmoid, "gb": ACT.Sigmoid, "qr": ACT.Silu, "gr": ACT.Silu,
                    "fr": ACT.Sigmoid}

            def attention1():
                for what, i in schedule1():
                    if what == "proj":
                        name, off = IN1_SLOTS[i]
                        eng.wait_ge(slot_used, HALVES * (i + 1))
                        eng.activation(raw1[name][:, :, off:off + SC], bank(4 + i % 2).rearrange("p (t c) -> p t c", t=TT),
                                       FUNC.get(name, ACT.Copy)).then_inc(proj_copied, 1)
                        if i not in DVE_SPLITS:
                            highs_to(HALVES * (i + 1) + RING)
                    elif what == "headnorm":
                        eng.wait_ge(hvar, i + 1)
                        eng.activation(stat[:, 7, :], stat[:, 6, :], ACT.Sqrt).then_inc(hstd, 1)
                    elif what == "headT":
                        name = ("rq", "rk", "sq", "sk")[i]
                        for r in range(2):
                            eng.wait_ge(hTr, 2 * i + r + 1)
                            eng.activation(headsT1[name][:, 2 * r:2 * r + 2, :],
                                           bank((7, 1)[r]).rearrange("p (j c) -> p j c", j=2), ACT.Copy).then_inc(hTc, 1)
                    elif what == "ret_values":
                        eng.wait_ge(rv_ready, i + 1)
                        eng.activation(rety[:, :, i, :], bank(6, 0, S).rearrange("p (t c) -> p t c", t=TT), ACT.Copy)\
                           .then_inc(rv_copied, 1)
                    elif what == "ret_norm" and i == 2:
                        eng.wait_ge(rg_var, 1)
                        eng.activation(stat[:, 4, :], stat[:, 5, :], ACT.Sqrt).then_inc(rg_std, 1)
                    elif what == "sb_scores":
                        eng.wait_ge(neg_ready, i + 1)
                        b = sbt[:, i % 2, :, :]
                        settle(eng.activation(b[:, 3, :], b[:, 2, :], ACT.Exp))
                        eng.activation(b[:, 4, :], b[:, 3, :], ACT.Ln, bias=1.0).then_inc(ln_ready, 1)
                    elif what == "sb_later":
                        eng.wait_ge(arg_ready, i + 1)
                        b = sbt[:, i % 2, :, :]
                        eng.activation(b[:, 3, :], b[:, 2, :], ACT.Exp).then_inc(wexp_ready, 1)
                    elif what == "sb_values":
                        eng.wait_ge(so_ready, i + 1)
                        eng.activation(sbT[rows(i), i // 2, :], ps[rows(i), 2, 0:S], ACT.Copy).then_inc(so_copied, 1)
                turned(0)
                split[0] = FIRST["ret"] + RING
                eng.wait_ge(hi_ready, split[0])
                highs_to(FIRST["out1"] + RING)
                turned(1)
                highs_to(FIRST["q1"] + RING)

            def attention2():
                base = len(IN1_SLOTS)
                eng.wait_ge(g_lbm, 1)
                eng.activation(lbs[:, 4:6, :], lbs[:, 2:4, :], ACT.Exp).then_inc(g_lbe, 1)
                for what, i in schedule2():
                    if what == "proj":
                        name, off = IN2_SLOTS[i]
                        u = base + i
                        eng.wait_ge(slot_used, FIRST["in2"] + HALVES * (i + 1))
                        dst = (colT[name][:, off // P:off // P + 2, :] if name in colT else raw2[name][:, :, off:off + SC])
                        eng.activation(dst, bank(4 + u % 2).rearrange("p (t c) -> p t c", t=2), FUNC.get(name, ACT.Copy))\
                           .then_inc(proj_copied, 1)
                        highs_to(FIRST["in2"] + HALVES * (i + 1) + RING)
                    elif what == "m_scores":
                        eng.wait_ge(m_max, i + 1)
                        for t in range(TT):
                            c = slice(0, P) if t == 0 else slice(P, P + S)
                            eng.activation(ml[:, i % 2, c], ml[:, i % 2, c], ACT.Exp, bias=mstat(i, 0, t),
                                           accum_out=mstat(i, 1, t)).then_inc(m_exp, 1)
                    elif what == "m_turn":
                        eng.wait_ge(m_T, i + 1)
                        if i >= 2:
                            eng.wait_ge(m_out, i - 1)
                        eng.activation(mpT[:, i % 2, :], bank(1, 0, 384), ACT.Copy).then_inc(m_Tc, 1)
                    elif what == "m_values":
                        eng.wait_ge(m_out, i + 1)
                        eng.activation(catT[rows(i), i // 2, :], ps[rows(i), 2, 0:S], ACT.Copy).then_inc(m_outc, 1)
                    elif what == "rec_prep":
                        eng.wait_ge(g_f, 1)
                        eng.activation(dlt.rearrange("p h t c -> p (h t c)"), colT["fr"].rearrange("p h c -> p (h c)"),
                                       ACT.Ln).then_inc(g_log, 1)
                    elif what == "rec_decay" and i:
                        eng.wait_ge(g_dlt, i)
                        if i < 8:
                            v, h = level(dlt, i)
                            eng.activation(v[:, :, h:], v[:, :, h:], ACT.Exp)
                            eng.activation(v[:, :, 0:h], v[:, :, 0:h], ACT.Exp, scale=-1.0).then_inc(g_exp, 1)
                        else:
                            eng.activation(dlt[:, :, 0, :], dlt[:, :, 0, :], ACT.Exp, scale=-1.0)
                            eng.activation(dlt[:, :, 1, :], cum[:, :, 1, :], ACT.Exp).then_inc(g_exp, 1)
                    elif what == "rec_level" and i == 8:
                        eng.wait_ge(g_s, TT * 8 + 1)
                        eng.activation(Sx.rearrange("p h c -> p (h c)"), bank(6), ACT.Copy).then_inc(g_sx, 1)
                    elif what == "rec_values":
                        for t in range(TT):
                            eng.wait_ge(g_y, t + 1)
                            eng.activation(ry[:, t, :, :].rearrange("p h c -> p (h c)"), bank(6 + t), ACT.Copy)\
                               .then_inc(g_yc, 1)
                    elif what == "rec_norm":
                        eng.wait_ge(g_var, 1)
                        eng.activation(stat[:, 7, 0:8], stat[:, 6, 0:8], ACT.Sqrt).then_inc(g_std, 1)
                for b in range(2):
                    eng.wait_ge(t_ready, 8 + b + 1)
                    eng.activation(catT[:, 4 + 2 * b:6 + 2 * b, :], bank(6 + b).rearrange("p (j c) -> p j c", j=2),
                                   ACT.Copy).then_inc(t_copied, 1)
                highs_to(FIRST["q2"] + RING)

            def experts(b):
                n = peer[b]
                first_q, first_u, first_v = FIRST[f"q{b + 1}"], FIRST[f"u{b + 1}"], FIRST[f"v{b + 1}"]

                def high(m, j, k=0):
                    eng.wait_ge(slot_in[j], k * 16 + 16 * (m // RING + 1))
                    eng.wait_ge(slot_used, k * RING + (m - RING + 1))
                    eng.activation(whi[:, j, :], ring[:, j, :], ACT.Copy).then_inc(hi_ready, 1)

                for h in range(HEADS + 1):
                    if h < HEADS:
                        eng.wait_ge(slot_used, first_q + 2 * h + 2)
                        if h >= 2:
                            eng.wait_ge(n["s_ready"], h - 1)
                        eng.activation(qT[:, h % 2, :, :], bank(4 + h % 2).rearrange("p (c t) -> p c t", c=2), ACT.Copy)\
                           .then_inc(n["q_copied"], 1)
                        for c in range(2):
                            high(first_q + 2 * h + c + RING, (2 * h + c) % RING)
                    if h:
                        eng.wait_ge(n["s_ready"], h)
                        if h > 4:
                            eng.wait_ge(n["scores_used"], h - 4)
                        eng.activation(scores[:, (h - 1) % 4, :, :, :],
                                       bank(6 + (h - 1) % 2).rearrange("p (t c k) -> p t c k", t=TT, c=2), ACT.Copy)\
                           .then_inc(n["s_copied"], 1)

                def u_round(k):
                    for j in range(0, RING, 2):
                        high(first_u + j + RING, j, k)
                        high(first_u + j + 1 + RING, j + 1, k)
                        dst = act[:, :, bass.ds(k * RING + j, 2)].rearrange("p t e -> p e t")
                        eng.activation(dst, bank(j // 2).rearrange("p (e t) -> p e t", e=2),
                                       ACT.Gelu_apprx_tanh if b == 0 else ACT.Gelu).then_inc(n["gelu_done"], 1)

                with eng.Fori(0, U_MID) as k:
                    u_round(k)
                eng.wait_ge(n["sums_ready"], 1)
                eng.activation(esel[:, :, 2, :, :].rearrange("p t h k -> p t (h k)"),
                               esel[:, :, 2, :, :].rearrange("p t h k -> p t (h k)"), ACT.Exp).then_inc(n["exp_ready"], 1)
                with eng.Fori(U_MID, ROUNDS) as k:
                    u_round(k)

                with eng.Fori(0, ROUNDS - 1) as k:
                    for j in range(RING):
                        high(first_v + j + RING, j, k)
                split[0] = first_v + E_TILES

            eng.dma_start(ident[:, :], gains["ident"]).then_inc(turn_in, 16)
            eng.dma_start(gcol[:, :, :], gains["gcol"]).then_inc(turn_in, 16)
            eng.wait_ge(turn_in, N_TURN)
            norm(0, x_in, 16 * TT)
            attention1()
            norm(1, o_used, 4)
            eng.wait_ge(const_in, N_CONST)
            experts(0)
            highs_to(FIRST["in2"] + RING)
            eng.wait_ge(peer[0]["done"], 4)
            eng.dma_start(c2, const2).then_inc(const2_in, 16)
            eng.dma_start(keys2, keys_in[1]).then_inc(keys2_in, 16)
            norm(2, peer[0]["done"], 4)
            attention2()
            norm(3, o_used, 8)
            experts(1)
            eng.wait_ge(peer[1]["done"], 4)
            eng.dma_start(fgain, gains["fgain"]).then_inc(fgain_in, 16)
            for t in range(TT):
                eng.activation(xs[:, t, :], xres[:, t, :], ACT.Square, accum_out=stat[:, 0, t:t + 1]).then_inc(fin_sq, 1)
            eng.wait_ge(fin_var, 1)
            eng.activation(stat[:, 2, 0:TT], stat[:, 1, 0:TT], ACT.Sqrt).then_inc(fin_std, 1)
            for t in range(TT):
                eng.wait_ge(fin_ready, t + 1)
                eng.dma_start(out[0, t * P:(t + 1) * P, :], xs[:, t, :]).then_inc(out_done, 16)
            eng.wait_ge(out_done, 16 * TT)

        @block.vector
        def _(eng):
            steps = [0]

            def tick(ins):
                steps[0] += 1
                ins.then_inc(dve_step, 1)

            def settle(ins):
                tick(ins)
                eng.wait_ge(dve_step, steps[0])

            def norm(k):
                eng.wait_ge(nsq, TT * (k + 1))
                eng.tensor_scalar(stat[:, 1, 0:TT], stat[:, 0, 0:TT], 1.0 / D, EPS, ALU.mult, ALU.add).then_inc(nvar, 1)
                eng.wait_ge(nstd, k + 1)
                settle(eng.reciprocal(stat[:, 3, 0:TT], stat[:, 2, 0:TT]))
                for t in range(TT):
                    eng.tensor_scalar(xs[:, t, :], xres[:, t, :], stat[:, 3, t:t + 1], None, ALU.mult).then_inc(nxs, 1)
                for b in (0, 2):
                    eng.wait_ge(nT, 4 * k + b + 1)
                    for j in range(2):
                        c = 2 * b + j
                        eng.tensor_scalar(hhi[:, c, :], bank(b, j * S, (j + 1) * S), gcol[:, k, c:c + 1], None, ALU.mult)
                        eng.tensor_scalar(hT[:, c, :], bank(b, j * S, (j + 1) * S), gcol[:, k, c:c + 1], None, ALU.mult)\
                           .then_inc(nout, 1)
                    eng.wait_ge(nout, 4 * k + b + 2)
                    rest(b, hT)
                    eng.wait_ge(nfree, 4 * k + b + 2)
                    rest(b + 1, hT)

            def rest(b, src):
                c = slice(2 * b, 2 * b + 2)
                eng.tensor_tensor(hlo[:, c, :], src[:, c, :], hhi[:, c, :].bitcast(F32), ALU.subtract).then_inc(left_ready, 1)

            def split_left(b, src):
                c = slice(2 * b, 2 * b + 2)
                settle(eng.tensor_copy(hhi[:, c, :], src[:, c, :]))
                rest(b, src)

            def over(ap, n):
                return ap.unsqueeze(2).to_broadcast([P, ap.shape[1], n])

            def attention1():
                split = DVE_SPLITS[0] * HALVES + RING
                for what, i in schedule1():
                    if what == "proj" and i in DVE_SPLITS:
                        if i == DVE_SPLITS[0]:
                            eng.wait_ge(hi_ready, split)
                        for m in range(split, split + HALVES):
                            eng.wait_ge(slot_in[m % RING], 16 * (m // RING + 1))
                            eng.wait_ge(slot_used, m - RING + 1)
                            eng.tensor_copy(whi[:, m % RING, :], ring[:, m % RING, :]).then_inc(hi_ready, 1)
                        split += HALVES
                    elif what == "headnorm":
                        name = ("rq", "rk", "sq", "sk")[i]
                        X = tiles(raw1[name])
                        A, B = tiles(tmpA), tiles(tmpB)
                        eng.wait_ge(proj_copied, HEADNORM[i] + 1)
                        if i:
                            eng.wait_ge(hready, i)
                        settle(eng.tensor_tensor(A, X, X, ALU.mult))
                        settle(eng.tensor_reduce(stat[:, 5, :], A, AX.X, ALU.add))
                        eng.tensor_scalar(stat[:, 6, :], stat[:, 5, :], 1.0 / HD, EPS, ALU.mult, ALU.add).then_inc(hvar, 1)
                        eng.wait_ge(hstd, i + 1)
                        settle(eng.reciprocal(stat[:, 5, :], stat[:, 7, :]))
                        settle(eng.tensor_tensor(X, X, over(stat[:, 5, :], HD), ALU.mult))
                        g = hgain[:, i:i + 1, :].to_broadcast([P, 16, HD])
                        last = eng.tensor_tensor(X, X, g, ALU.mult)
                        if i < 2:
                            settle(last)
                            X4, A4, B4 = (v.rearrange("p (t h) c -> p t h c", t=TT) for v in (X, A, B))
                            for t in range(TT):
                                cs = rope[:, t, 2 * i:2 * i + 1, :].to_broadcast([P, HEADS, HD])
                                sn = rope[:, t, 2 * i + 1:2 * i + 2, :].to_broadcast([P, HEADS, HD])
                                tick(eng.tensor_tensor(A4[:, t], X4[:, t], cs, ALU.mult))
                                settle(eng.tensor_tensor(B4[:, t], X4[:, t], sn, ALU.mult))
                            H2 = HD // 2
                            tick(eng.tensor_tensor(X[:, :, 0:H2], A[:, :, 0:H2], B[:, :, H2:HD], ALU.subtract))
                            last = eng.tensor_tensor(X[:, :, H2:HD], B[:, :, 0:H2], A[:, :, H2:HD], ALU.add)
                        last.then_inc(hready, 1)
                    elif what == "ret_scores":
                        eng.wait_ge(rs_ready, i + 1)
                        if i >= 2:
                            eng.wait_ge(rv_ready, i - 1)
                        eng.tensor_tensor(retm[:, i % 2, :], bank(3, 0, 384), dmask[:, i, :], ALU.mult).then_inc(rm_ready, 1)
                    elif what == "ret_norm":
                        Y = rety.rearrange("p t h c -> p (t h) c")
                        A = xs.rearrange("p t (h c) -> p (t h) c", c=RDV)
                        if i == 0:
                            eng.wait_ge(rv_copied, HEADS)
                            settle(eng.tensor_reduce(stat[:, 4, :], Y, AX.X, ALU.add))
                            settle(eng.tensor_scalar(stat[:, 5, :], stat[:, 4, :], 1.0 / RDV, None, ALU.mult))
                            tick(eng.tensor_tensor(Y, Y, over(stat[:, 5, :], RDV), ALU.subtract))
                        elif i == 1:
                            eng.wait_ge(dve_step, steps[0])
                            settle(eng.tensor_tensor(A, Y, Y, ALU.mult))
                            settle(eng.tensor_reduce(stat[:, 4, :], A, AX.X, ALU.add))
                            eng.tensor_scalar(stat[:, 5, :], stat[:, 4, :], 1.0 / RDV, EPS, ALU.mult, ALU.add)\
                               .then_inc(rg_var, 1)
                        elif i == 2:
                            eng.wait_ge(rg_std, 1)
                            settle(eng.reciprocal(stat[:, 5, :], stat[:, 4, :]))
                            settle(eng.tensor_tensor(Y, Y, over(stat[:, 5, :], RDV), ALU.mult))
                            for t in range(TT):
                                tick(eng.tensor_tensor(rety[:, t], rety[:, t], ggain, ALU.mult))
                        else:
                            eng.wait_ge(dve_step, steps[0])
                            eng.wait_ge(proj_copied, 18)
                            eng.tensor_tensor(Y, Y, raw1["rg"].rearrange("p t (h c) -> p (t h) c", c=RDV), ALU.mult)\
                               .then_inc(rg_ready, 1)
                    elif what == "sb_scores":
                        b = sbt[:, i % 2, :, :]
                        z = bank(0, 0, 384)
                        sc = HD ** -0.5
                        eng.wait_ge(z_ready, i + 1)
                        if i >= 2:
                            eng.wait_ge(w_ready, i - 1)
                        tick(eng.tensor_scalar(b[:, 0, :], z, -sc, 0.0, ALU.mult, ALU.min))
                        settle(eng.tensor_scalar(b[:, 1, :], z, sc, 0.0, ALU.mult, ALU.min))
                        eng.tensor_tensor(b[:, 2, :], b[:, 0, :], b[:, 1, :], ALU.add).then_inc(neg_ready, 1)
                        eng.wait_ge(ln_ready, i + 1)
                        eng.wait_ge(dve_step, steps[0])
                        tick(eng.tensor_tensor(b[:, 1, :], b[:, 1, :], b[:, 4, :], ALU.subtract))
                        settle(eng.tensor_tensor(b[:, 0, :], b[:, 0, :], b[:, 4, :], ALU.subtract))
                        eng.tensor_tensor(b[:, 0, :], b[:, 0, :], strict, ALU.mult).then_inc(stay_ready, 1)
                    elif what == "sb_later":
                        b = sbt[:, i % 2, :, :]
                        eng.wait_ge(later_ready, i + 1)
                        eng.tensor_tensor(b[:, 2, :], b[:, 1, :], bank(1, 0, 384), ALU.add).then_inc(arg_ready, 1)
                        if i >= 2:
                            eng.wait_ge(so_ready, i - 1)
                        eng.wait_ge(wexp_ready, i + 1)
                        eng.tensor_tensor(b[:, 5, :], b[:, 3, :], strict, ALU.mult).then_inc(w_ready, 1)
                eng.wait_ge(so_copied, HEADS)
                settle(eng.tensor_copy(sbhi[:, :, :], sbT))
                eng.tensor_tensor(sblo[:, :, :], sbT, sbhi[:, :, :].bitcast(F32), ALU.subtract).then_inc(sb_left, 1)
                for b in range(4):
                    eng.wait_ge(t_copied, b + 1)
                    split_left(b, hT)
                eng.wait_ge(proj_copied, len(IN1_SLOTS))
                for u in range(8):
                    c = slice((u % 4) * SC, (u % 4 + 1) * SC)
                    y = bank(4 + u % 2).rearrange("p (t c) -> p t c", t=TT)
                    if u < 4:
                        eng.wait_ge(slot_used, FIRST["ret"] + HALVES * (u + 1))
                        eng.tensor_tensor(mixed[:, :, c], y, raw1["ga"][:, :, c], ALU.mult).then_inc(ya_used, 1)
                    else:
                        eng.wait_ge(slot_used, FIRST["sb"] + u - 4 + 1)
                        eng.tensor_tensor(tmpA[:, :, 0:SC], y, raw1["gb"][:, :, c], ALU.mult).then_inc(ya_used, 1)
                        eng.wait_ge(ya_used, u + 1)
                        last = eng.tensor_tensor(mixed[:, :, c], mixed[:, :, c], tmpA[:, :, 0:SC], ALU.add)
                        if u < 7:
                            settle(last)
                last.then_inc(mix_ready, 1)
                for b in range(4):
                    eng.wait_ge(t_copied, 4 + b + 1)
                    split_left(b, hT)
                residual(0)

            def residual(k):
                for u in range(4):
                    c = slice(u * SC, (u + 1) * SC)
                    eng.wait_ge(slot_used, FIRST[f"out{k + 1}"] + HALVES * (u + 1))
                    eng.tensor_tensor(xres[:, :, c], xres[:, :, c], bank(4 + u % 2).rearrange("p (t c) -> p t c", t=TT),
                                      ALU.add).then_inc(o_used, 1)

            def attention2():
                base = len(IN1_SLOTS)
                eng.wait_ge(const2_in, 16)
                settle(eng.tensor_tensor(lbs[:, 0, :], lbl[:, 0, :], lbl[:, 1, :], ALU.max))
                tick(eng.tensor_tensor(lbs[:, 2, :], lbl[:, 0, :], lbs[:, 0, :], ALU.subtract))
                eng.tensor_tensor(lbs[:, 3, :], lbl[:, 1, :], lbs[:, 0, :], ALU.subtract).then_inc(g_lbm, 1)
                tick(eng.memset(qL, 0.0))
                tick(eng.memset(kL, 0.0))
                tick(eng.memset(Ssum, 0.0))
                eng.wait_ge(g_lbe, 1)
                settle(eng.tensor_tensor(lbs[:, 0, :], lbs[:, 4, :], lbs[:, 5, :], ALU.add))
                settle(eng.reciprocal(lbs[:, 1, :], lbs[:, 0, :]))
                settle(eng.tensor_tensor(lbs[:, 6, :], lbs[:, 4, :], lbs[:, 1, :], ALU.mult))
                settle(eng.tensor_scalar(lbs[:, 7, :], lbs[:, 6, :], -1.0, 1.0, ALU.mult, ALU.add))
                for what, i in schedule2():
                    if what == "m_scores":
                        l = ml[:, i % 2, :]
                        eng.wait_ge(m_ready, i + 1)
                        if i >= 2:
                            eng.wait_ge(m_T, i - 1)
                        settle(eng.scalar_tensor_tensor(l, bank(0, 0, 384), HD ** -0.5, c2a[:, i, :], ALU.mult, ALU.add))
                        eng.tensor_reduce(mstat(i, 0, 0), l[:, 0:P], AX.X, ALU.max, negate=True)
                        eng.tensor_reduce(mstat(i, 0, 1), l[:, P:P + S], AX.X, ALU.max, negate=True).then_inc(m_max, 1)
                    elif what == "m_norm":
                        l = ml[:, i % 2, :]
                        eng.wait_ge(m_exp, TT * (i + 1))
                        settle(eng.reciprocal(mstat2(i, 2), mstat2(i, 1)))
                        eng.tensor_scalar(l[:, 0:P], l[:, 0:P], mstat(i, 2, 0), None, ALU.mult)
                        eng.tensor_scalar(l[:, P:P + S], l[:, P:P + S], mstat(i, 2, 1), None, ALU.mult).then_inc(m_prob, 1)
                    elif what == "rec_prep":
                        f = colT["fr"]
                        eng.wait_ge(proj_copied, base + 4)
                        for h in range(REC_H):
                            tick(eng.tensor_scalar(f[:, h, :], f[:, h, :], lbs[:, 7, h:h + 1], lbs[:, 6, h:h + 1],
                                                   ALU.mult, ALU.add))
                        eng.wait_ge(dve_step, steps[0])
                        eng.tensor_scalar(kk.rearrange("p h t c -> p (h t c)"), f.rearrange("p h c -> p (h c)"), -1.0, 1.0,
                                          ALU.mult, ALU.add).then_inc(g_f, 1)
                        eng.wait_ge(g_log, 1)
                        for h in range(REC_H):
                            for t in range(TT):
                                tick(eng.tensor_tensor_scan(cum[:, h, t, :], ones2, dlt[:, h, t, :], 0.0, ALU.mult, ALU.add))
                        eng.wait_ge(dve_step, steps[0])
                    elif what == "rec_decay" and i:
                        eng.wait_ge(g_qk, i)
                        if i < 8:
                            d, h = level(dlt, i)
                            c = level(cum, i)[0]
                            eng.tensor_tensor(d, c, c[:, :, h - 1:h].to_broadcast([P, c.shape[1], 2 * h]), ALU.subtract)\
                               .then_inc(g_dlt, 1)
                        else:
                            eng.tensor_tensor(dlt[:, :, 0, :], cum[:, :, 0, :],
                                              cum[:, :, 0, P - 1:P].to_broadcast([P, REC_H, P]), ALU.subtract)\
                               .then_inc(g_dlt, 1)
                    elif what == "rec_take":
                        for t in range(TT):
                            eng.wait_ge(g_s, TT * i + t + 1)
                            m = lmask[:, i:i + 1, :].bitcast(U32).to_broadcast([P, REC_H, P])
                            eng.copy_predicated(Ssum[:, t, :, :], m, bank(6 + t).rearrange("p (h c) -> p h c", h=REC_H))\
                               .then_inc(g_sc, 1)
                    elif what == "rec_factors":
                        q = colT["qr"].rearrange("p h (t c) -> p h t c", t=TT)
                        ql, kl = (qL2, kL2) if i % 2 else (qL, kL)
                        if i == 0:
                            eng.wait_ge(g_f, 1)
                            eng.nop().then_inc(g_qk, 1)
                        else:
                            eng.wait_ge(g_exp, i)
                            if i >= 2:
                                eng.wait_ge(g_s, TT * (i - 1))
                            if i < 8:
                                d, h = level(dlt, i)
                                eng.tensor_tensor(level(ql, i)[0][:, :, h:], d[:, :, h:], level(q, i)[0][:, :, h:], ALU.mult)
                                eng.tensor_tensor(level(kl, i)[0][:, :, 0:h], d[:, :, 0:h], level(kk, i)[0][:, :, 0:h], ALU.mult)\
                                   .then_inc(g_qk, 1)
                            else:
                                eng.tensor_tensor(ql[:, :, 1, :], dlt[:, :, 1, :], q[:, :, 1, :], ALU.mult)
                                eng.tensor_tensor(kl[:, :, 0, :], dlt[:, :, 0, :], kk[:, :, 0, :], ALU.mult).then_inc(g_qk, 1)
                    elif what == "rec_squares":
                        Y = ry.rearrange("p t h c -> p (t h) c")
                        A = rt.rearrange("p t h c -> p (t h) c")
                        eng.wait_ge(g_yc, TT)
                        settle(eng.tensor_tensor(A, Y, Y, ALU.mult))
                        settle(eng.tensor_reduce(stat[:, 5, 0:8], A, AX.X, ALU.add))
                        eng.tensor_scalar(stat[:, 6, 0:8], stat[:, 5, 0:8], 1.0 / P, EPS, ALU.mult, ALU.add).then_inc(g_var, 1)
                    elif what == "rec_norm":
                        eng.wait_ge(g_std, 1)
                        settle(eng.reciprocal(stat[:, 5, 0:8], stat[:, 7, 0:8]))
                        settle(eng.tensor_tensor(Y, Y, over(stat[:, 5, 0:8], P), ALU.mult))
                        for t in range(TT):
                            tick(eng.tensor_tensor(ry[:, t], ry[:, t], rgain, ALU.mult))
                        eng.wait_ge(dve_step, steps[0])
                        eng.wait_ge(proj_copied, base + len(IN2_SLOTS))
                        eng.tensor_tensor(Y, Y, raw2["gr"].rearrange("p t (h c) -> p (t h) c", c=P), ALU.mult)\
                           .then_inc(g_out, 1)
                eng.wait_ge(m_outc, HEADS)
                for b in range(4):
                    if b >= 2:
                        eng.wait_ge(t_copied, 8 + b - 1)
                    split_left(b, catT)
                residual(1)

            def top16(ins, tmp, vals, ids):
                for s, v in zip(ins, vals):
                    tick(eng.max(v[:, 0:8], s))
                eng.wait_ge(dve_step, steps[0])
                for s, w, v, x in zip(ins, tmp, vals, ids):
                    tick(eng.max_index(x[:, 0:8], v[:, 0:8], s))
                    tick(eng.match_replace(w, v[:, 0:8], s, -3.0e38))
                eng.wait_ge(dve_step, steps[0])
                for w, v in zip(tmp, vals):
                    tick(eng.max(v[:, 8:16], w))
                eng.wait_ge(dve_step, steps[0])
                for w, v, x in zip(tmp, vals, ids):
                    tick(eng.max_index(x[:, 8:16], v[:, 8:16], w))
                eng.wait_ge(dve_step, steps[0])

            def experts(b):
                n = peer[b]
                first_v = FIRST[f"v{b + 1}"]
                for h in range(HEADS):
                    eng.wait_ge(n["s_copied"], h + 1)
                    for t in range(TT):
                        top16([scores[:, h % 4, t, c, :] for c in range(2)], [cand[:, 2, c * NKEY:(c + 1) * NKEY] for c in range(2)],
                              [val[:, c, :] for c in range(2)], [idx[:, t, h, c, :] for c in range(2)])
                        s = cand[:, 0, :]
                        last = eng.tensor_tensor(s.rearrange("p (a b) -> p a b", a=TOPK), over(val[:, 0, :], TOPK),
                                                 val[:, 1:2, :].to_broadcast([P, TOPK, TOPK]), ALU.add)
                        if t == TT - 1:
                            last.then_inc(n["scores_used"], 1)
                            eng.wait_ge(n["scores_used"], h + 1)
                        else:
                            settle(last)
                        top16([s], [cand[:, 1, :]], [top[:, t, h, :]], [pos[:, t, h, :]])
                hk = HEADS * TOPK
                big = work[:, 0:2048]
                eq = big.rearrange("p (m a) -> p m a", a=TOPK)
                eq4 = big.rearrange("p (h k a) -> p h k a", h=HEADS, k=TOPK)
                for t in range(TT):
                    tick(eng.tensor_scalar(posab[:, 0, :, :], pos[:, t, :, :], 4, None, ALU.logical_shift_right))
                    tick(eng.tensor_scalar(posab[:, 1, :, :], pos[:, t, :, :], TOPK - 1, None, ALU.bitwise_and))
                    tick(eng.tensor_copy(idxf[:, :, :, :], idx[:, t, :, :, :]))
                    eng.wait_ge(dve_step, steps[0])
                    settle(eng.tensor_copy(posf[:, :, :, :], posab[:, :, :, :]))
                    for c in range(2):
                        settle(eng.tensor_tensor(eq, iota16[:, :].unsqueeze(1).to_broadcast([P, hk, TOPK]),
                                                 over(posf[:, c, :, :].rearrange("p h k -> p (h k)"), TOPK), ALU.is_equal))
                        settle(eng.tensor_tensor(eq4, eq4, idxf[:, :, c, :].unsqueeze(2).to_broadcast([P, HEADS, TOPK, TOPK]),
                                                 ALU.mult))
                        settle(eng.tensor_reduce(esel[:, t, c, :, :].rearrange("p h k -> p (h k)"), eq, AX.X, ALU.add))
                    last = eng.tensor_tensor(esel[:, t, 2, :, :], top[:, t, :, :],
                                             top[:, t, :, 0:1].to_broadcast([P, HEADS, TOPK]), ALU.subtract)
                    if t == 0:
                        settle(last)
                last.then_inc(n["sums_ready"], 1)
                eng.wait_ge(n["exp_ready"], 1)
                g = esel[:, :, 2, :, :]
                for t in range(TT):
                    tick(eng.tensor_reduce(stat[:, 0, t * HEADS:(t + 1) * HEADS], g[:, t], AX.X, ALU.add))
                eng.wait_ge(dve_step, steps[0])
                settle(eng.reciprocal(stat[:, 1, 0:16], stat[:, 0, 0:16]))
                settle(eng.tensor_scalar(stat[:, 1, 0:16], stat[:, 1, 0:16], GATE_SCALE, None, ALU.mult))
                for t in range(TT):
                    last = eng.tensor_tensor(g[:, t], g[:, t], over(stat[:, 1, t * HEADS:(t + 1) * HEADS], TOPK), ALU.mult)
                    if t == 0:
                        tick(last)
                last.then_inc(n["sel_ready"], 1)
                eng.wait_ge(n["selT_ready"], 1)
                tick(eng.tensor_copy(rowT[:, 0:2, :], bank(4).rearrange("p (w t) -> p w t", w=2)))
                settle(eng.tensor_copy(rowT[:, 2, :], bank(5, 0, S)))
                eng.tensor_tensor(rowT[:, 3, :], bank(5, 0, S), rowT[:, 2, :], ALU.subtract).then_inc(n["rows_ready"], 1)
                eng.wait_ge(n["rows_ready"], 1)

                def hot(k, c, base, half, j):
                    def row(w, width):
                        return rowT[:, w, bass.ds(k * (4 * RING) + 4 * c, 4)].unsqueeze(2).to_broadcast([P, 4, width])
                    eng.tensor_tensor(eq1[:, j], iota[:, half * HALF:(half + 1) * HALF].unsqueeze(1).to_broadcast([P, 4, HALF]),
                                      row(0, HALF), ALU.is_equal).then_inc(n["eq_ready"], 1)
                    eng.tensor_tensor(hot2[:, j], iota[:, :].unsqueeze(1).to_broadcast([P, 4, NKEY]), row(1, NKEY), ALU.is_equal)
                    eng.wait_ge(n["eq_ready"], k * RING + (base + c + 1))
                    eng.tensor_tensor(hot1[:, j, 0], eq1[:, j], row(2, HALF), ALU.mult)
                    eng.tensor_tensor(hot1[:, j, 1], eq1[:, j], row(3, HALF), ALU.mult).then_inc(n["hot_ready"], 1)

                def apply(k, c, base, half, j):
                    eng.wait_ge(n["gates_ready"], k * RING + (base + c + 1))
                    a = act[:, bass.ds(k * (4 * RING) + 4 * c, 4), half * HALF:(half + 1) * HALF]
                    eng.tensor_tensor(a, bank(6 + j, 0, 4 * HALF).rearrange("p (q k) -> p q k", q=4), a, ALU.mult)\
                       .then_inc(n["gates_used"], 1)

                hot(0, 0, 0, 0, 0)
                hot(0, 1, 0, 0, 1)
                eng.wait_ge(n["gelu_done"], E_TILES // 4)
                with eng.Fori(0, HALF_ROUND - 1) as k:
                    for c in range(RING):
                        apply(k, c, 0, 0, c % 2)
                        hot(k, c + 2, 0, 0, c % 2)
                last_k = HALF_ROUND - 1
                for c in range(RING):
                    apply(last_k, c, 0, 0, c % 2)
                    if c < 2:
                        hot(last_k, c + 2, 0, 0, c % 2)
                    else:
                        hot(0, c - 2, GROUPS, 1, c % 2)
                eng.wait_ge(n["gates_used"], GROUPS)

                def pair(p, j, first=False):
                    if not first:
                        eng.wait_ge(slot_used, p * 2 + (first_v - 2))
                    src = act[:, :, bass.ds(p * 2, 2)].rearrange("p t e -> p e t")
                    eng.tensor_copy(shi[:, j, :, :], src).then_inc(n["shi_ready"], 1)
                    eng.wait_ge(n["shi_ready"], p + 1)
                    eng.tensor_tensor(slo[:, j, :, :], src, shi[:, j, :, :].bitcast(F32), ALU.subtract)\
                       .then_inc(n["pair_ready"], 1)

                def gated(k, cs, last=False):
                    for c in cs:
                        apply(k, c, GROUPS, 1, c % 2)
                        if not last or c < 2:
                            hot(k, c + 2, GROUPS, 1, c % 2)

                pair(0, 0, first=True)
                pair(1, 1, first=True)
                eng.wait_ge(n["gelu_done"], E_TILES // 2)
                gated(0, (0, 1))
                pair(2, 0)
                gated(0, (2, 3))
                with eng.Fori(1, HALF_ROUND - 1) as k:
                    pair(k * 2 + 1, 1)
                    gated(k, (0, 1))
                    pair(k * 2 + 2, 0)
                    gated(k, (2, 3))
                pair(2 * last_k + 1, 1)
                gated(last_k, (0, 1, 2, 3), last=True)
                eng.wait_ge(n["gates_used"], 2 * GROUPS)
                pair(2 * last_k + 2, 0)
                with eng.Fori(HALF_ROUND, ROUNDS - 1) as k:
                    pair(k * 2 + 1, 1)
                    pair(k * 2 + 2, 0)
                pair(2 * ROUNDS - 1, 1)
                eng.wait_ge(n["acc_ready"], 1)
                for a in range(4):
                    c = slice((a % 2) * 512, (a % 2 + 1) * 512)
                    eng.scalar_tensor_tensor(xres[:, a // 2, c], bank(a), 1.0 / GATE_SCALE, xres[:, a // 2, c], ALU.mult, ALU.add)\
                       .then_inc(n["done"], 1)

            eng.wait_ge(turn_in, N_TURN)
            eng.wait_ge(x_in, 16 * TT)
            norm(0)
            eng.wait_ge(const_in, N_CONST)
            attention1()
            norm(1)
            experts(0)
            norm(2)
            attention2()
            norm(3)
            experts(1)
            eng.wait_ge(fin_sq, TT)
            eng.tensor_scalar(stat[:, 1, 0:TT], stat[:, 0, 0:TT], 1.0 / D, EPS, ALU.mult, ALU.add).then_inc(fin_var, 1)
            eng.wait_ge(fin_std, 1)
            settle(eng.reciprocal(stat[:, 3, 0:TT], stat[:, 2, 0:TT]))
            eng.wait_ge(fgain_in, 16)
            for t in range(TT):
                settle(eng.tensor_scalar(xs[:, t, :], xres[:, t, :], stat[:, 3, t:t + 1], None, ALU.mult))
                eng.tensor_tensor(xs[:, t, :], xs[:, t, :], fgain, ALU.mult).then_inc(fin_ready, 1)


def shape_constants():
    f = np.float32
    half = HD // 2
    pos = np.arange(S, dtype=f)
    freqs = (f(10000.0) ** (-np.arange(half, dtype=f) / f(half))).astype(f)
    ang = pos[:, None] * freqs[None, :]
    cos, sin = np.cos(ang), np.sin(ang)
    cos, sin = np.concatenate([cos, cos], 1), np.concatenate([sin, sin], 1)
    sc = f(HD ** -0.5)
    rope = np.stack([cos, sin, cos * sc, sin * sc], 1).reshape(TT, P, 4 * HD).transpose(1, 0, 2).reshape(P, -1)
    j, i = np.arange(P)[:, None], np.arange(S)[None, :]
    i1 = np.arange(P, S)[None, :]
    lg = np.log1p(-np.exp2(-5.0 - np.arange(HEADS)))

    def decay(key, query):
        d = query - key
        return np.where(d >= 0, np.exp(lg[:, None, None] * np.maximum(d, 0)), 0.0)
    dm = np.concatenate([decay(j, i), decay(j + P, i1)], 2).transpose(1, 0, 2).reshape(P, -1)
    tri = (np.arange(P)[:, None] > np.arange(P)[None, :]).astype(f)
    strict = np.concatenate([j < i, j + P < i1], 1).astype(f)
    c1 = [rope, dm, tri, np.ones((P, P)), strict]
    t = np.arange(P)[:, None]
    s0, s1 = np.arange(P)[None, :], np.arange(S)[None, :]
    slopes = 2.0 ** (-8.0 * np.arange(1, HEADS + 1) / HEADS)

    def alibi(q, k):
        return np.where(k <= q, -slopes[:, None, None] * (q - k), -1.0e30)
    ab = np.concatenate([alibi(t, s0), alibi(t + P, s1)], 2).transpose(1, 0, 2).reshape(P, -1)
    k_, q_ = np.arange(P)[:, None], np.arange(P)[None, :]
    lm = [k_ == q_]
    for l in range(7):
        b = 1 << l
        lm.append((k_ // (2 * b) == q_ // (2 * b)) & (k_ % (2 * b) < b) & (q_ % (2 * b) >= b))
    lm = np.stack(lm, 1).astype(f).reshape(P, -1)
    c2 = [ab, lm, np.ones((P, P))]
    return [a.astype(f) for a in c1], [a.astype(f) for a in c2]


def rows_of(v):
    return np.broadcast_to(np.asarray(v).reshape(1, -1), (P, np.asarray(v).size))


def slot_rows(w):
    r, c = w.shape
    return w.reshape(r // P // KH, KH, P, c // SC, SC).transpose(3, 0, 2, 1, 4).reshape(-1, P, SLOT)


def slot_tiles(w):
    return w.reshape(-1, P, KC, P).transpose(0, 3, 2, 1).reshape(-1, P, SLOT)


def kernel(**inputs):
    import concourse.bacc as _bacc
    from concourse.bass_utils import run_bass_kernel_spmd as _run

    w = {k: np.asarray(v) for k, v in inputs.items()}
    in1, in2 = w["w_in"][0], w["w_in_2"][0]
    parts = [slot_rows(in1[:, a:a + n]) for _, a, n in IN1]
    parts += [slot_rows(w["w_branch_ret"][0]), slot_rows(w["w_branch_sb"][0]), slot_rows(w["w_out"][0]),
              slot_tiles(w["peer_w_q"][0].T), slot_tiles(w["peer_u"][0]), w["peer_v"][0].reshape(-1, P, D)]
    parts += [slot_rows(in2[:, a:a + n]) for _, a, n in IN2]
    parts += [slot_rows(w["w_out_2"][0]), slot_tiles(w["peer_wq_2"][0].T), slot_tiles(w["peer_u_2"][0]),
              w["peer_v_2"][0].reshape(-1, P, D)]
    c1, c2 = shape_constants()
    c1 += [rows_of(w[k][0]) for k in ("ret_q_norm", "ret_k_norm", "sb_q_norm", "sb_k_norm")]
    c1 += [rows_of(w["ret_group_norm"][0])]
    c2 += [w["rec_lb_logits_2"].reshape(2, REC_H, P).transpose(2, 0, 1).reshape(P, -1), rows_of(w["rec_norm_g_2"][0])]
    gcol = np.stack([w[k][0].reshape(KC, P) for k in ("norm_attn", "norm_ffn", "norm1_g_2", "norm2_g_2")])
    arrays = {
        "weights": np.concatenate(parts),
        "const1": np.concatenate(c1, 1),
        "const2": np.concatenate(c2, 1),
        "fgain": rows_of(w["normf_g_2"]),
        "gcol": gcol.transpose(2, 0, 1),
        "ident": np.eye(P, dtype=np.float32),
        "iota": np.broadcast_to(np.arange(NKEY, dtype=np.float16), (P, NKEY)),
        "iota16": np.broadcast_to(np.arange(TOPK, dtype=np.float32), (P, TOPK)),
        "keys1": np.stack([w["peer_sub_keys_1"][0].T, w["peer_sub_keys_2"][0].T], 1),
        "keys2": w["peer_subkeys_2"][0].reshape(HEADS * 2, NKEY, P).transpose(2, 0, 1),
        "x": w["x"],
    }
    arrays = {k: np.ascontiguousarray(v) for k, v in arrays.items()}
    nc = _bacc.Bacc("TRN2", target_bir_lowering=False, num_devices=1, dynamic_dma_scratch_size=256)
    ap = {k: nc.dram_tensor("in_" + k, v.shape, mybir.dt.from_np(v.dtype), kind="ExternalInput").ap() for k, v in arrays.items()}
    out = nc.dram_tensor("out", (1, S, D), F32, kind="ExternalOutput").ap()
    block_program(nc, ap["weights"], ap["const1"], ap["const2"], ap, (ap["keys1"], ap["keys2"]), ap["x"], out)
    r = _run(nc, [{"in_" + k: v for k, v in arrays.items()}], core_ids=[0])
    return r.results[0]["out"]
```
